# Optimizing a Trainium2 kernel written in Bass

```python
import jax, jax.numpy as jnp
from jax import lax

D_MODEL = 1024
BATCH = 1
SEQ = 1024
DEPTH = 1

D_CONV = D_MODEL // 2
CONV_GROUPS = 8
CONV_WIDTH = 3
N_HEADS = 8
HEAD_DIM = 64
N_KV = 2
HPG = N_HEADS // N_KV
D_ATTN = N_HEADS * HEAD_DIM
D_MIX = D_CONV + D_ATTN
KV_DIM = N_KV * HEAD_DIM
CMP_LEN = 32
CMP_STRIDE = 16
CMP_HIDDEN = 2 * HEAD_DIM
SEL_LEN = 64
TOP_N = 16
WINDOW = 512
Q_BLOCK = 128
D_FF = -(-8 * D_MODEL // (3 * 256)) * 256
D_IN = 3 * D_CONV + D_ATTN + 6 * KV_DIM + 3 * N_HEADS
NEG = -1e30
FORCE = 1e9

kernel_name = "hybrid_conv_nsa_sandwich_adaln"

def rmsnorm(x, g, eps=1e-6):
    xf = x.astype(jnp.float32)
    y = xf * lax.rsqrt(jnp.mean(xf * xf, axis=-1, keepdims=True) + eps)
    return (y * g.astype(jnp.float32)).astype(x.dtype)

def alibi_slopes():
    h = jnp.arange(N_HEADS, dtype=jnp.float32) + 1.0
    return (2.0 ** (-8.0 * h / N_HEADS)).reshape(N_KV, HPG)

def short_conv_mixer(u, conv_w):
    b_gate, c_gate, v = jnp.split(u, 3, axis=-1)
    z = c_gate * v
    rhs = conv_w.astype(z.dtype)[:, None, :]
    zc = lax.conv_general_dilated(z, rhs, window_strides=(1,), padding=[(CONV_WIDTH - 1, 0)],
                                  dimension_numbers=("NWC", "WIO", "NWC"), feature_group_count=D_CONV)
    return b_gate * zc

def compress(kv, pos, w1, w2):
    B, S = kv.shape[:2]
    ch = kv.reshape(B, S // CMP_STRIDE, CMP_STRIDE, N_KV, HEAD_DIM)
    blk = jnp.concatenate([ch[:, :-1], ch[:, 1:]], axis=2) + pos.astype(kv.dtype)[None, None, :, None, :]
    h = jax.nn.gelu(jnp.einsum("bclgd,ldh->bcgh", blk, w1))
    return jnp.einsum("bcgh,hd->bcgd", h, w2)

def gather_blocks(blocks, idx):
    return jax.vmap(jax.vmap(lambda b_, i_: b_[i_]))(blocks, idx)

def nsa_mixer(q, k_cmp, v_cmp, k_sel, v_sel, k_win, v_win, gates, pos_cmp, w_ck1, w_ck2, w_cv1, w_cv2):
    B, S = q.shape[:2]
    f32 = jnp.float32
    kc = compress(k_cmp, pos_cmp, w_ck1, w_ck2)
    vc = compress(v_cmp, pos_cmp, w_cv1, w_cv2)
    NC = kc.shape[1]
    NS = S // SEL_LEN
    top_n = min(TOP_N, NS)
    ksb = k_sel.reshape(B, NS, SEL_LEN, N_KV, HEAD_DIM).transpose(0, 3, 1, 2, 4)
    vsb = v_sel.reshape(B, NS, SEL_LEN, N_KV, HEAD_DIM).transpose(0, 3, 1, 2, 4)
    pad = ((0, 0), (WINDOW, 0), (0, 0), (0, 0))
    kw_pad = jnp.pad(k_win, pad)
    vw_pad = jnp.pad(v_win, pad)
    sl = alibi_slopes()
    sl5 = sl[None, :, :, None, None]
    cmp_start = jnp.arange(NC) * CMP_STRIDE
    cmp_end = cmp_start + CMP_LEN - 1
    sel_start = jnp.arange(NS) * SEL_LEN
    overlap = ((cmp_start[:, None] < sel_start[None, :] + SEL_LEN) &
               (cmp_start[:, None] + CMP_LEN > sel_start[None, :])).astype(f32)
    scale = HEAD_DIM ** -0.5
    nq = S // Q_BLOCK
    qb = q.reshape(B, nq, Q_BLOCK, N_KV, HPG, HEAD_DIM).transpose(1, 0, 2, 3, 4, 5)
    gb = gates.reshape(B, nq, Q_BLOCK, N_KV, HPG, 3).transpose(1, 0, 2, 3, 4, 5)
    blk_ids = jnp.arange(NS)

    def block(args):
        q_c, g_c, q0 = args
        t = q0 + jnp.arange(Q_BLOCK)
        s = jnp.einsum("bqgnd,bkgd->bgnqk", q_c, kc, preferred_element_type=f32) * scale
        valid = cmp_end[None, :] <= t[:, None]
        dist = (t[:, None] - cmp_end[None, :]).astype(f32)
        s = jnp.where(valid, s - sl5 * dist, NEG)
        p = jax.nn.softmax(s, axis=-1) * jnp.any(valid, axis=-1)[:, None].astype(f32)
        o_cmp = jnp.einsum("bgnqk,bkgd->bqgnd", p.astype(vc.dtype), vc)
        imp = jnp.einsum("bgnqk,ks->bgqs", p, overlap)
        cur = t // SEL_LEN
        forced = (blk_ids[None, :] == 0) | (blk_ids[None, :] == cur[:, None]) | (blk_ids[None, :] == cur[:, None] - 1)
        causal_blk = sel_start[None, :] <= t[:, None]
        imp = jnp.where(causal_blk, jnp.where(forced, FORCE, imp), NEG)
        top_val, top_idx = lax.top_k(imp, top_n)
        kg = gather_blocks(ksb, top_idx)
        vg = gather_blocks(vsb, top_idx)
        kpos = top_idx[..., None] * SEL_LEN + jnp.arange(SEL_LEN)
        ok = (top_val > NEG / 2)[..., None] & (kpos <= t[:, None, None])
        s = jnp.einsum("bqgnd,bgqkld->bgnqkl", q_c, kg, preferred_element_type=f32) * scale
        dist = (t[:, None, None] - kpos).astype(f32)[:, :, None]
        s = jnp.where(ok[:, :, None], s - sl[None, :, :, None, None, None] * dist, NEG)
        p = jax.nn.softmax(s, axis=(-2, -1))
        o_sel = jnp.einsum("bgnqkl,bgqkld->bqgnd", p.astype(vg.dtype), vg)
        kw = lax.dynamic_slice_in_dim(kw_pad, q0, Q_BLOCK + WINDOW, axis=1)
        vw = lax.dynamic_slice_in_dim(vw_pad, q0, Q_BLOCK + WINDOW, axis=1)
        wpos = q0 - WINDOW + jnp.arange(Q_BLOCK + WINDOW)
        d = t[:, None] - wpos[None, :]
        okw = (d >= 0) & (d < WINDOW) & (wpos >= 0)[None, :]
        s = jnp.einsum("bqgnd,bkgd->bgnqk", q_c, kw, preferred_element_type=f32) * scale
        s = jnp.where(okw, s - sl5 * d.astype(f32), NEG)
        p = jax.nn.softmax(s, axis=-1)
        o_win = jnp.einsum("bgnqk,bkgd->bqgnd", p.astype(vw.dtype), vw)
        return g_c[..., 0:1] * o_cmp + g_c[..., 1:2] * o_sel + g_c[..., 2:3] * o_win

    out = lax.map(block, (qb, gb, jnp.arange(nq) * Q_BLOCK))
    return out.transpose(1, 0, 2, 3, 4, 5).reshape(B, S, N_KV, HPG, HEAD_DIM)

def setup_inputs(seed: int = 0) -> dict:
    key = jax.random.key(seed)
    ks = jax.random.split(key, 24)
    f32 = jnp.float32
    L = DEPTH

    def nrm(k, shape, s):
        return jax.random.normal(k, shape, f32) * s

    def gain(k, shape):
        return 1.0 + 0.02 * jax.random.normal(k, shape, f32)

    return {
        "x": nrm(ks[0], (BATCH, SEQ, D_MODEL), 1.0),
        "c": nrm(ks[1], (BATCH, D_MODEL), 1.0),
        "w_mod": nrm(ks[2], (L, D_MODEL, 6 * D_MODEL), 0.5 * D_MODEL ** -0.5),
        "b_mod": nrm(ks[3], (L, 6 * D_MODEL), 0.01),
        "g_pre_mix": gain(ks[4], (L, D_MODEL)),
        "w_in": nrm(ks[5], (L, D_MODEL, D_IN), D_MODEL ** -0.5),
        "conv_w": nrm(ks[6], (L, CONV_WIDTH, D_CONV), CONV_WIDTH ** -0.5),
        "pos_cmp": nrm(ks[7], (L, CMP_LEN, HEAD_DIM), 0.1),
        "w_ck1": nrm(ks[8], (L, CMP_LEN, HEAD_DIM, CMP_HIDDEN), (CMP_LEN * HEAD_DIM) ** -0.5),
        "w_ck2": nrm(ks[9], (L, CMP_HIDDEN, HEAD_DIM), CMP_HIDDEN ** -0.5),
        "w_cv1": nrm(ks[10], (L, CMP_LEN, HEAD_DIM, CMP_HIDDEN), (CMP_LEN * HEAD_DIM) ** -0.5),
        "w_cv2": nrm(ks[11], (L, CMP_HIDDEN, HEAD_DIM), CMP_HIDDEN ** -0.5),
        "g_conv_out": gain(ks[12], (L, D_CONV)),
        "g_attn_out": gain(ks[13], (L, D_ATTN)),
        "w_out": nrm(ks[14], (L, D_MIX, D_MODEL), D_MIX ** -0.5),
        "g_post_mix": gain(ks[15], (L, D_MODEL)),
        "g_pre_ffn": gain(ks[16], (L, D_MODEL)),
        "w_gate": nrm(ks[17], (L, D_MODEL, D_FF), D_MODEL ** -0.5),
        "w_up": nrm(ks[18], (L, D_MODEL, D_FF), D_MODEL ** -0.5),
        "w_down": nrm(ks[19], (L, D_FF, D_MODEL), D_FF ** -0.5),
        "g_post_ffn": gain(ks[20], (L, D_MODEL)),
    }

def reference(x, c, w_mod, b_mod, g_pre_mix, w_in, conv_w, pos_cmp, w_ck1, w_ck2, w_cv1, w_cv2,
              g_conv_out, g_attn_out, w_out, g_post_mix, g_pre_ffn, w_gate, w_up, w_down, g_post_ffn):
    B, S, _ = x.shape
    splits = [3 * D_CONV, 3 * D_CONV + D_ATTN, 3 * D_CONV + D_ATTN + 6 * KV_DIM]
    for l in range(DEPTH):
        mod = (jax.nn.silu(c) @ w_mod[l] + b_mod[l])[:, None, :]
        sh_m, sc_m, ga_m, sh_f, sc_f, ga_f = jnp.split(mod, 6, axis=-1)
        h = rmsnorm(x, g_pre_mix[l]) * (1.0 + sc_m) + sh_m
        u = h @ w_in[l]
        u_conv, q, kv, gl = jnp.split(u, splits, axis=-1)
        y_conv = rmsnorm(short_conv_mixer(u_conv, conv_w[l]), g_conv_out[l])
        q = q.reshape(B, S, N_KV, HPG, HEAD_DIM)
        k_cmp, v_cmp, k_sel, v_sel, k_win, v_win = [a.reshape(B, S, N_KV, HEAD_DIM) for a in jnp.split(kv, 6, axis=-1)]
        gates = jax.nn.sigmoid(gl.astype(jnp.float32)).astype(x.dtype).reshape(B, S, N_KV, HPG, 3)
        y_attn = nsa_mixer(q, k_cmp, v_cmp, k_sel, v_sel, k_win, v_win, gates,
                           pos_cmp[l], w_ck1[l], w_ck2[l], w_cv1[l], w_cv2[l])
        y_attn = rmsnorm(y_attn, g_attn_out[l].reshape(N_KV, HPG, HEAD_DIM)).reshape(B, S, D_ATTN)
        y = jnp.concatenate([y_conv, y_attn], axis=-1) @ w_out[l]
        x = x + ga_m * rmsnorm(y, g_post_mix[l])
        h = rmsnorm(x, g_pre_ffn[l]) * (1.0 + sc_f) + sh_f
        f = (jax.nn.silu(h @ w_gate[l]) * (h @ w_up[l])) @ w_down[l]
        x = x + ga_f * rmsnorm(f, g_post_ffn[l])
    return x


_drawn_inputs = setup_inputs


def setup_inputs(seed=0):
    import zlib

    import numpy as np

    out = dict(_drawn_inputs(seed))
    spreads = {}
    factors = {'b_mod': 3.569,
     'g_pre_mix': 6.708,
     'pos_cmp': 3.848,
     'g_conv_out': 28.447,
     'g_attn_out': 28.659,
     'g_post_mix': 8.0,
     'g_pre_ffn': 22.236,
     'g_post_ffn': 35.063}
    for name, (base, spread) in spreads.items():
        noise = np.random.default_rng([zlib.crc32(name.encode()), seed]).standard_normal(out[name].shape)
        drawn = base * np.exp(spread * noise) if base else spread * noise
        out[name] = __import__('jax').numpy.asarray(drawn.astype(out[name].dtype))
    for name, factor in factors.items():
        out[name] = (out[name] * factor).astype(out[name].dtype)
    return out
```

```python
from contextlib import ExitStack

import numpy as np

import concourse.bass as bass
from concourse import mybir

F32 = mybir.dt.float32
F32R = mybir.dt.float32r
ALU = mybir.AluOpType
ACT = mybir.ActivationFunctionType
AX_X = mybir.AxisListType.X

P = 128
SEQ = 1024
D = 1024
DT = D // P
HALF = 512
NHF = SEQ // HALF
TT = HALF // P
D_CONV = 512
CT = D_CONV // P
N_KV, HPG, HD = 2, 4, 64
N_HEADS = N_KV * HPG
CMP_STRIDE = 16
CMP_LEN = 32
N_CMP = SEQ // CMP_STRIDE
CPH = N_CMP // NHF
WIN_T = 5
D_FF = 2816
FT = D_FF // P
COL_Q, COL_KV, COL_G = 1536, 2048, 2816
BIG = 1e30
EPS = 1e-6

PROJ = ([("kcmp", 0), ("vcmp", 0), ("ksel", 0), ("vsel", 0), ("kwin", 0), ("vwin", 0), ("gate", 0)]
        + [("q", j) for j in range(CT)]
        + [(kind, j) for j in range(CT) for kind in ("cb", "cc", "cv")])
NPROJ = len(PROJ)
PER_HALF = NPROJ + DT
FFN0 = NHF * PER_HALF
PER_FFN = 3 * FT

NORMS = []
for _h in range(NHF):
    NORMS += [("n1", _h, DT), ("conv", _h, CT), ("mix", _h, DT)]
for _h in range(NHF):
    NORMS += [("n2", _h, DT), ("ffn", _h, DT)]
NORM = {}
_at = 0
for _i, (_name, _h, _n) in enumerate(NORMS):
    NORM[_name, _h] = (_i, _at, _n)
    _at += _n

VEC_N = (DT, 6 * DT, DT, DT, DT, DT, CT, CT, CT, CT, CT)
VEC_AT = [(sum(VEC_N[:i]), sum(VEC_N[:i + 1])) for i in range(len(VEC_N))]
NVEC = sum(VEC_N)

PARTS = 3
MODC = 2048


def attention_order(hf):
    units = [(qt, g) for qt in range(TT * hf, TT * hf + TT) for g in range(N_KV)]
    order = [("S", 0, h) for h in range(HPG)] + [("W", 0, 0)]
    for u, (qt, g) in enumerate(units):
        n = len(key_tiles(qt))
        nxt = [("S", u + 1, h) for h in range(HPG)] + [("W", u + 1, 0)] if u + 1 < len(units) else []
        fin = [("O1", u - 1, 0), ("O2", u - 1, 0)] if u else []
        mids = []
        for i in range(n):
            mids.append([("T", u, i)] + ([("V", u, i - 1)] if i else []))
        for i in range(n):
            order += mids[i]
            if i == 1:
                order += fin[:1]
            if i == min(3, n - 1):
                order += fin[1:]
            while nxt and (i + 1) * 5 >= (6 - len(nxt)) * n:
                order.append(nxt.pop(0))
        order += nxt
        order += [("V", u, n - 1), ("C", u, 0)]
    order += [("O1", len(units) - 1, 0), ("O2", len(units) - 1, 0)]
    return units, order


def key_tiles(qt):
    first = max(0, qt - (WIN_T - 1))
    return [("cmp", 0)] + [("sel", k) for k in range(qt + 1)] + [("win", k) for k in range(first, qt + 1)]


def score_banks(qt, hf):
    wc = CPH * (hf + 1)
    sel = P * (qt + 1)
    first = max(0, qt - (WIN_T - 1))
    win = P * (qt + 1 - first)
    banks = [[("cmp", 0, wc, 0)]]
    if win > 512:
        banks[0].append(("win", P * first + 512, win - 512, 64))
    banks.append([("win", P * first, min(win, 512), 0)])
    for c in range(0, sel, 512):
        banks.append([("sel", c, min(512, sel - c), 0)])
    return banks


UNITS, ORDER = {}, {}
for _h in range(NHF):
    UNITS[_h], ORDER[_h] = attention_order(_h)
NU = len(UNITS[0])


def tiles_before(hf, u):
    return sum(len(key_tiles(qt)) for h in range(hf + 1) for v, (qt, g) in enumerate(UNITS[h]) if (h, v) < (hf, u))


def banks_before(hf, u, h):
    n = 0
    for a in range(hf + 1):
        for v, (qt, g) in enumerate(UNITS[a]):
            if (a, v) < (hf, u):
                n += HPG * len(score_banks(qt, a))
            elif (a, v) == (hf, u):
                n += h * len(score_banks(qt, a))
    return n


def build(nc, x, c, w_mod, b_mod, g_pre_mix, w_in, conv_w, pos_cmp, w_ck1, w_ck2, w_cv1, w_cv2,
          g_conv_out, g_attn_out, w_out, g_post_mix, g_pre_ffn, w_gate, w_up, w_down, g_post_ffn, out):
    xin_v = x[0].rearrange("(t p) d -> t p d", p=P)
    out_v = out[0].rearrange("(t p) d -> t p d", p=P)
    xT_dram = nc.dram_tensor("xT_dram", [NHF, P, DT * HALF], F32, kind="Internal").ap()
    x1_dram = nc.dram_tensor("x1_dram", [NHF, P, DT * HALF], F32, kind="Internal").ap()

    keep = ExitStack()
    with keep:
        def alloc(stack):
            def sb(name, shape, dt=F32):
                return stack.enter_context(nc.sbuf_tensor(name, shape, dt))
            return sb

        def sem(name):
            return keep.enter_context(nc.semaphore(name))

        sb = alloc(keep)
        raw = sb("raw", [P, 2, D])
        whi = sb("whi", [P, 2, D], F32R)
        wlo = sb("wlo", [P, 2, D], F32R)
        ident = sb("ident", [P, P])
        ones = sb("ones", [P, P])
        dist_sel = sb("dist_sel", [P, SEQ])
        dist_win = sb("dist_win", [P, WIN_T * P])
        dist_cmp = sb("dist_cmp", [P, 120])
        sq = sb("sq", [P, 2, HALF])
        ssum = sb("ssum", [P, HALF])
        rstd = sb("rstd", [P, HALF])
        vcol = sb("vcol", [P, NVEC])
        cT, bmodT, g1T, gpmT, g2T, gpfT, gcT, gaT, cw0, cw1, cw2 = (vcol[:, a:b] for a, b in VEC_AT)
        siluc = sb("siluc", [P, DT])
        modT = sb("modT", [P, 6 * DT])
        a1 = sb("a1", [P, DT])
        a2 = sb("a2", [P, DT])
        cm = sb("cm", [P, DT])
        cf = sb("cf", [P, DT])
        posT = sb("posT", [P, CMP_LEN])
        smin = sb("smin", [P, 2, 3 * HPG])
        ssumexp = sb("ssumexp", [P, 2, 3 * HPG])
        wgt = sb("wgt", [P, 2, 3 * HPG])
        nz = sb("nz", [P, 1])
        gate = sb("gate", [P, TT, 3 * N_HEADS])
        zcar = sb("zcar", [P, CT, 2])
        hs = sb("hs", [P, HPG])
        hv = sb("hv", [P, HPG])
        hr = sb("hr", [P, HPG])
        half_neg = sb("half_neg", [P, HPG])

        mixer = ExitStack()
        sb = alloc(mixer)
        KS = sb("KS", [P, N_KV, N_CMP + 2 * SEQ], F32R)
        VS = sb("VS", [P, 2, SEQ // P, N_KV, P], F32R)
        VC = sb("VC", [N_CMP, N_KV, P], F32R)
        wk2 = sb("wk2", [P, 2, HD])
        acar = sb("acar", [HD, 2, CMP_STRIDE, N_KV])
        attn = ExitStack()
        sb = alloc(attn)
        qhi = sb("qhi", [P, N_HEADS, HALF], F32R)
        qlo = sb("qlo", [P, N_HEADS, HALF], F32R)
        yahi = sb("yahi", [P, CT, HALF], F32R)
        yalo = sb("yalo", [P, CT, HALF], F32R)
        ychi = sb("ychi", [P, CT, HALF], F32R)
        yclo = sb("yclo", [P, CT, HALF], F32R)
        PW = N_CMP + SEQ + WIN_T * P
        prob = sb("prob", [P, 2, HPG, PW])
        pth = sb("pth", [P, 2, HALF], F32R)
        ptl = sb("ptl", [P, 2, HALF], F32R)
        osb = sb("osb", [P, HALF])
        oq = sb("oq", [P, HPG, P])
        ob = sb("ob", [P, HPG, HD])
        attn.close()
        proj = ExitStack()
        sb = alloc(proj)
        xin = sb("xin", [P, TT, D])
        XT = sb("XT", [P, DT, HALF])
        wc1 = sb("wc1", [P, 2, CMP_STRIDE, P])
        sb("under_conv_out", [P, 2, CT, HALF])
        hhi = sb("hhi", [P, DT, HALF], F32R)
        hlo = sb("hlo", [P, DT, HALF], F32R)
        cin = sb("cin", [P, 2, CMP_STRIDE, N_KV, CPH])
        vtmp = sb("vtmp", [P, 3, HALF])
        cc_sb = sb("cc_sb", [P, HALF])
        cb_sb = sb("cb_sb", [P, HALF])
        z = sb("z", [P, HALF + 2])
        zc = sb("zc", [P, HALF])
        yc = sb("yc", [P, CT, HALF])
        ck = sb("ck", [P, 2, N_KV * CPH])
        vrow = sb("vrow", [NVEC, P])
        posr = sb("posr", [CMP_LEN, P])
        proj.close()
        nrm = ExitStack()
        sb = alloc(nrm)
        sb("under_x", [P, 2, DT, HALF])
        sb("under_conv_w", [P, 2, 2 * CT, HALF])
        sb("under_h", [P, 2, DT, HALF])
        tn = sb("tn", [P, 2, HALF])
        hn = sb("hn", [P, 2, HALF])
        nrm.close()
        post = ExitStack()
        sb = alloc(post)
        sb("under_q", [P, 2, DT, HALF])
        sb("under_y", [P, 4, CT, HALF])
        XR = sb("XR", [P, DT, HALF])
        res = sb("res", [P, DT, HALF])
        post.close()
        modv = ExitStack()
        sb = alloc(modv)
        wm = sb("wm", [P, 2, MODC])
        macc = sb("macc", [P, MODC])
        modv.close()
        modv0 = ExitStack()
        sb = alloc(modv0)
        sb("under_all", [P, 2 * DT + 4 * CT, HALF])
        wm0 = sb("wm0", [P, 2, MODC])
        macc0 = sb("macc0", [P, MODC])
        modv0.close()
        mixer.close()
        ffn = ExitStack()
        sb = alloc(ffn)
        h2hi = sb("h2hi", [P, DT, HALF], F32R)
        h2lo = sb("h2lo", [P, DT, HALF], F32R)
        ahi = sb("ahi", [P, FT, HALF], F32R)
        alo = sb("alo", [P, FT, HALF], F32R)
        X1 = sb("X1", [P, DT, HALF])
        fres = sb("fres", [P, DT, HALF])
        ffn.close()
        ffn2 = ExitStack()
        sb = alloc(ffn2)
        sb("under_h2", [P, 2, DT, HALF])
        sb("under_a", [P, 2, FT, HALF])
        sb("under_x1", [P, 2, DT, HALF])
        tn2 = sb("tn2", [P, 2, HALF])
        hn2 = sb("hn2", [P, 2, HALF])
        sg = sb("sg", [P, HALF])
        aa = sb("aa", [P, HALF])
        ffn2.close()
        outv = ExitStack()
        sb = alloc(outv)
        sb("under_h3", [P, 2, DT, HALF])
        osum = sb("osum", [P, TT, D])
        outv.close()

        ps = keep.enter_context(nc.psum_tensor("ps", [P, 8, HALF], F32))
        B_PJ, B_S, NS_B, B_PT, B_O, B_OT = 0, 0, 3, 3, 5, 7

        small_in = sem("small_in")
        consts = sem("consts")
        raw_in = [sem("raw_in0"), sem("raw_in1")]
        w_hi = sem("w_hi")
        w_lo = sem("w_lo")
        w_done = sem("w_done")
        mod_in = [sem("mod_in0"), sem("mod_in1")]
        mod_acc = sem("mod_acc")
        mod_sum = sem("mod_sum")
        mod_ready = sem("mod_ready")
        vec_ps = sem("vec_ps")
        vec_ok = sem("vec_ok")
        wk2_in = sem("wk2_in")
        silu_c = sem("silu_c")
        x_in = sem("x_in")
        xt_ps = sem("xt_ps")
        xt_sb = sem("xt_sb")
        xt_out = sem("xt_out")
        sq_done = sem("sq_done")
        ssum_done = sem("ssum_done")
        ms_ps = sem("ms_ps")
        ms_sb = sem("ms_sb")
        rms_sb = sem("rms_sb")
        rstd_ok = sem("rstd_ok")
        tn_done = sem("tn_done")
        hn_done = sem("hn_done")
        h_hi = sem("h_hi")
        h_lo = sem("h_lo")
        pj_free = sem("pj_free")
        ev_a = sem("ev_a")
        vt_ps = sem("vt_ps")
        vt_hi = sem("vt_hi")
        vt_ok = sem("vt_ok")
        gate_exp = sem("gate_exp")
        gate_ok = sem("gate_ok")
        wc_in = sem("wc_in")
        cmp_ps = sem("cmp_ps")
        gelu_a = sem("gelu_a")
        kc_ps = sem("kc_ps")
        kc_hi = sem("kc_hi")
        kc_ok = sem("kc_ok")
        conv_y = sem("conv_y")
        conv_n = sem("conv_n")
        conv_hi = sem("conv_hi")
        conv_ok = sem("conv_ok")
        s_ps = sem("s_ps")
        s_used = sem("s_used")
        e_done = sem("e_done")
        wgt_ok = sem("wgt_ok")
        p_ok = sem("p_ok")
        pt_ps = sem("pt_ps")
        pt_hi = sem("pt_hi")
        pt_lo = sem("pt_lo")
        pv_done = sem("pv_done")
        o_sb = sem("o_sb")
        ot_ps = sem("ot_ps")
        oq_sb = sem("oq_sb")
        o_sum = sem("o_sum")
        o_sq = sem("o_sq")
        o_ms = sem("o_ms")
        o_rstd = sem("o_rstd")
        o_norm = sem("o_norm")
        y_ps = sem("y_ps")
        y_hi = sem("y_hi")
        y_ok = sem("y_ok")
        res_sb = sem("res_sb")
        xr_in = sem("xr_in")
        x1_ok = sem("x1_ok")
        x1_out = sem("x1_out")
        x1_in = sem("x1_in")
        silu_ok = sem("silu_ok")
        a_ok = sem("a_ok")
        a_hi = sem("a_hi")
        a_lo = sem("a_lo")
        ft_ps = sem("ft_ps")
        ft_sb = sem("ft_sb")
        y_out = sem("y_out")
        dchain = sem("dchain")
        achain = sem("achain")
        pchain = sem("pchain")
        echain = sem("echain")

        def ms_bank(norm):
            return 2 if norm == "conv" else 0

        block = keep.enter_context(nc.Block())

        class Chain:
            def __init__(self, eng, s):
                self.eng, self.s, self.n = eng, s, 0

            def inc(self, ins):
                ins.then_inc(self.s, 1)
                self.n += 1

            def wait(self):
                self.eng.wait_ge(self.s, self.n)

        @block.sync
        def _(sp):
            def small(dst, src):
                sp.dma_start(dst, src).then_inc(small_in, 16)

            def load_raw(n, src):
                if n >= 2:
                    sp.wait_ge(w_lo, n - 1)
                for dst, s in src:
                    sp.dma_start(dst, s).then_inc(raw_in[n % 2], 16)

            def tile_of(n, w, c0):
                return [(raw[:, n % 2, :].rearrange("p (k m) -> p k m", k=DT),
                         w[:, c0:c0 + P].rearrange("(k p) m -> p k m", p=P))]

            for (a, b), v in zip(VEC_AT, (c[0], b_mod[0], g_pre_mix[0], g_post_mix[0], g_pre_ffn[0], g_post_ffn[0],
                                          g_conv_out[0], g_attn_out[0], conv_w[0, 0], conv_w[0, 1], conv_w[0, 2])):
                small(vrow[a:b, :], v.rearrange("(k p) -> k p", p=P))
            for g in range(N_KV):
                small(posr[:, g * HD:(g + 1) * HD], pos_cmp[0])
            for hf in range(NHF):
                if hf:
                    sp.wait_ge(pt_ps, tiles_before(1, 0))
                    sp.wait_ge(x1_ok, DT)
                    sp.wait_ge(mod_ready, PARTS)
                for t in range(TT):
                    sp.dma_start(xin[:, t, :], xin_v[hf * TT + t]).then_inc(x_in, 16)
                if hf == 0:
                    for k in range(DT):
                        if k >= 2:
                            sp.wait_ge(mod_acc, k - 1)
                        sp.dma_start(wm0[:, k % 2, :], w_mod[0, k * P:(k + 1) * P, 0:MODC]).then_inc(mod_in[k % 2], 16)
                    sp.dma_start(wk2[:, 0, :], w_ck2[0]).then_inc(wk2_in, 16)
                    sp.dma_start(wk2[:, 1, :], w_cv2[0]).then_inc(wk2_in, 16)
                for t, (kind, j) in enumerate(PROJ):
                    n = hf * PER_HALF + t
                    if t == 0:
                        for kv, w1 in ((0, w_ck1), (1, w_cv1)):
                            for h2 in range(2):
                                sp.dma_start(wc1[h2 * HD:(h2 + 1) * HD, kv, :, :],
                                             w1[0, h2 * CMP_STRIDE:(h2 + 1) * CMP_STRIDE].rearrange("l d h -> d l h")
                                             ).then_inc(wc_in, 16)
                    c0 = {"kcmp": COL_KV, "vcmp": COL_KV + P, "ksel": COL_KV + 2 * P, "vsel": COL_KV + 3 * P,
                          "kwin": COL_KV + 4 * P, "vwin": COL_KV + 5 * P, "gate": COL_G, "q": COL_Q + j * P,
                          "cb": j * P, "cc": D_CONV + j * P, "cv": 2 * D_CONV + j * P}[kind]
                    if kind == "gate":
                        ng = 3 * N_HEADS
                        r = raw[:, n % 2, :].rearrange("p (k m) -> p k m", k=DT)
                        src = [(r[:, :, 0:ng], w_in[0][:, COL_G:COL_G + ng].rearrange("(k p) m -> p k m", p=P)),
                               (r[:, :, ng:P], w_in[0][:, 0:P - ng].rearrange("(k p) m -> p k m", p=P))]
                        load_raw(n, src)
                    else:
                        load_raw(n, tile_of(n, w_in[0], c0))
                    if t == 1:
                        sp.wait_ge(xt_sb, DT * (hf + 1))
                        sp.dma_start(xT_dram[hf], XT[:].rearrange("p k n -> p (k n)")).then_inc(xt_out, 16)
                for k in range(DT):
                    n = hf * PER_HALF + NPROJ + k
                    load_raw(n, [(raw[:, n % 2, :], w_out[0, k * P:(k + 1) * P, :])])
                sp.wait_ge(xt_out, 16 * (hf + 1))
                sp.wait_ge(pt_ps, tiles_before(hf + 1, 0) if hf + 1 < NHF else tiles_before(NHF - 1, NU))
                sp.dma_start(XR[:].rearrange("p k n -> p (k n)"), xT_dram[hf]).then_inc(xr_in, 16)
                if hf == 0:
                    for part in range(1, PARTS):
                        for k in range(DT):
                            m = part * DT + k
                            sp.wait_ge(mod_acc, m - 1)
                            sp.dma_start(wm[:, m % 2, :], w_mod[0, k * P:(k + 1) * P, part * MODC:(part + 1) * MODC]
                                         ).then_inc(mod_in[m % 2], 16)
                sp.wait_ge(x1_ok, DT * (hf + 1))
                sp.dma_start(x1_dram[hf], XR[:].rearrange("p k n -> p (k n)")).then_inc(x1_out, 16)
            sp.wait_ge(x1_out, 16 * NHF)
            for hf in range(NHF):
                base = FFN0 + hf * PER_FFN
                if hf:
                    sp.wait_ge(ft_ps, DT)
                sp.dma_start(X1[:].rearrange("p k n -> p (k n)"), x1_dram[hf]).then_inc(x1_in, 16)
                with sp.Fori(0, FT) as f:
                    for s, w in ((0, w_gate), (1, w_up)):
                        sp.wait_ge(w_lo, f * 2 + (base + s - 1))
                        sp.dma_start(raw[:, (base + s) % 2, :].rearrange("p (k m) -> p k m", k=DT),
                                     w[0][:, bass.ts(f, P)].rearrange("(k p) m -> p k m", p=P)
                                     ).then_inc(raw_in[(base + s) % 2], 16)
                with sp.Fori(0, FT // 2) as f:
                    for s in range(2):
                        sp.wait_ge(w_lo, f * 2 + (base + 2 * FT + s - 1))
                        sp.dma_start(raw[:, (base + s) % 2, :], w_down[0][bass.ds(f * (2 * P) + s * P, P), :]
                                     ).then_inc(raw_in[(base + s) % 2], 16)
                for t in range(TT):
                    sp.wait_ge(ft_sb, (hf * TT + t + 1) * 2)
                    sp.dma_start(out_v[hf * TT + t], osum[:, t, :]).then_inc(y_out, 16)
            sp.wait_ge(y_out, 16 * TT * NHF)
            sp.wait_ge(xt_out, 16 * NHF)

        @block.gpsimd
        def _(pool):
            ch = Chain(pool, pchain)
            nc.gpsimd.memset(ones[:], 1.0).then_inc(consts, 1)
            ch.inc(nc.gpsimd.memset(ident[:], 0.0))
            ch.inc(nc.gpsimd.memset(nz[:], 1.0))
            ch.inc(nc.gpsimd.memset(half_neg[:], -0.5))
            ch.inc(nc.gpsimd.iota(dist_sel[:], pattern=[[-1, SEQ]], base=SEQ - P, channel_multiplier=1,
                                  allow_small_or_imprecise_dtypes=True))
            ch.inc(nc.gpsimd.iota(dist_win[:], pattern=[[-1, WIN_T * P]], base=(WIN_T - 1) * P, channel_multiplier=1,
                                  allow_small_or_imprecise_dtypes=True))
            ch.inc(nc.gpsimd.iota(dist_cmp[:], pattern=[[-CMP_STRIDE, 120]], base=56 * CMP_STRIDE - (CMP_STRIDE - 1),
                                  channel_multiplier=1, allow_small_or_imprecise_dtypes=True))
            ch.wait()
            ch.inc(nc.gpsimd.affine_select(out=ident[:], in_=ident[:], compare_op=ALU.not_equal, fill=1.0, base=0,
                                           pattern=[[-1, P]], channel_multiplier=1))
            ch.inc(nc.gpsimd.affine_select(out=nz[:], in_=nz[:], compare_op=ALU.is_ge, fill=0.0, base=-(CMP_LEN - 1),
                                           pattern=[[0, 1]], channel_multiplier=1))
            ch.inc(nc.gpsimd.affine_select(out=dist_sel[:], in_=dist_sel[:], compare_op=ALU.is_ge, fill=BIG,
                                           base=SEQ - P, pattern=[[-1, SEQ]], channel_multiplier=1))
            ch.inc(nc.gpsimd.affine_select(out=dist_win[:], in_=dist_win[:], compare_op=ALU.is_ge, fill=BIG,
                                           base=(WIN_T - 1) * P, pattern=[[-1, WIN_T * P]], channel_multiplier=1))
            ch.inc(nc.gpsimd.affine_select(out=dist_cmp[:], in_=dist_cmp[:], compare_op=ALU.is_ge, fill=BIG,
                                           base=56 * CMP_STRIDE - (CMP_STRIDE - 1), pattern=[[-CMP_STRIDE, 120]],
                                           channel_multiplier=1))
            ch.wait()
            ch.inc(nc.gpsimd.affine_select(out=dist_win[:], in_=dist_win[:], compare_op=ALU.is_ge, fill=BIG,
                                           base=511 - (WIN_T - 1) * P, pattern=[[1, WIN_T * P]],
                                           channel_multiplier=-1))
            ch.wait()
            nc.gpsimd.memset(acar[:], 0.0).then_inc(consts, 1)

            for hf in range(NHF):
                for what, u, i in ORDER[hf]:
                    qt, g = UNITS[hf][u]
                    U = hf * NU + u
                    if what == "W":
                        pool.wait_ge(wgt_ok, U + 1)
                        wc = CPH * (hf + 1)
                        ns = P * (qt + 1)
                        nw = P * min(qt + 1, WIN_T)
                        for h in range(HPG):
                            for b, lo_, n_ in ((0, 0, wc), (1, N_CMP, ns), (2, N_CMP + ns, nw)):
                                v = prob[:, U % 2, h, lo_:lo_ + n_]
                                r = nc.gpsimd.tensor_scalar(v, v, wgt[:, U % 2, 3 * h + b:3 * h + b + 1], 1.0,
                                                            ALU.mult, ALU.mult)
                            r.then_inc(p_ok, 1)
                    elif what == "O1":
                        pool.wait_ge(oq_sb, U + 1)
                        if U:
                            pool.wait_ge(y_ps, U)
                        nc.gpsimd.tensor_tensor(ob[:], oq[:, :, 0:HD], oq[:, :, HD:P], ALU.add).then_inc(o_sum, 1)
                        pool.wait_ge(o_sum, U + 1)
                        nc.gpsimd.tensor_tensor(oq[:, :, 0:HD], ob[:], ob[:], ALU.mult).then_inc(o_sq, 1)
                        pool.wait_ge(o_ms, U + 1)
                        nc.gpsimd.tensor_tensor(hr[:], hv[:], half_neg[:], ALU.pow).then_inc(o_rstd, 1)
                        pool.wait_ge(o_rstd, U + 1)
                        nc.gpsimd.tensor_tensor(ob[:], ob[:], hr[:].unsqueeze(2).to_broadcast([P, HPG, HD]),
                                                ALU.mult).then_inc(o_norm, 1)

        @block.scalar
        def _(act):
            ch = Chain(act, achain)

            def split_hi(n):
                extra = sum(1 for h in range(NHF) for t, (k, _j) in enumerate(PROJ)
                            if k == "gate" and h * PER_HALF + t <= n and (h * PER_HALF + t) % 2 == n % 2)
                act.wait_ge(raw_in[n % 2], 16 * (n // 2 + 1 + extra))
                if n >= 2:
                    act.wait_ge(w_done, n - 1)
                nc.scalar.activation(whi[:, n % 2, :], raw[:, n % 2, :], ACT.Copy).then_inc(w_hi, 1)

            def squares(norm, hf, src, ready):
                i, at, n = NORM[norm, hf]
                for k in range(n):
                    ready(k)
                    if at + k >= 2:
                        act.wait_ge(ssum_done, at + k - 1)
                    nc.scalar.activation(sq[:, (at + k) % 2, :], src(k), ACT.Square).then_inc(sq_done, 1)

            def root(norm, hf):
                i, at, n = NORM[norm, hf]
                act.wait_ge(ms_sb, i + 1)
                nc.scalar.activation(ssum[:], ssum[:], ACT.Sqrt).then_inc(rms_sb, 1)

            def modulate(norm, hf, m0, a, b0, hn_, hi_):
                for k in range(DT):
                    act.wait_ge(tn_done, m0 + k + 1)
                    if m0 + k >= 2:
                        act.wait_ge(h_lo, m0 + k - 1)
                    nc.scalar.activation(hn_[:, k % 2, :], (tn if hn_ is hn else tn2)[:, k % 2, :], ACT.Identity,
                                         scale=a[:, k:k + 1], bias=modT[:, b0 + k:b0 + k + 1]).then_inc(hn_done, 1)
                    act.wait_ge(hn_done, m0 + k + 1)
                    nc.scalar.activation(hi_[:, k, :], hn_[:, k % 2, :], ACT.Copy).then_inc(h_hi, 1)

            act.wait_ge(vec_ps, 1)
            nc.scalar.activation(vcol[:], ps[:, 0, 0:NVEC], ACT.Copy)
            nc.scalar.activation(posT[:], ps[:, 0, P:P + CMP_LEN], ACT.Copy).then_inc(vec_ok, 1)
            act.wait_ge(vec_ok, 1)
            nc.scalar.activation(siluc[:], cT, ACT.Silu).then_inc(silu_c, 1)

            nq = 0
            for hf in range(NHF):
                base = hf * PER_HALF
                for k in range(DT):
                    act.wait_ge(xt_ps, hf * DT + k + 1)
                    nc.scalar.activation(XT[:, k, :], ps[:, k, :], ACT.Copy).then_inc(xt_sb, 1)
                squares("n1", hf, lambda k: XT[:, k, :], lambda k: act.wait_ge(xt_sb, hf * DT + k + 1))
                root("n1", hf)
                if hf == 0:
                    act.wait_ge(mod_ready, 1)
                else:
                    act.wait_ge(x1_out, 16 * hf)
                modulate("n1", hf, hf * DT, a1, 0, hn, hhi)
                split_hi(base)
                split_hi(base + 1)
                for t, (kind, j) in enumerate(PROJ):
                    T = hf * NPROJ + t
                    if t + 2 < NPROJ:
                        split_hi(base + t + 2)
                    bank = ps[:, B_PJ + t % 2, :]
                    act.wait_ge(w_done, base + t + 1)
                    if kind in ("ksel", "kwin"):
                        o = N_CMP + (SEQ if kind == "kwin" else 0) + hf * HALF
                        for g in range(N_KV):
                            r = nc.scalar.activation(KS[0:HD, g, o:o + HALF], bank[g * HD:(g + 1) * HD, :], ACT.Copy)
                    elif kind == "q":
                        if j == 0:
                            act.wait_ge(h_lo, (hf + 1) * DT)
                            act.wait_ge(xt_out, 16 * (hf + 1))
                        for s in range(2):
                            h = 2 * j + s
                            for r_ in range(2):
                                r = nc.scalar.activation(qhi[r_ * HD:(r_ + 1) * HD, h, :], bank[s * HD:(s + 1) * HD, :],
                                                         ACT.Copy, scale=-(2.0 ** (h + 1)) / 8.0)
                    else:
                        continue
                    r.then_inc(ev_a, 1)
                for kv in range(2):
                    s = hf * 2 + kv
                    act.wait_ge(cmp_ps, s + 1)
                    nc.scalar.activation(ck[:, kv, :], ps[:, 2 + kv, 0:N_KV * CPH], ACT.Gelu_apprx_tanh
                                         ).then_inc(gelu_a, 1)
                for s in range(2):
                    act.wait_ge(vt_ps, hf * 3 + s + 1)
                    nc.scalar.activation(VS[:, s, hf * TT:(hf + 1) * TT, :, 0:HD],
                                         ps[:, 4 + s, :].rearrange("p (t g d) -> p t g d", t=TT, g=N_KV),
                                         ACT.Copy).then_inc(vt_hi, 1)
                act.wait_ge(vt_ps, hf * 3 + 3)
                nc.scalar.activation(gate[:], ps[:, 6, 0:TT * 3 * N_HEADS].rearrange("p (t n) -> p t n", t=TT), ACT.Exp,
                                     scale=-1.0).then_inc(gate_exp, 1)
                act.wait_ge(kc_ps, hf + 1)
                nc.scalar.activation(KS[0:HD, :, CPH * hf:CPH * (hf + 1)],
                                     ps[0:HD, 7, 0:N_KV * CPH].rearrange("p (g c) -> p g c", g=N_KV), ACT.Copy)
                nc.scalar.activation(VC[CPH * hf:CPH * (hf + 1), :, 0:HD],
                                     ps[0:CPH, 7, 128:256].rearrange("p (g d) -> p g d", g=N_KV),
                                     ACT.Copy).then_inc(kc_hi, 1)
                squares("conv", hf, lambda k: yc[:, k, :], lambda k: act.wait_ge(conv_y, hf * CT + k + 1))
                root("conv", hf)
                for k in range(CT):
                    act.wait_ge(conv_n, hf * CT + k + 1)
                    nc.scalar.activation(ychi[:, k, :], yc[:, k, :], ACT.Copy, scale=gcT[:, k:k + 1]).then_inc(conv_hi, 1)
                for what, u, i in ORDER[hf]:
                    qt, g = UNITS[hf][u]
                    U = hf * NU + u
                    wc = CPH * (hf + 1)
                    ns = P * (qt + 1)
                    nw = P * min(qt + 1, WIN_T)
                    if what == "S":
                        act.wait_ge(s_used, banks_before(hf, u, i) + len(score_banks(qt, hf)))
                        for b, lo_, n_ in ((0, 1, wc - 1), (1, N_CMP, ns), (2, N_CMP + ns, nw)):
                            v = prob[:, U % 2, i, lo_:lo_ + n_]
                            s = 3 * i + b
                            nc.scalar.activation(v, v, ACT.Exp, bias=smin[:, U % 2, s:s + 1], scale=-1.0,
                                                 accum_out=ssumexp[:, U % 2, s:s + 1]).then_inc(e_done, 1)
                    elif what == "T":
                        M = tiles_before(hf, u) + i
                        n_ = CPH * (hf + 1) if i == 0 else P
                        act.wait_ge(pt_ps, M + 1)
                        if M >= 2:
                            act.wait_ge(pv_done, M - 1)
                        nc.scalar.activation(pth[0:n_, M % 2, :], ps[0:n_, B_PT + M % 2, :], ACT.Copy).then_inc(pt_hi, 1)
                    elif what == "C":
                        act.wait_ge(pv_done, tiles_before(hf, u + 1))
                        if U:
                            act.wait_ge(ot_ps, U)
                        nc.scalar.activation(osb[:], ps[:, B_O + U % 2, :], ACT.Copy).then_inc(o_sb, 1)
                    elif what == "O1":
                        act.wait_ge(ot_ps, U + 1)
                        nc.scalar.activation(oq[:], ps[:, B_OT, :].rearrange("p (h d) -> p h d", h=HPG),
                                             ACT.Copy).then_inc(oq_sb, 1)
                    elif what == "O2":
                        act.wait_ge(y_ps, U + 1)
                        k0 = 2 * g
                        q0 = (qt % TT) * P
                        for k in range(2):
                            r = nc.scalar.activation(yahi[:, k0 + k, q0:q0 + P], ps[:, B_OT, k * P:(k + 1) * P],
                                                     ACT.Copy, scale=gaT[:, k0 + k:k0 + k + 1])
                        r.then_inc(y_hi, 1)
                for k in range(DT):
                    split_hi(base + NPROJ + k)
                for k in range(DT):
                    act.wait_ge(w_done, base + PER_HALF)
                    nc.scalar.activation(res[:, k, :], ps[:, k, :], ACT.Copy).then_inc(res_sb, 1)
                squares("mix", hf, lambda k: res[:, k, :], lambda k: act.wait_ge(res_sb, hf * DT + k + 1))
                root("mix", hf)
            for hf in range(NHF):
                base = FFN0 + hf * PER_FFN
                squares("n2", hf, lambda k: X1[:, k, :], lambda k: act.wait_ge(x1_in, 16 * (hf + 1)))
                root("n2", hf)
                modulate("n2", hf, (NHF + hf) * DT, a2, 3 * DT, hn2, h2hi)
                extra = [sum(1 for h in range(NHF) for t, (k, _j) in enumerate(PROJ)
                             if k == "gate" and (h * PER_HALF + t) % 2 == s) for s in range(2)]

                def split_hi_f(n0, f2):
                    act.wait_ge(raw_in[n0 % 2], f2 * 8 + 16 * (n0 // 2 + 1 + extra[n0 % 2]))
                    act.wait_ge(w_done, f2 + (n0 - 1))
                    nc.scalar.activation(whi[:, n0 % 2, :], raw[:, n0 % 2, :], ACT.Copy).then_inc(w_hi, 1)

                split_hi_f(base, 0)
                split_hi_f(base + 1, 0)
                if hf:
                    act.wait_ge(y_out, 16 * TT * hf)

                def gate_up(f, more):
                    if more:
                        split_hi_f(base + 2, f * 2)
                    act.wait_ge(w_done, f * 2 + (base + 1))
                    act.wait_ge(a_ok, f + hf * FT)
                    nc.scalar.activation(sg[:], ps[:, 0, :], ACT.Silu).then_inc(silu_ok, 1)
                    if more:
                        split_hi_f(base + 3, f * 2)
                    act.wait_ge(a_ok, f + (hf * FT + 1))
                    nc.scalar.activation(ahi[:, bass.ds(f, 1), :].rearrange("p a n -> p (a n)"), aa[:], ACT.Copy
                                         ).then_inc(a_hi, 1)

                with act.Fori(0, FT) as f:
                    gate_up(f, True)
                with act.Fori(0, FT // 2 - 1) as f:
                    for s in range(2):
                        split_hi_f(base + 2 * FT + 2 + s, f * 2)
                for k in range(DT):
                    act.wait_ge(w_done, base + PER_FFN)
                    nc.scalar.activation(fres[:, k, :], ps[:, k, :], ACT.Copy).then_inc(res_sb, 1)
                squares("ffn", hf, lambda k: fres[:, k, :], lambda k: act.wait_ge(res_sb, (NHF + hf) * DT + k + 1))
                root("ffn", hf)
                for t in range(TT):
                    for s in range(2):
                        act.wait_ge(ft_ps, hf * 2 * TT + 2 * t + s + 1)
                        nc.scalar.activation(osum[:, t, s * HALF:(s + 1) * HALF], ps[:, 2 * t + s, :],
                                             ACT.Copy).then_inc(ft_sb, 1)

        @block.vector
        def _(dve):
            ch = Chain(dve, dchain)

            def split_lo(n):
                dve.wait_ge(w_hi, n + 1)
                nc.vector.tensor_tensor(wlo[:, n % 2, :], raw[:, n % 2, :], whi[:, n % 2, :].bitcast(F32),
                                        ALU.subtract).then_inc(w_lo, 1)

            def sum_squares(norm, hf, width):
                i, at, n = NORM[norm, hf]
                for k in range(n):
                    dve.wait_ge(sq_done, at + k + 1)
                    if k == 0:
                        if i:
                            dve.wait_ge(rstd_ok, i)
                        nc.vector.tensor_copy(ssum[:], sq[:, (at + k) % 2, :]).then_inc(ssum_done, 1)
                    else:
                        dve.wait_ge(ssum_done, at + k)
                        nc.vector.tensor_tensor(ssum[:], ssum[:], sq[:, (at + k) % 2, :], ALU.add).then_inc(ssum_done, 1)
                dve.wait_ge(ms_ps, i + 1)
                nc.vector.tensor_scalar(ssum[:], ps[:, ms_bank(norm), :], 1.0 / width, EPS, ALU.mult, ALU.add
                                        ).then_inc(ms_sb, 1)
                dve.wait_ge(rms_sb, i + 1)
                nc.vector.reciprocal(rstd[:], ssum[:]).then_inc(rstd_ok, 1)
                dve.wait_ge(rstd_ok, i + 1)

            def normed(m0, src, tn_, hn_, hi_, lo_):
                for k in range(DT + 1):
                    if k < DT:
                        if m0 + k >= 2:
                            dve.wait_ge(hn_done, m0 + k - 1)
                        nc.vector.tensor_tensor(tn_[:, k % 2, :], src[:, k, :], rstd[:], ALU.mult).then_inc(tn_done, 1)
                    if k:
                        dve.wait_ge(h_hi, m0 + k)
                        nc.vector.tensor_tensor(lo_[:, k - 1, :], hn_[:, (k - 1) % 2, :], hi_[:, k - 1, :].bitcast(F32),
                                                ALU.subtract).then_inc(h_lo, 1)

            def mod_part(part, wm_, macc_):
                for k in range(DT):
                    m = part * DT + k
                    dve.wait_ge(mod_in[m % 2], 16 * (m // 2 + 1))
                    if k == 0:
                        dve.wait_ge(silu_c, 1)
                        if part > 1:
                            dve.wait_ge(mod_sum, part)
                        nc.vector.tensor_scalar(macc_[:], wm_[:, m % 2, :], siluc[:, k:k + 1], None, ALU.mult
                                                ).then_inc(mod_acc, 1)
                    else:
                        dve.wait_ge(mod_acc, m)
                        nc.vector.scalar_tensor_tensor(macc_[:], wm_[:, m % 2, :], siluc[:, k:k + 1], macc_[:],
                                                       ALU.mult, ALU.add).then_inc(mod_acc, 1)

            def mod_vectors(part):
                dve.wait_ge(mod_sum, part + 1)
                if part == 0:
                    dve.wait_ge(vec_ok, 1)
                n = MODC // P
                s = slice(part * n, (part + 1) * n)
                ch.inc(nc.vector.tensor_tensor(modT[:, s], ps[:, 7, 0:n], bmodT[:, s], ALU.add))
                ch.wait()
                if part == 0:
                    r = nc.vector.scalar_tensor_tensor(a1[:], modT[:, DT:2 * DT], 1.0, g1T, ALU.add, ALU.mult)
                elif part == 1:
                    r = nc.vector.tensor_tensor(cm[:], modT[:, 2 * DT:3 * DT], gpmT, ALU.mult)
                else:
                    ch.inc(nc.vector.scalar_tensor_tensor(a2[:], modT[:, 4 * DT:5 * DT], 1.0, g2T, ALU.add, ALU.mult))
                    r = nc.vector.tensor_tensor(cf[:], modT[:, 5 * DT:6 * DT], gpfT, ALU.mult)
                r.then_inc(mod_ready, 1)
                dve.wait_ge(mod_ready, part + 1)
                ch.wait()

            def residual(hf, m0, src, coef, xt):
                for k in range(DT):
                    ch.inc(nc.vector.tensor_tensor(src[:, k, :], src[:, k, :], rstd[:], ALU.mult))
                ch.wait()
                for k in range(DT):
                    nc.vector.scalar_tensor_tensor(xt[:, k, :], src[:, k, :], coef[:, k:k + 1], xt[:, k, :],
                                                   ALU.mult, ALU.add).then_inc(x1_ok, 1)

            nv = 0
            for hf in range(NHF):
                base = hf * PER_HALF
                if hf == 0:
                    mod_part(0, wm0, macc0)
                sum_squares("n1", hf, D)
                if hf == 0:
                    mod_vectors(0)
                normed(hf * DT, XT, tn, hn, hhi, hlo)
                dve.wait_ge(h_lo, (hf + 1) * DT)
                if hf == 0:
                    ch.inc(nc.vector.memset(cin[0:HD, :, :, :, 0:1], 0.0))
                    nc.vector.memset(z[:, 0:2], 0.0).then_inc(pj_free, 2)
                    ch.wait()
                split_lo(base)
                split_lo(base + 1)
                ev = hf * 6
                for t, (kind, j) in enumerate(PROJ):
                    T = hf * NPROJ + t
                    if t + 2 < NPROJ:
                        split_lo(base + t + 2)
                    bank = ps[:, B_PJ + t % 2, :]
                    dve.wait_ge(w_done, base + t + 1)
                    if kind in ("kcmp", "vcmp"):
                        kv = ("kcmp", "vcmp").index(kind)
                        v = bank.rearrange("p (c l) -> p l c", l=CMP_STRIDE)
                        if hf:
                            nc.vector.tensor_copy(cin[0:HD, kv, :, :, 0], acar[:, kv, :, :])
                        for g in range(N_KV):
                            gs = slice(g * HD, (g + 1) * HD)
                            pa = posT[gs, 0:CMP_STRIDE].unsqueeze(2).to_broadcast([HD, CMP_STRIDE, CPH - 1])
                            pb = posT[gs, CMP_STRIDE:CMP_LEN].unsqueeze(2).to_broadcast([HD, CMP_STRIDE, CPH])
                            nc.vector.tensor_tensor(cin[0:HD, kv, :, g, 1:CPH], v[gs, :, 0:CPH - 1], pa, ALU.add)
                            r = nc.vector.tensor_tensor(cin[HD:P, kv, :, g, :], v[gs, :, :], pb, ALU.add)
                            if hf == 0:
                                r = nc.vector.tensor_tensor(acar[:, kv, :, g], v[gs, :, CPH - 1],
                                                            posT[gs, 0:CMP_STRIDE], ALU.add)
                        r.then_inc(pj_free, 1)
                    elif kind in ("ksel", "kwin"):
                        ev += 1
                        dve.wait_ge(ev_a, ev)
                        o = N_CMP + (SEQ if kind == "kwin" else 0) + hf * HALF
                        for g in range(N_KV):
                            r = nc.vector.tensor_tensor(KS[HD:P, g, o:o + HALF], bank[g * HD:(g + 1) * HD, :],
                                                        KS[0:HD, g, o:o + HALF].bitcast(F32), ALU.subtract)
                        r.then_inc(pj_free, 1)
                    elif kind == "q":
                        ev += 1
                        dve.wait_ge(ev_a, ev)
                        for s in range(2):
                            h = 2 * j + s
                            for r_ in range(2):
                                r = nc.vector.scalar_tensor_tensor(
                                    qlo[r_ * HD:(r_ + 1) * HD, h, :], bank[s * HD:(s + 1) * HD, :],
                                    -(2.0 ** (h + 1)) / 8.0, qhi[r_ * HD:(r_ + 1) * HD, h, :].bitcast(F32),
                                    ALU.mult, ALU.subtract)
                        r.then_inc(pj_free, 1)
                    elif kind == "cv":
                        dve.wait_ge(pj_free, T + 2)
                        ch.wait()
                        if hf:
                            ch.inc(nc.vector.tensor_copy(z[:, 0:2], zcar[:, j, :]))
                        nc.vector.tensor_tensor(z[:, 2:HALF + 2], bank, cc_sb[:], ALU.mult).then_inc(pj_free, 1)
                        dve.wait_ge(pj_free, T + 3)
                        if hf:
                            ch.wait()
                        if hf == 0:
                            ch.inc(nc.vector.tensor_copy(zcar[:, j, :], z[:, HALF:HALF + 2]))
                        ch.inc(nc.vector.tensor_scalar(zc[:], z[:, 2:HALF + 2], cw2[:, j:j + 1], None, ALU.mult))
                        ch.wait()
                        ch.inc(nc.vector.scalar_tensor_tensor(zc[:], z[:, 1:HALF + 1], cw1[:, j:j + 1], zc[:],
                                                              ALU.mult, ALU.add))
                        ch.wait()
                        ch.inc(nc.vector.scalar_tensor_tensor(zc[:], z[:, 0:HALF], cw0[:, j:j + 1], zc[:],
                                                              ALU.mult, ALU.add))
                        ch.wait()
                        nc.vector.tensor_tensor(yc[:, j, :], zc[:], cb_sb[:], ALU.mult).then_inc(conv_y, 1)
                    else:
                        dst = {"vsel": vtmp[:, 0, :], "vwin": vtmp[:, 1, :], "gate": vtmp[:, 2, :],
                               "cb": cb_sb[:], "cc": cc_sb[:]}[kind]
                        if kind == "cb" and T > j:
                            dve.wait_ge(conv_y, hf * CT + j)
                        nc.vector.tensor_copy(dst, bank).then_inc(pj_free, 1)
                for s in range(2):
                    dve.wait_ge(vt_hi, hf * 2 + s + 1)
                    nc.vector.tensor_tensor(VS[:, s, hf * TT:(hf + 1) * TT, :, HD:P],
                                            ps[:, 4 + s, :].rearrange("p (t g d) -> p t g d", t=TT, g=N_KV),
                                            VS[:, s, hf * TT:(hf + 1) * TT, :, 0:HD].bitcast(F32),
                                            ALU.subtract).then_inc(vt_ok, 1)
                dve.wait_ge(gate_exp, hf + 1)
                ch.inc(nc.vector.tensor_scalar(gate[:], gate[:], 1.0, None, ALU.add))
                ch.wait()
                ch.inc(nc.vector.reciprocal(gate[:], gate[:]))
                ch.wait()
                if hf == 0:
                    gv = gate[:, 0, :].rearrange("p (h b) -> p h b", b=3)[:, :, 0]
                    ch.inc(nc.vector.tensor_scalar(gv, gv, nz[:], None, ALU.mult))
                    ch.wait()
                dve.wait_ge(kc_hi, hf + 1)
                ch.inc(nc.vector.tensor_tensor(KS[HD:P, :, CPH * hf:CPH * (hf + 1)],
                                               ps[0:HD, 7, 0:N_KV * CPH].rearrange("p (g c) -> p g c", g=N_KV),
                                               KS[0:HD, :, CPH * hf:CPH * (hf + 1)].bitcast(F32), ALU.subtract))
                nc.vector.tensor_tensor(VC[CPH * hf:CPH * (hf + 1), :, HD:P],
                                        ps[0:CPH, 7, 128:256].rearrange("p (g d) -> p g d", g=N_KV),
                                        VC[CPH * hf:CPH * (hf + 1), :, 0:HD].bitcast(F32),
                                        ALU.subtract).then_inc(kc_ok, 1)
                sum_squares("conv", hf, D_CONV)
                for k in range(CT):
                    nc.vector.tensor_tensor(yc[:, k, :], yc[:, k, :], rstd[:], ALU.mult).then_inc(conv_n, 1)
                for k in range(CT):
                    dve.wait_ge(conv_hi, hf * CT + k + 1)
                    nc.vector.scalar_tensor_tensor(yclo[:, k, :], yc[:, k, :], gcT[:, k:k + 1],
                                                   ychi[:, k, :].bitcast(F32), ALU.mult, ALU.subtract
                                                   ).then_inc(conv_ok, 1)
                dve.wait_ge(conv_ok, (hf + 1) * CT)
                ch.inc(nc.vector.memset(prob[:, :, :, 0:1], 0.0))
                ch.wait()
                for what, u, i in ORDER[hf]:
                    qt, g = UNITS[hf][u]
                    U = hf * NU + u
                    ns = P * (qt + 1)
                    if what == "S":
                        slope = 2.0 ** -(g * HPG + i + 1)
                        first = max(0, qt - (WIN_T - 1))
                        nb = banks_before(hf, u, i)
                        if i == 0 and u >= 2:
                            dve.wait_ge(pt_ps, tiles_before(hf, u - 1))
                        done = set()
                        for b, pieces in enumerate(score_banks(qt, hf)):
                            dve.wait_ge(s_ps, nb + b + 1)
                            for branch, k0, n_, at in pieces:
                                br = ("cmp", "sel", "win").index(branch)
                                s = smin[:, U % 2, 3 * i + br:3 * i + br + 1]
                                if branch == "cmp":
                                    skip = 1
                                    tab = dist_cmp[:, 56 - 8 * qt + 1:56 - 8 * qt + n_]
                                    dst = prob[:, U % 2, i, 1:n_]
                                elif branch == "sel":
                                    skip = 0
                                    tab = dist_sel[:, k0 - P * qt + SEQ - P:k0 - P * qt + SEQ - P + n_]
                                    dst = prob[:, U % 2, i, N_CMP + k0:N_CMP + k0 + n_]
                                else:
                                    skip = 0
                                    tab = dist_win[:, k0 - P * qt + (WIN_T - 1) * P:k0 - P * qt + (WIN_T - 1) * P + n_]
                                    d0 = N_CMP + ns + k0 - P * first
                                    dst = prob[:, U % 2, i, d0:d0 + n_]
                                init = s if br in done else 3.0e38
                                if br in done:
                                    dve.wait_ge(s_used, nb + b)
                                done.add(br)
                                r = nc.vector.tensor_tensor_reduce(
                                    dst, ps[:, B_S + (nb + b) % NS_B, at + skip:at + n_], tab, slope, init,
                                    ALU.add, ALU.min, s)
                            r.then_inc(s_used, 1)
                    elif what == "W":
                        dve.wait_ge(e_done, 3 * HPG * (U + 1))
                        ch.inc(nc.vector.reciprocal(wgt[:, U % 2, :], ssumexp[:, U % 2, :]))
                        ch.wait()
                        nc.vector.tensor_tensor(wgt[:, U % 2, :], wgt[:, U % 2, :],
                                                gate[:, qt % TT, g * 3 * HPG:(g + 1) * 3 * HPG],
                                                ALU.mult).then_inc(wgt_ok, 1)
                    elif what == "T":
                        M = tiles_before(hf, u) + i
                        n_ = CPH * (hf + 1) if i == 0 else P
                        dve.wait_ge(pt_hi, M + 1)
                        nc.vector.tensor_tensor(ptl[0:n_, M % 2, :], ps[0:n_, B_PT + M % 2, :],
                                                pth[0:n_, M % 2, :].bitcast(F32), ALU.subtract).then_inc(pt_lo, 1)
                    elif what == "O1":
                        dve.wait_ge(o_sq, U + 1)
                        ch.inc(nc.vector.tensor_reduce(hs[:], oq[:, :, 0:HD], AX_X, ALU.add))
                        ch.wait()
                        nc.vector.tensor_scalar(hv[:], hs[:], 1.0 / HD, EPS, ALU.mult, ALU.add).then_inc(o_ms, 1)
                        dve.wait_ge(o_ms, U + 1)
                    elif what == "O2":
                        dve.wait_ge(y_hi, U + 1)
                        k0 = 2 * g
                        q0 = (qt % TT) * P
                        for k in range(2):
                            r = nc.vector.scalar_tensor_tensor(
                                yalo[:, k0 + k, q0:q0 + P], ps[:, B_OT, k * P:(k + 1) * P], gaT[:, k0 + k:k0 + k + 1],
                                yahi[:, k0 + k, q0:q0 + P].bitcast(F32), ALU.mult, ALU.subtract)
                        r.then_inc(y_ok, 1)
                for k in range(DT):
                    split_lo(base + NPROJ + k)
                if hf == 0:
                    for part in range(1, PARTS):
                        mod_part(part, wm, macc)
                        mod_vectors(part)
                sum_squares("mix", hf, D)
                dve.wait_ge(xr_in, 16 * (hf + 1))
                residual(hf, hf * DT, res, cm, XR)
            for hf in range(NHF):
                base = FFN0 + hf * PER_FFN
                sum_squares("n2", hf, D)
                normed((NHF + hf) * DT, X1, tn2, hn2, h2hi, h2lo)

                def split_lo_f(n0, f2):
                    dve.wait_ge(w_hi, f2 + (n0 + 1))
                    nc.vector.tensor_tensor(wlo[:, n0 % 2, :], raw[:, n0 % 2, :], whi[:, n0 % 2, :].bitcast(F32),
                                            ALU.subtract).then_inc(w_lo, 1)

                split_lo_f(base, 0)
                split_lo_f(base + 1, 0)
                with dve.Fori(0, FT) as f:
                    split_lo_f(base + 2, f * 2)
                    split_lo_f(base + 3, f * 2)
                    dve.wait_ge(silu_ok, f + (hf * FT + 1))
                    dve.wait_ge(w_done, f * 2 + (base + 2))
                    dve.wait_ge(a_lo, f + hf * FT)
                    nc.vector.tensor_tensor(aa[:], ps[:, 1, :], sg[:], ALU.mult).then_inc(a_ok, 1)
                    dve.wait_ge(a_hi, f + (hf * FT + 1))
                    nc.vector.tensor_tensor(alo[:, bass.ds(f, 1), :].rearrange("p a n -> p (a n)"), aa[:],
                                            ahi[:, bass.ds(f, 1), :].rearrange("p a n -> p (a n)").bitcast(F32),
                                            ALU.subtract).then_inc(a_lo, 1)
                with dve.Fori(0, FT // 2 - 1) as f:
                    for s in range(2):
                        split_lo_f(base + 2 * FT + 2 + s, f * 2)
                sum_squares("ffn", hf, D)
                residual(hf, (NHF + hf) * DT, fres, cf, X1)

        @block.tensor
        def _(pe):
            def mean_square(norm, hf):
                i, at, n = NORM[norm, hf]
                pe.wait_ge(ssum_done, at + n)
                nc.tensor.matmul(ps[:, ms_bank(norm), :], ones[:], ssum[:], start=True, stop=True).then_inc(ms_ps, 1)

            def three(dst, whi_, wlo_, mhi, mlo, start, stop):
                nc.tensor.matmul(dst, whi_, mhi, start=start, stop=False)
                nc.tensor.matmul(dst, whi_, mlo, start=False, stop=False)
                return nc.tensor.matmul(dst, wlo_, mhi, start=False, stop=stop)

            def feature_tile(dst, slot, hi_, lo_):
                for k in range(DT):
                    s = slice(k * P, (k + 1) * P)
                    r = three(dst, whi[:, slot, s], wlo[:, slot, s], hi_[:, k, :], lo_[:, k, :], k == 0, k == DT - 1)
                return r

            def row_tile(slot, mhi, mlo, start, stop):
                for m in range(DT):
                    s = slice(m * P, (m + 1) * P)
                    r = three(ps[:, m, :], whi[:, slot, s], wlo[:, slot, s], mhi, mlo, start, stop)
                return r

            def mod_sums(part, macc_):
                pe.wait_ge(mod_acc, (part + 1) * DT)
                for m in range(MODC // P):
                    r = nc.tensor.matmul(ps[:, 7, m:m + 1], macc_[:, m * P:(m + 1) * P], ones[:, 0:1],
                                         start=True, stop=True)
                r.then_inc(mod_sum, 1)

            pe.wait_ge(consts, 2)
            pe.wait_ge(small_in, 16 * (len(VEC_N) + N_KV))
            nc.tensor.transpose(ps[:, 0, 0:NVEC], vrow[:], ident[0:NVEC, 0:NVEC])
            nc.tensor.transpose(ps[:, 0, P:P + CMP_LEN], posr[:], ident[0:CMP_LEN, 0:CMP_LEN]).then_inc(vec_ps, 1)
            pe.wait_ge(vec_ok, 1)
            for hf in range(NHF):
                base = hf * PER_HALF
                pe.wait_ge(x_in, 16 * TT * (hf + 1))
                if hf:
                    pe.wait_ge(res_sb, hf * DT)
                    pe.wait_ge(ms_sb, NORM["mix", hf - 1][0] + 1)
                    pe.wait_ge(mod_ready, PARTS)
                for k in range(DT):
                    for t in range(TT):
                        r = nc.tensor.transpose(ps[:, k, t * P:(t + 1) * P], xin[:, t, k * P:(k + 1) * P], ident[:])
                    r.then_inc(xt_ps, 1)
                mean_square("n1", hf)
                if hf == 0:
                    mod_sums(0, macc0)
                pe.wait_ge(ms_sb, NORM["n1", hf][0] + 1)
                pe.wait_ge(h_lo, (hf + 1) * DT)

                def pj(t0, i2):
                    pe.wait_ge(w_lo, i2 + (base + t0 + 1))
                    pe.wait_ge(pj_free, i2 + (hf * NPROJ + t0 + 1))
                    feature_tile(ps[:, B_PJ + t0 % 2, :], (base + t0) % 2, hhi, hlo).then_inc(w_done, 1)

                with pe.Fori(0, NPROJ // 2) as i:
                    pj(0, i * 2)
                    pj(1, i * 2)
                pj(NPROJ - 1, 0)
                pe.wait_ge(pj_free, (hf + 1) * NPROJ + 2)
                pe.wait_ge(wc_in, 64 * (hf + 1))
                for kv in range(2):
                    for l_ in range(CMP_STRIDE):
                        r = nc.tensor.matmul(ps[:, 2 + kv, 0:N_KV * CPH], wc1[:, kv, l_, :],
                                             cin[:, kv, l_, :, :].rearrange("p g c -> p (g c)"),
                                             start=(l_ == 0), stop=(l_ == CMP_STRIDE - 1))
                    r.then_inc(cmp_ps, 1)
                for s in range(3):
                    for t in range(TT):
                        if s < 2:
                            r = nc.tensor.transpose(ps[:, 4 + s, t * P:(t + 1) * P], vtmp[:, s, t * P:(t + 1) * P],
                                                    ident[:])
                        else:
                            ng = 3 * N_HEADS
                            r = nc.tensor.transpose(ps[:, 6, t * ng:(t + 1) * ng], vtmp[0:ng, s, t * P:(t + 1) * P],
                                                    ident[0:ng, 0:ng])
                    r.then_inc(vt_ps, 1)
                pe.wait_ge(gelu_a, 2 * hf + 2)
                pe.wait_ge(wk2_in, 32)
                nc.tensor.matmul(ps[0:HD, 7, 0:N_KV * CPH], wk2[:, 0, :], ck[:, 0, :], start=True, stop=True)
                for g in range(N_KV):
                    r = nc.tensor.matmul(ps[0:CPH, 7, 128 + g * HD:128 + (g + 1) * HD],
                                         ck[:, 1, g * CPH:(g + 1) * CPH], wk2[:, 1, :], start=True, stop=True)
                r.then_inc(kc_ps, 1)
                mean_square("conv", hf)
                pe.wait_ge(kc_ok, hf + 1)
                pe.wait_ge(vt_ok, 2 * hf + 2)
                pe.wait_ge(ms_sb, NORM["conv", hf][0] + 1)
                pe.wait_ge(gate_exp, hf + 1)
                for what, u, i in ORDER[hf]:
                    qt, g = UNITS[hf][u]
                    U = hf * NU + u
                    q0 = (qt % TT) * P
                    if what == "S":
                        nb = banks_before(hf, u, i)
                        h = g * HPG + i
                        for b, pieces in enumerate(score_banks(qt, hf)):
                            if nb + b >= NS_B:
                                pe.wait_ge(s_used, nb + b - NS_B + 1)
                            for branch, k0, n_, at in pieces:
                                o = {"cmp": 0, "sel": N_CMP, "win": N_CMP + SEQ}[branch] + k0
                                dst = ps[:, B_S + (nb + b) % NS_B, at:at + n_]
                                nc.tensor.matmul(dst, qhi[:, h, q0:q0 + P], KS[:, g, o:o + n_], start=True, stop=False)
                                r = nc.tensor.matmul(dst, qlo[:, h, q0:q0 + P], KS[:, g, o:o + n_],
                                                     start=False, stop=True)
                            r.then_inc(s_ps, 1)
                    elif what == "T":
                        M = tiles_before(hf, u) + i
                        branch, kt = key_tiles(qt)[i]
                        if i == 0:
                            pe.wait_ge(p_ok, HPG * (U + 1))
                        if M >= 2:
                            pe.wait_ge(pt_lo, M - 1)
                        n_ = P
                        if branch == "cmp":
                            at, n_ = 0, CPH * (hf + 1)
                        elif branch == "sel":
                            at = N_CMP + P * kt
                        else:
                            at = N_CMP + P * (qt + 1) + P * (kt - max(0, qt - (WIN_T - 1)))
                        for h in range(HPG):
                            r = nc.tensor.transpose(ps[0:n_, B_PT + M % 2, h * P:(h + 1) * P],
                                                    prob[:, U % 2, h, at:at + n_], ident[:])
                        r.then_inc(pt_ps, 1)
                    elif what == "V":
                        M = tiles_before(hf, u) + i
                        tiles = key_tiles(qt)
                        branch, kt = tiles[i]
                        if i == 0 and U >= 2:
                            pe.wait_ge(o_sb, U - 1)
                        pe.wait_ge(pt_lo, M + 1)
                        if branch == "cmp":
                            n_ = CPH * (hf + 1)
                            v = VC[0:n_, g, :]
                        else:
                            n_ = P
                            v = VS[:, ("sel", "win").index(branch), kt, g, :]
                        dst = ps[:, B_O + U % 2, :]
                        nc.tensor.matmul(dst, v, pth[0:n_, M % 2, :], start=(i == 0), stop=False)
                        nc.tensor.matmul(dst, v, ptl[0:n_, M % 2, :], start=False, stop=(i == len(tiles) - 1)
                                         ).then_inc(pv_done, 1)
                    elif what == "O1":
                        pe.wait_ge(o_sb, U + 1)
                        if U:
                            pe.wait_ge(y_ok, U)
                        for h in range(HPG):
                            r = nc.tensor.transpose(ps[:, B_OT, h * P:(h + 1) * P], osb[:, h * P:(h + 1) * P], ident[:])
                        r.then_inc(ot_ps, 1)
                    elif what == "O2":
                        pe.wait_ge(o_norm, U + 1)
                        for k in range(2):
                            r = nc.tensor.transpose(ps[:, B_OT, k * P:(k + 1) * P],
                                                    ob[:, 2 * k:2 * k + 2, :].rearrange("p h d -> p (h d)"), ident[:])
                        r.then_inc(y_ps, 1)
                pe.wait_ge(conv_ok, (hf + 1) * CT)
                pe.wait_ge(y_ok, (hf + 1) * NU)
                for k in range(DT):
                    n = base + NPROJ + k
                    pe.wait_ge(w_lo, n + 1)
                    hi_, lo_ = (ychi, yclo) if k < CT else (yahi, yalo)
                    row_tile(n % 2, hi_[:, k % CT, :], lo_[:, k % CT, :], k == 0, k == DT - 1).then_inc(w_done, 1)
                if hf == 0:
                    pe.wait_ge(res_sb, DT)
                    for part in range(1, PARTS):
                        mod_sums(part, macc)
                mean_square("mix", hf)
            for hf in range(NHF):
                base = FFN0 + hf * PER_FFN
                mean_square("n2", hf)
                pe.wait_ge(ms_sb, NORM["n2", hf][0] + 1)
                pe.wait_ge(h_lo, (NHF + hf + 1) * DT)
                with pe.Fori(0, FT) as f:
                    pe.wait_ge(w_lo, f * 2 + (base + 1))
                    pe.wait_ge(silu_ok, f + hf * FT)
                    feature_tile(ps[:, 0, :], base % 2, h2hi, h2lo).then_inc(w_done, 1)
                    pe.wait_ge(w_lo, f * 2 + (base + 2))
                    pe.wait_ge(a_ok, f + hf * FT)
                    feature_tile(ps[:, 1, :], (base + 1) % 2, h2hi, h2lo).then_inc(w_done, 1)
                pe.wait_ge(a_lo, (hf + 1) * FT)

                def down(s, f2, start, stop):
                    n = FFN0 + hf * PER_FFN + 2 * FT + s
                    pe.wait_ge(w_lo, f2 + (n + 1))
                    f = bass.ds(f2 + s, 1)
                    row_tile(n % 2, ahi[:, f, :].rearrange("p a n -> p (a n)"),
                             alo[:, f, :].rearrange("p a n -> p (a n)"), start, stop).then_inc(w_done, 1)

                down(0, 0, True, False)
                down(1, 0, False, False)
                with pe.Fori(1, FT // 2 - 1) as i:
                    down(0, i * 2, False, False)
                    down(1, i * 2, False, False)
                down(0, FT - 2, False, False)
                down(1, FT - 2, False, True)
                mean_square("ffn", hf)
                pe.wait_ge(x1_ok, (NHF + hf + 1) * DT)
                for t in range(TT):
                    for s in range(2):
                        for k in range(4):
                            r = nc.tensor.transpose(ps[:, 2 * t + s, k * P:(k + 1) * P],
                                                    X1[:, 4 * s + k, t * P:(t + 1) * P], ident[:])
                        r.then_inc(ft_ps, 1)
                pe.wait_ge(ft_sb, (hf + 1) * 2 * TT)


_INS = ["x", "c", "w_mod", "b_mod", "g_pre_mix", "w_in", "conv_w", "pos_cmp", "w_ck1", "w_ck2", "w_cv1", "w_cv2",
        "g_conv_out", "g_attn_out", "w_out", "g_post_mix", "g_pre_ffn", "w_gate", "w_up", "w_down", "g_post_ffn"]


def kernel(**inputs):
    import concourse.bacc as _bacc
    from concourse.bass_utils import run_bass_kernel_spmd as _run

    nc = _bacc.Bacc("TRN2", target_bir_lowering=False, num_devices=1)
    arrays, args = {}, []
    for name in _INS:
        a = np.ascontiguousarray(inputs[name])
        arrays[f"in_{name}"] = a
        args.append(nc.dram_tensor(f"in_{name}", a.shape, mybir.dt.from_np(a.dtype), kind="ExternalInput").ap())
    out = nc.dram_tensor("out_x", [1, SEQ, D], F32, kind="ExternalOutput").ap()
    build(nc, *args, out)
    r = _run(nc, [arrays], core_ids=[0])
    return r.results[0]["out_x"]
```

```python
from contextlib import ExitStack

import numpy as np

import concourse.bass as bass
from concourse import mybir

F32 = mybir.dt.float32
F32R = mybir.dt.float32r
ALU = mybir.AluOpType
ACT = mybir.ActivationFunctionType
AX_X = mybir.AxisListType.X

P = 128
SEQ = 1024
D = 1024
DT = D // P
HALF = 512
NHF = SEQ // HALF
TT = HALF // P
D_CONV = 512
CT = D_CONV // P
N_KV, HPG, HD = 2, 4, 64
N_HEADS = N_KV * HPG
CMP_STRIDE = 16
CMP_LEN = 32
N_CMP = SEQ // CMP_STRIDE
CPH = N_CMP // NHF
WIN_T = 5
D_FF = 2816
FT = D_FF // P
COL_Q, COL_KV, COL_G = 1536, 2048, 2816
BIG = 1e30
EPS = 1e-6

PROJ = ([("kcmp", 0), ("vcmp", 0), ("vsel", 0), ("vwin", 0), ("gate", 0), ("ksel", 0), ("kwin", 0)]
        + [("q", j) for j in range(CT)]
        + [(kind, j) for j in range(CT) for kind in ("cb", "cc", "cv")])
NPROJ = len(PROJ)
AFTER_CMP, AFTER_KC = 5, 7
MOD_TILES = {2: (0, 5, 7), 3: (6, 11, 13), 4: (12, 17, 19), 5: (18, NPROJ - 1, NPROJ - 1)}
PER_HALF = NPROJ + DT
FFN0 = NHF * PER_HALF
PEEL = 3
DOWN_K = [(0, DT), (DT, 2 * DT), (2 * DT, FT)]
PER_FFN = 2 * FT + len(DOWN_K) * DT
NTILES = FFN0 + NHF * PER_FFN

NORMS = [("n1", 0, DT), ("conv", 0, CT), ("n1", 1, DT), ("mix", 0, DT), ("conv", 1, CT), ("n2", 0, DT),
         ("mix", 1, DT), ("n2", 1, DT), ("ffn", 0, DT), ("ffn", 1, DT)]
NORM = {}
_at = 0
for _i, (_name, _h, _n) in enumerate(NORMS):
    NORM[_name, _h] = (_i, _at, _n)
    _at += _n

VEC_N = (DT, 6 * DT, DT, DT, DT, DT, CT, CT, CT, CT, CT)
VEC_AT = [(sum(VEC_N[:i]), sum(VEC_N[:i + 1])) for i in range(len(VEC_N))]
NVEC = sum(VEC_N)

MIX_SQUARES = {3: (0, 1), 4: (2, 3), 5: (4, 5), 6: (6,), 7: (7,)}
LAG = 2
WLAG = 2
FRONT = 1.5
PARTS = 6
NM = 4


def attention_order(hf):
    units = [(qt, g) for qt in range(TT * hf, TT * hf + TT) for g in range(N_KV)]

    def scores(u):
        nb = len(score_banks(units[u][0], hf))
        steps = []
        for h in range(HPG):
            for b in range(nb):
                steps.append(("S", u, (h, b)))
                if b == WLAG - 1 and h:
                    steps.append(("W", u, h - 1))
        return steps + [("W", u, HPG - 1)]

    order = scores(0) + [("N1", 0, 0)]
    for u, (qt, g) in enumerate(units):
        n = len(key_tiles(qt))
        nxt = scores(u + 1) if u + 1 < len(units) else []
        total = len(nxt)
        fin = [("O1", u - 1, 0), ("O2", u - 1, 0)] if u else []
        for i in range(n):
            order.append(("T", u, i))
            if i >= LAG:
                order.append(("V", u, i - LAG))
            if i == 1:
                order += fin[:1] if u else [("N2", 0, 0)]
            if i == min(5, n - 1):
                order += fin[1:]
            while nxt and (total - len(nxt)) < (i + 1) * total * FRONT / n:
                order.append(nxt.pop(0))
        order += nxt
        order += [("V", u, i) for i in range(n - LAG, n)] + [("C", u, 0)]
    order += [("O1", len(units) - 1, 0), ("O2", len(units) - 1, 0)]
    return units, order


def delayed(order, kinds):
    out, held = [], []
    last = {u: i for what, u, i in order if what == "T"}
    at = None
    for step in order:
        if step[0] == "T":
            out += [step] + held
            held, at = [], step
        elif step[0] in kinds and at and at[2] < last[at[1]]:
            held.append(step)
        else:
            out.append(step)
    return out


def key_tiles(qt):
    first = max(0, qt - (WIN_T - 1))
    return [("cmp", 0)] + [("sel", k) for k in range(qt + 1)] + [("win", k) for k in range(first, qt + 1)]


def score_banks(qt, hf):
    wc = CPH * (hf + 1)
    sel = P * (qt + 1)
    first = max(0, qt - (WIN_T - 1))
    win = P * (qt + 1 - first)
    banks = [[("cmp", 0, wc, 0)]]
    if win > 512:
        banks[0].append(("win", P * first + 512, win - 512, 64))
    banks.append([("win", P * first, min(win, 512), 0)])
    for c in range(0, sel, 512):
        banks.append([("sel", c, min(512, sel - c), 0)])
    return banks


UNITS, ORDER, ORDER_DVE, ORDER_ACT = {}, {}, {}, {}
for _h in range(NHF):
    UNITS[_h], ORDER[_h] = attention_order(_h)
    ORDER_DVE[_h] = delayed(ORDER[_h], ("W",))
    ORDER_ACT[_h] = delayed(ORDER[_h], ("S",))
NU = len(UNITS[0])


def tiles_before(hf, u):
    return sum(len(key_tiles(qt)) for h in range(hf + 1) for v, (qt, g) in enumerate(UNITS[h]) if (h, v) < (hf, u))


def banks_before(hf, u, h):
    n = 0
    for a in range(hf + 1):
        for v, (qt, g) in enumerate(UNITS[a]):
            if (a, v) < (hf, u):
                n += HPG * len(score_banks(qt, a))
            elif (a, v) == (hf, u):
                n += h * len(score_banks(qt, a))
    return n


def build(nc, x, c, w_mod, b_mod, g_pre_mix, w_in, conv_w, pos_cmp, w_ck1, w_ck2, w_cv1, w_cv2,
          g_conv_out, g_attn_out, w_out, g_post_mix, g_pre_ffn, w_gate, w_up, w_down, g_post_ffn, out):
    xin_v = x[0].rearrange("(t p) d -> t p d", p=P)
    out_v = out[0].rearrange("(t p) d -> t p d", p=P)
    xT_dram = nc.dram_tensor("xT_dram", [NHF, P, DT * HALF], F32, kind="Internal").ap()
    x1_dram = nc.dram_tensor("x1_dram", [NHF, P, DT * HALF], F32, kind="Internal").ap()

    keep = ExitStack()
    with keep:
        def alloc(stack):
            def sb(name, shape, dt=F32):
                return stack.enter_context(nc.sbuf_tensor(name, shape, dt))
            return sb

        def sem(name):
            return keep.enter_context(nc.semaphore(name))

        sb = alloc(keep)
        raw = sb("raw", [P, 2, D])
        whi = sb("whi", [P, 2, D], F32R)
        wlo = sb("wlo", [P, 2, D], F32R)
        ident = sb("ident", [P, P])
        ones = sb("ones", [P, P])
        dist_sel = sb("dist_sel", [P, SEQ])
        dist_win = sb("dist_win", [P, WIN_T * P])
        dist_cmp = sb("dist_cmp", [P, 120])
        sq = sb("sq", [P, 2, HALF])
        ssum = sb("ssum", [P, HALF])
        rstd = sb("rstd", [P, HALF])
        vcol = sb("vcol", [P, NVEC])
        cT, bmodT, g1T, gpmT, g2T, gpfT, gcT, gaT, cw0, cw1, cw2 = (vcol[:, a:b] for a, b in VEC_AT)
        siluc = sb("siluc", [P, DT])
        modT = sb("modT", [P, 6 * DT])
        a1 = sb("a1", [P, DT])
        a2 = sb("a2", [P, DT])
        cm = sb("cm", [P, DT])
        cf = sb("cf", [P, DT])
        posT = sb("posT", [P, CMP_LEN])
        smin = sb("smin", [P, 2, 3 * HPG])
        ssumexp = sb("ssumexp", [P, 2, 3 * HPG])
        wgt = sb("wgt", [P, 2, 3 * HPG])
        nz = sb("nz", [P, 1])
        gate = sb("gate", [P, TT, 3 * N_HEADS])
        zcar = sb("zcar", [P, CT, 2])
        hs = sb("hs", [P, HPG])
        hv = sb("hv", [P, HPG])
        hr = sb("hr", [P, HPG])
        half_neg = sb("half_neg", [P, HPG])

        mixer = ExitStack()
        sb = alloc(mixer)
        KS = sb("KS", [P, N_KV, N_CMP + 2 * SEQ], F32R)
        VS = sb("VS", [P, 2, SEQ // P, N_KV, P], F32R)
        VC = sb("VC", [N_CMP, N_KV, P], F32R)
        wk2 = sb("wk2", [P, 2, HD])
        acar = sb("acar", [HD, 2, CMP_STRIDE, N_KV])
        attn = ExitStack()
        sb = alloc(attn)
        qhi = sb("qhi", [P, N_HEADS, HALF], F32R)
        qlo = sb("qlo", [P, N_HEADS, HALF], F32R)
        yahi = sb("yahi", [P, CT, HALF], F32R)
        yalo = sb("yalo", [P, CT, HALF], F32R)
        ychi = sb("ychi", [P, CT, HALF], F32R)
        yclo = sb("yclo", [P, CT, HALF], F32R)
        PW = N_CMP + SEQ + WIN_T * P
        prob1 = sb("prob1", [P, 2, HPG, PW])
        pth = sb("pth", [P, 2, HALF], F32R)
        ptl = sb("ptl", [P, 2, HALF], F32R)
        osb = sb("osb", [P, HALF])
        oq = sb("oq", [P, HPG, P])
        ob = sb("ob", [P, HPG, HD])
        attn.close()
        first = ExitStack()
        sb = alloc(first)
        sb("under_q0", [P, 2, DT, HALF])
        sb("under_y0", [P, 4, CT, HALF])
        prob0 = sb("prob0", [P, 2, HPG, N_CMP + 2 * HALF])
        sb("between", [P, 2 * P])
        xin1 = sb("xin1", [P, TT, D])
        prob = (prob0, prob1)
        first.close()
        proj = ExitStack()
        sb = alloc(proj)
        xin0 = sb("xin0", [P, TT, D])
        XT = sb("XT", [P, DT, HALF])
        wc1 = sb("wc1", [P, 2, CMP_STRIDE, P])
        sb("under_conv_out", [P, 2, CT, HALF])
        hhi = sb("hhi", [P, DT, HALF], F32R)
        hlo = sb("hlo", [P, DT, HALF], F32R)
        macc = sb("macc", [P, 2, D])
        cin = sb("cin", [P, 2, CMP_STRIDE, N_KV, CPH])
        vtmp = sb("vtmp", [P, 3, HALF])
        cc_sb = sb("cc_sb", [P, HALF])
        cb_sb = sb("cb_sb", [P, HALF])
        z = sb("z", [P, HALF + 2])
        zc = sb("zc", [P, HALF])

        ck = sb("ck", [P, 2, N_KV * CPH])
        vrow = sb("vrow", [NVEC, P])
        posr = sb("posr", [CMP_LEN, P])
        proj.close()
        convv = ExitStack()
        sb = alloc(convv)
        sb("under_x2", [P, 2, DT, HALF])
        sb("under_yahi", [P, CT, HALF])
        yc = sb("yc", [P, CT, HALF])
        wm = sb("wm", [P, NM, D])
        xin = (xin0, xin1)
        convv.close()
        nrm = ExitStack()
        sb = alloc(nrm)
        sb("under_x", [P, 2, DT, HALF])
        sb("under_conv_w", [P, 2, 2 * CT, HALF])
        sb("under_h", [P, 2, DT, HALF])
        sb("under_macc", [P, 2, D])
        tn = sb("tn", [P, 2, HALF])
        hn = sb("hn", [P, 2, HALF])
        nrm.close()
        post = ExitStack()
        sb = alloc(post)
        res0 = sb("res0", [P, DT, HALF])
        sb("under_y", [P, 2 * DT, HALF])
        XR = sb("XR", [P, DT, HALF])
        post.close()
        mixer.close()
        ffn = ExitStack()
        sb = alloc(ffn)
        h2hi = sb("h2hi", [P, DT, HALF], F32R)
        h2lo = sb("h2lo", [P, DT, HALF], F32R)
        ahi = sb("ahi", [P, FT, HALF], F32R)
        alo = sb("alo", [P, FT, HALF], F32R)
        X1 = sb("X1", [P, DT, HALF])
        fres = sb("fres", [P, DT, HALF])
        ffn.close()
        ffn2 = ExitStack()
        sb = alloc(ffn2)
        sb("under_h2", [P, 2, DT, HALF])
        sb("under_a", [P, 2, FT, HALF])
        sb("under_x1", [P, 2, DT, HALF])
        tn2 = sb("tn2", [P, 2, HALF])
        hn2 = sb("hn2", [P, 2, HALF])
        sg = sb("sg", [P, HALF])
        aa = sb("aa", [P, HALF])
        ffn2.close()
        outv = ExitStack()
        sb = alloc(outv)
        sb("under_h3", [P, 2, DT, HALF])
        sb("under_a3", [P, 2, FT, HALF])
        sb("under_x3", [P, DT, HALF])
        osum = sb("osum", [P, TT, D])
        res = (res0, fres)
        outv.close()

        ps = keep.enter_context(nc.psum_tensor("ps", [P, 8, HALF], F32))
        B_PJ, B_S, NS_B, B_PT, NPT, B_O, NO, B_OT = 0, 0, 3, 3, 3, 6, 1, 7
        B_Y, NY = 0, 2
        B_GU = 2
        B_X1, NX1 = 2, 4
        B_OUT = (0, 1, 6)

        small_in = sem("small_in")
        consts = sem("consts")
        raw_in = [sem("raw_in0"), sem("raw_in1")]
        w_hi = sem("w_hi")
        w_lo = sem("w_lo")
        w_done = sem("w_done")
        mod_in = [sem(f"mod_in{s}") for s in range(NM)]
        mod_acc = sem("mod_acc")
        mod_sum = sem("mod_sum")
        mod_ready = sem("mod_ready")
        vec_ps = sem("vec_ps")
        vec_ok = sem("vec_ok")
        wk2_in = sem("wk2_in")
        silu_c = sem("silu_c")
        x_in = sem("x_in")
        xt_ps = sem("xt_ps")
        xt_sb = sem("xt_sb")
        xt_out = sem("xt_out")
        sq_done = sem("sq_done")
        ssum_done = sem("ssum_done")
        ms_ps = sem("ms_ps")
        ms_sb = sem("ms_sb")
        rms_sb = sem("rms_sb")
        rstd_ok = sem("rstd_ok")
        tn_done = sem("tn_done")
        hn_done = sem("hn_done")
        h_hi = sem("h_hi")
        h_lo = sem("h_lo")
        pj_free = sem("pj_free")
        ev_a = sem("ev_a")
        vt_ps = sem("vt_ps")
        vt_hi = sem("vt_hi")
        vt_ok = sem("vt_ok")
        gate_exp = sem("gate_exp")
        gate_ok = sem("gate_ok")
        wc_in = sem("wc_in")
        cmp_ps = sem("cmp_ps")
        gelu_a = sem("gelu_a")
        kc_ps = sem("kc_ps")
        kc_hi = sem("kc_hi")
        kc_ok = sem("kc_ok")
        conv_y = sem("conv_y")
        conv_n = sem("conv_n")
        conv_hi = sem("conv_hi")
        conv_ok = sem("conv_ok")
        s_ps = sem("s_ps")
        s_used = sem("s_used")
        e_done = sem("e_done")
        wgt_ok = sem("wgt_ok")
        p_ok = sem("p_ok")
        pt_ps = sem("pt_ps")
        pt_hi = sem("pt_hi")
        pt_lo = sem("pt_lo")
        pv_done = sem("pv_done")
        o_sb = sem("o_sb")
        ot_ps = sem("ot_ps")
        oq_sb = sem("oq_sb")
        o_sum = sem("o_sum")
        o_sq = sem("o_sq")
        o_ms = sem("o_ms")
        o_rstd = sem("o_rstd")
        o_norm = sem("o_norm")
        y_ps = sem("y_ps")
        y_hi = sem("y_hi")
        y_ok = sem("y_ok")
        res_sb = sem("res_sb")
        xr_in = sem("xr_in")
        x1_ok = sem("x1_ok")
        x1_out = sem("x1_out")
        x1_in = sem("x1_in")
        silu_ok = sem("silu_ok")
        a_ok = sem("a_ok")
        a_hi = sem("a_hi")
        a_lo = sem("a_lo")
        ft_ps = sem("ft_ps")
        ft_sb = sem("ft_sb")
        y_out = sem("y_out")
        dchain = sem("dchain")
        achain = sem("achain")
        pchain = sem("pchain")
        echain = sem("echain")

        def mod_bank(part):
            return ps[:, 2 + part % 2, 0:DT]

        def tile_width(n):
            t = (n - FFN0) % PER_FFN - 2 * FT
            k0, k1 = DOWN_K[t % len(DOWN_K)] if n >= FFN0 and t >= 0 else (0, DT)
            return (k1 - k0) * P

        block = keep.enter_context(nc.Block())

        class Chain:
            def __init__(self, eng, s):
                self.eng, self.s, self.n = eng, s, 0

            def inc(self, ins):
                ins.then_inc(self.s, 1)
                self.n += 1

            def wait(self):
                self.eng.wait_ge(self.s, self.n)

        @block.sync
        def _(sp):
            def small(dst, src):
                sp.dma_start(dst, src).then_inc(small_in, 16)

            def load_raw(n, src):
                if n >= 2:
                    sp.wait_ge(w_lo, n - 1)
                for dst, s in src:
                    sp.dma_start(dst, s).then_inc(raw_in[n % 2], 16)

            def tile_of(n, w, c0):
                return [(raw[:, n % 2, :].rearrange("p (k m) -> p k m", k=DT),
                         w[:, c0:c0 + P].rearrange("(k p) m -> p k m", p=P))]

            for (a, b), v in zip(VEC_AT, (c[0], b_mod[0], g_pre_mix[0], g_post_mix[0], g_pre_ffn[0], g_post_ffn[0],
                                          g_conv_out[0], g_attn_out[0], conv_w[0, 0], conv_w[0, 1], conv_w[0, 2])):
                small(vrow[a:b, :], v.rearrange("(k p) -> k p", p=P))
            for g in range(N_KV):
                small(posr[:, g * HD:(g + 1) * HD], pos_cmp[0])
            def load_w(n, w, c0):
                load_raw(n, tile_of(n, w, c0))

            def gate_up_pair(base, f2):
                for s in range(2):
                    for w_, w in enumerate((w_gate, w_up)):
                        sp.wait_ge(w_lo, f2 * 2 + (base + 2 * s + w_ - 1))
                        sp.dma_start(raw[:, w_, :].rearrange("p (k m) -> p k m", k=DT),
                                     w[0][:, bass.ds(f2 * P + s * P, P)].rearrange("(k p) m -> p k m", p=P)
                                     ).then_inc(raw_in[w_], 16)

            def store_out(hf):
                for t in range(TT):
                    sp.wait_ge(ft_sb, (hf * TT + t + 1) * 2)
                    sp.dma_start(out_v[hf * TT + t], osum[:, t, :]).then_inc(y_out, 16)

            for t in range(TT):
                sp.dma_start(xin0[:, t, :], xin_v[t]).then_inc(x_in, 16)
            sp.dma_start(wk2[:, 0, :], w_ck2[0]).then_inc(wk2_in, 16)
            sp.dma_start(wk2[:, 1, :], w_cv2[0]).then_inc(wk2_in, 16)
            for hf in range(NHF):
                for t, (kind, j) in enumerate(PROJ):
                    n = hf * PER_HALF + t
                    c0 = {"kcmp": COL_KV, "vcmp": COL_KV + P, "ksel": COL_KV + 2 * P, "vsel": COL_KV + 3 * P,
                          "kwin": COL_KV + 4 * P, "vwin": COL_KV + 5 * P, "gate": COL_G, "q": COL_Q + j * P,
                          "cb": j * P, "cc": D_CONV + j * P, "cv": 2 * D_CONV + j * P}[kind]
                    if kind == "gate":
                        ng = 3 * N_HEADS
                        r = raw[:, n % 2, :].rearrange("p (k m) -> p k m", k=DT)
                        src = [(r[:, :, 0:ng], w_in[0][:, COL_G:COL_G + ng].rearrange("(k p) m -> p k m", p=P)),
                               (r[:, :, ng:P], w_in[0][:, 0:P - ng].rearrange("(k p) m -> p k m", p=P))]
                        load_raw(n, src)
                    else:
                        load_w(n, w_in[0], c0)
                    if t == 1:
                        if hf:
                            sp.wait_ge(w_done, hf * PER_HALF)
                            sp.dma_start(XR[:].rearrange("p k n -> p (k n)"), xT_dram[0]).then_inc(xr_in, 16)
                        for kv, w1 in ((0, w_ck1), (1, w_cv1)):
                            for h2 in range(2):
                                sp.dma_start(wc1[h2 * HD:(h2 + 1) * HD, kv, :, :],
                                             w1[0, h2 * CMP_STRIDE:(h2 + 1) * CMP_STRIDE].rearrange("l d h -> d l h")
                                             ).then_inc(wc_in, 16)
                        sp.wait_ge(xt_sb, DT * (hf + 1))
                        sp.dma_start(xT_dram[hf], XT[:].rearrange("p k n -> p (k n)")).then_inc(xt_out, 16)
                    if hf and t == 8:
                        sp.wait_ge(x1_ok, DT)
                        sp.dma_start(x1_dram[0], XR[:].rearrange("p k n -> p (k n)")).then_inc(x1_out, 16)
                for m in range(DT):
                    if hf == 0 and m == 2:
                        sp.wait_ge(conv_y, CT)
                        sp.wait_ge(mod_sum, PARTS)
                        for t in range(TT):
                            sp.dma_start(xin1[:, t, :], xin_v[TT + t]).then_inc(x_in, 16)
                    if hf and m == 4:
                        sp.wait_ge(x1_out, 16)
                        sp.wait_ge(pt_ps, tiles_before(1, NU))
                        sp.dma_start(X1[:].rearrange("p k n -> p (k n)"), x1_dram[0]).then_inc(x1_in, 16)
                    load_w(hf * PER_HALF + NPROJ + m, w_out[0], m * P)
            for hf in range(NHF):
                base = FFN0 + hf * PER_FFN
                gate_up_pair(base, 0)
                if hf == 0:
                    sp.wait_ge(tn_done, (NHF + 1) * DT)
                    sp.wait_ge(xt_out, 16 * NHF)
                    sp.dma_start(X1[:].rearrange("p k n -> p (k n)"), xT_dram[1]).then_inc(xr_in, 16)
                else:
                    sp.wait_ge(tn_done, 2 * NHF * DT)
                    sp.wait_ge(x1_out, 32)
                    sp.dma_start(X1[:].rearrange("p k n -> p (k n)"), x1_dram[0]).then_inc(x1_in, 16)
                for fp in range(1, PEEL + 1):
                    gate_up_pair(base, 2 * fp)
                if hf == 0:
                    sp.wait_ge(x1_ok, NHF * DT)
                    sp.dma_start(x1_dram[1], X1[:].rearrange("p k n -> p (k n)")).then_inc(x1_out, 16)
                else:
                    store_out(0)
                with sp.Fori(PEEL + 1, FT // 2) as fp:
                    gate_up_pair(base, fp * 2)
                if hf == 1:
                    sp.wait_ge(ft_ps, 2 * TT)
                    sp.dma_start(X1[:].rearrange("p k n -> p (k n)"), x1_dram[1]).then_inc(x1_in, 16)
                with sp.Fori(0, DT // 2) as i:
                    for s in range(2 * len(DOWN_K)):
                        k0, k1 = DOWN_K[s % len(DOWN_K)]
                        sp.wait_ge(w_lo, i * (2 * len(DOWN_K)) + (base + 2 * FT + s - 1))
                        sp.dma_start(raw[:, s % 2, 0:(k1 - k0) * P].rearrange("p (k m) -> p k m", m=P),
                                     w_down[0][k0 * P:k1 * P, bass.ds(i * (2 * P) + s // len(DOWN_K) * P, P)]
                                     .rearrange("(k p) m -> p k m", p=P)).then_inc(raw_in[s % 2], 16)
            store_out(1)
            sp.wait_ge(y_out, 16 * TT * NHF)

        @block.gpsimd
        def _(pool):
            ch = Chain(pool, pchain)

            def load_mod(m):
                if m >= NM:
                    pool.wait_ge(mod_acc, m - NM + 1)
                part, k = m // DT, m % DT
                nc.gpsimd.dma_start(wm[:, m % NM, :], w_mod[0, k * P:(k + 1) * P, part * D:(part + 1) * D]
                                    ).then_inc(mod_in[m % NM], 16)

            for m in range(NM):
                load_mod(m)
            nc.gpsimd.memset(ones[:], 1.0).then_inc(consts, 1)
            ch.inc(nc.gpsimd.memset(ident[:], 0.0))
            ch.inc(nc.gpsimd.memset(nz[:], 1.0))
            ch.inc(nc.gpsimd.memset(half_neg[:], -0.5))
            ch.inc(nc.gpsimd.iota(dist_sel[:], pattern=[[-1, SEQ]], base=SEQ - P, channel_multiplier=1,
                                  allow_small_or_imprecise_dtypes=True))
            ch.inc(nc.gpsimd.iota(dist_win[:], pattern=[[-1, WIN_T * P]], base=(WIN_T - 1) * P, channel_multiplier=1,
                                  allow_small_or_imprecise_dtypes=True))
            ch.inc(nc.gpsimd.iota(dist_cmp[:], pattern=[[-CMP_STRIDE, 120]], base=56 * CMP_STRIDE - (CMP_STRIDE - 1),
                                  channel_multiplier=1, allow_small_or_imprecise_dtypes=True))
            ch.wait()
            ch.inc(nc.gpsimd.affine_select(out=ident[:], in_=ident[:], compare_op=ALU.not_equal, fill=1.0, base=0,
                                           pattern=[[-1, P]], channel_multiplier=1))
            ch.inc(nc.gpsimd.affine_select(out=nz[:], in_=nz[:], compare_op=ALU.is_ge, fill=0.0, base=-(CMP_LEN - 1),
                                           pattern=[[0, 1]], channel_multiplier=1))
            ch.inc(nc.gpsimd.affine_select(out=dist_sel[:], in_=dist_sel[:], compare_op=ALU.is_ge, fill=BIG,
                                           base=SEQ - P, pattern=[[-1, SEQ]], channel_multiplier=1))
            ch.inc(nc.gpsimd.affine_select(out=dist_win[:], in_=dist_win[:], compare_op=ALU.is_ge, fill=BIG,
                                           base=(WIN_T - 1) * P, pattern=[[-1, WIN_T * P]], channel_multiplier=1))
            ch.inc(nc.gpsimd.affine_select(out=dist_cmp[:], in_=dist_cmp[:], compare_op=ALU.is_ge, fill=BIG,
                                           base=56 * CMP_STRIDE - (CMP_STRIDE - 1), pattern=[[-CMP_STRIDE, 120]],
                                           channel_multiplier=1))
            ch.wait()
            ch.inc(nc.gpsimd.affine_select(out=dist_win[:], in_=dist_win[:], compare_op=ALU.is_ge, fill=BIG,
                                           base=511 - (WIN_T - 1) * P, pattern=[[1, WIN_T * P]],
                                           channel_multiplier=-1))
            ch.wait()
            nc.gpsimd.memset(acar[:], 0.0).then_inc(consts, 1)
            for m in range(NM, PARTS * DT):
                load_mod(m)

            for hf in range(NHF):
                for what, u, i in ORDER[hf]:
                    qt, g = UNITS[hf][u]
                    U = hf * NU + u
                    if what == "W":
                        pool.wait_ge(wgt_ok, HPG * U + i + 1)
                        wc = CPH * (hf + 1)
                        ns = P * (qt + 1)
                        nw = P * min(qt + 1, WIN_T)
                        for b, lo_, n_ in ((0, 0, wc), (1, N_CMP, ns), (2, N_CMP + ns, nw)):
                            v = prob[hf][:, U % 2, i, lo_:lo_ + n_]
                            r = nc.gpsimd.tensor_scalar(v, v, wgt[:, U % 2, 3 * i + b:3 * i + b + 1], 1.0,
                                                        ALU.mult, ALU.mult)
                        r.then_inc(p_ok, 1)
                    elif what == "O1":
                        pool.wait_ge(oq_sb, U + 1)
                        if U:
                            pool.wait_ge(y_ps, U)
                        nc.gpsimd.tensor_tensor(ob[:], oq[:, :, 0:HD], oq[:, :, HD:P], ALU.add).then_inc(o_sum, 1)
                        pool.wait_ge(o_sum, U + 1)
                        nc.gpsimd.tensor_tensor(oq[:, :, 0:HD], ob[:], ob[:], ALU.mult).then_inc(o_sq, 1)
                        pool.wait_ge(o_ms, U + 1)
                        nc.gpsimd.tensor_tensor(hr[:], hv[:], half_neg[:], ALU.pow).then_inc(o_rstd, 1)
                        pool.wait_ge(o_rstd, U + 1)
                        nc.gpsimd.tensor_tensor(ob[:], ob[:], hr[:].unsqueeze(2).to_broadcast([P, HPG, HD]),
                                                ALU.mult).then_inc(o_norm, 1)

        @block.scalar
        def _(act):
            ch = Chain(act, achain)

            def split_hi(n):
                extra = sum(1 for h in range(NHF) for t, (k, _j) in enumerate(PROJ)
                            if k == "gate" and h * PER_HALF + t <= n and (h * PER_HALF + t) % 2 == n % 2)
                act.wait_ge(raw_in[n % 2], 16 * (n // 2 + 1 + extra))
                if n >= 2:
                    act.wait_ge(w_done, n - 1)
                v = slice(0, tile_width(n))
                nc.scalar.activation(whi[:, n % 2, v], raw[:, n % 2, v], ACT.Copy).then_inc(w_hi, 1)

            def square(norm, hf, k, src):
                i, at, n = NORM[norm, hf]
                if at + k >= 2:
                    act.wait_ge(ssum_done, at + k + i)
                nc.scalar.activation(sq[:, (at + k) % 2, :], src, ACT.Square).then_inc(sq_done, 1)

            def squares(norm, hf, src, ready):
                for k in range(NORM[norm, hf][2]):
                    ready(k)
                    square(norm, hf, k, src(k))

            def root(norm, hf):
                i, at, n = NORM[norm, hf]
                act.wait_ge(ms_sb, i + 1)
                nc.scalar.activation(ssum[:], ssum[:], ACT.Sqrt).then_inc(rms_sb, 1)

            def modulate(norm, hf, k0, k1):
                m0 = (hf if norm == "n1" else NHF + hf) * DT
                tn_, hn_, hi_, a, b0 = {"n1": (tn, hn, hhi, a1, 0), "n2": (tn2, hn2, h2hi, a2, 3 * DT)}[norm]
                for k in range(k0, k1):
                    act.wait_ge(tn_done, m0 + k + 1)
                    if m0 + k >= 2:
                        act.wait_ge(h_lo, m0 + k - 1)
                    nc.scalar.activation(hn_[:, k % 2, :], tn_[:, k % 2, :], ACT.Identity,
                                         scale=a[:, k:k + 1], bias=modT[:, b0 + k:b0 + k + 1]).then_inc(hn_done, 1)
                    act.wait_ge(hn_done, m0 + k + 1)
                    nc.scalar.activation(hi_[:, k, :], hn_[:, k % 2, :], ACT.Copy).then_inc(h_hi, 1)

            def xt_copy(hf, k, bank):
                act.wait_ge(xt_ps, hf * DT + k + 1)
                nc.scalar.activation(XT[:, k, :], ps[:, bank, :], ACT.Copy).then_inc(xt_sb, 1)
                act.wait_ge(xt_sb, hf * DT + k + 1)
                square("n1", hf, k, XT[:, k, :])

            def result_out(hf):
                for n in range(2 * TT):
                    t, s = n // 2, n % 2
                    act.wait_ge(ft_ps, hf * 2 * TT + n + 1)
                    nc.scalar.activation(osum[:, t, s * HALF:(s + 1) * HALF], ps[:, B_OUT[n % len(B_OUT)], :],
                                         ACT.Copy).then_inc(ft_sb, 1)

            def aux_cmp(hf):
                for kv in range(2):
                    s = hf * 2 + kv
                    act.wait_ge(cmp_ps, s + 1)
                    nc.scalar.activation(ck[:, kv, :], ps[:, 2 + kv, 0:N_KV * CPH], ACT.Gelu_apprx_tanh
                                         ).then_inc(gelu_a, 1)
                for s in range(2):
                    act.wait_ge(vt_ps, hf * 3 + s + 1)
                    nc.scalar.activation(VS[:, s, hf * TT:(hf + 1) * TT, :, 0:HD],
                                         ps[:, 4 + s, :].rearrange("p (t g d) -> p t g d", t=TT, g=N_KV),
                                         ACT.Copy).then_inc(vt_hi, 1)
                act.wait_ge(vt_ps, hf * 3 + 3)
                nc.scalar.activation(gate[:], ps[:, 6, 0:TT * 3 * N_HEADS].rearrange("p (t n) -> p t n", t=TT), ACT.Exp,
                                     scale=-1.0).then_inc(gate_exp, 1)

            def aux_kc(hf):
                act.wait_ge(kc_ps, hf + 1)
                nc.scalar.activation(KS[0:HD, :, CPH * hf:CPH * (hf + 1)],
                                     ps[0:HD, 7, 0:N_KV * CPH].rearrange("p (g c) -> p g c", g=N_KV), ACT.Copy)
                nc.scalar.activation(VC[CPH * hf:CPH * (hf + 1), :, 0:HD],
                                     ps[0:CPH, 7, 128:256].rearrange("p (g d) -> p g d", g=N_KV),
                                     ACT.Copy).then_inc(kc_hi, 1)

            act.wait_ge(vec_ps, 1)
            nc.scalar.activation(vcol[:], ps[:, 0, 0:NVEC], ACT.Copy)
            nc.scalar.activation(posT[:], ps[:, 0, P:P + CMP_LEN], ACT.Copy).then_inc(vec_ok, 1)
            act.wait_ge(vec_ok, 1)
            nc.scalar.activation(siluc[:], cT, ACT.Silu).then_inc(silu_c, 1)

            for k in range(DT):
                xt_copy(0, k, k)
            root("n1", 0)
            act.wait_ge(mod_ready, 2)
            modulate("n1", 0, 0, DT)
            split_hi(0)
            split_hi(1)
            for hf in range(NHF):
                base = hf * PER_HALF
                for t, (kind, j) in enumerate(PROJ):
                    split_hi(base + t + 2)
                    if hf and t == 1:
                        root("mix", 0)
                    bank = ps[:, B_PJ + t % 2, :]
                    act.wait_ge(w_done, base + t + 1)
                    if kind in ("ksel", "kwin"):
                        o = N_CMP + (SEQ if kind == "kwin" else 0) + hf * HALF
                        for g in range(N_KV):
                            r = nc.scalar.activation(KS[0:HD, g, o:o + HALF], bank[g * HD:(g + 1) * HD, :], ACT.Copy)
                    elif kind == "q":
                        if j == 0:
                            act.wait_ge(h_lo, (hf + 1) * DT)
                            act.wait_ge(xt_out, 16 * (hf + 1))
                        for s in range(2):
                            h = 2 * j + s
                            for r_ in range(2):
                                r = nc.scalar.activation(qhi[r_ * HD:(r_ + 1) * HD, h, :], bank[s * HD:(s + 1) * HD, :],
                                                         ACT.Copy, scale=-(2.0 ** (h + 1)) / 8.0)
                    else:
                        r = None
                    if r is not None:
                        r.then_inc(ev_a, 1)
                    if t == AFTER_CMP + 1:
                        aux_cmp(hf)
                    elif t == AFTER_KC + 1:
                        aux_kc(hf)
                    elif kind == "cb" and j:
                        act.wait_ge(conv_y, hf * CT + j)
                        square("conv", hf, j - 1, yc[:, j - 1, :])
                for what, u, i in ORDER_ACT[hf]:
                    qt, g = UNITS[hf][u]
                    U = hf * NU + u
                    wc = CPH * (hf + 1)
                    ns = P * (qt + 1)
                    nw = P * min(qt + 1, WIN_T)
                    if what == "N1":
                        act.wait_ge(conv_y, (hf + 1) * CT)
                        square("conv", hf, CT - 1, yc[:, CT - 1, :])
                        root("conv", hf)
                    elif what == "N2":
                        for k in range(CT):
                            act.wait_ge(conv_n, hf * CT + k + 1)
                            nc.scalar.activation(ychi[:, k, :], yc[:, k, :], ACT.Copy, scale=gcT[:, k:k + 1]
                                                 ).then_inc(conv_hi, 1)
                    elif what == "S":
                        h, bk = i
                        nb = len(score_banks(qt, hf))
                        br = {0: 0, 1: 2, nb - 1: 1}.get(bk)
                        if br is not None:
                            lo_, n_ = ((1, wc - 1), (N_CMP, ns), (N_CMP + ns, nw))[br]
                            act.wait_ge(s_used, banks_before(hf, u, h) + bk + 1)
                            v = prob[hf][:, U % 2, h, lo_:lo_ + n_]
                            s = 3 * h + br
                            nc.scalar.activation(v, v, ACT.Exp, bias=smin[:, U % 2, s:s + 1], scale=-1.0,
                                                 accum_out=ssumexp[:, U % 2, s:s + 1]).then_inc(e_done, 1)
                    elif what == "T":
                        M = tiles_before(hf, u) + i
                        n_ = CPH * (hf + 1) if i == 0 else P
                        act.wait_ge(pt_ps, M + 1)
                        if M >= 2:
                            act.wait_ge(pv_done, M - 1)
                        nc.scalar.activation(pth[0:n_, M % 2, :], ps[0:n_, B_PT + M % NPT, :], ACT.Copy).then_inc(pt_hi, 1)
                    elif what == "C":
                        act.wait_ge(pv_done, tiles_before(hf, u + 1))
                        if U:
                            act.wait_ge(ot_ps, U)
                        nc.scalar.activation(osb[:], ps[:, B_O + U % NO, :], ACT.Copy).then_inc(o_sb, 1)
                    elif what == "O1":
                        act.wait_ge(ot_ps, U + 1)
                        nc.scalar.activation(oq[:], ps[:, B_OT, :].rearrange("p (h d) -> p h d", h=HPG),
                                             ACT.Copy).then_inc(oq_sb, 1)
                    elif what == "O2":
                        act.wait_ge(y_ps, U + 1)
                        k0 = 2 * g
                        q0 = (qt % TT) * P
                        for k in range(2):
                            r = nc.scalar.activation(yahi[:, k0 + k, q0:q0 + P], ps[:, B_OT, k * P:(k + 1) * P],
                                                     ACT.Copy, scale=gaT[:, k0 + k:k0 + k + 1])
                        r.then_inc(y_hi, 1)
                nxt = ("n1", 1) if hf == 0 else ("n2", 0)
                for m in range(DT):
                    split_hi(base + NPROJ + m + 2)
                    act.wait_ge(w_done, base + NPROJ + m + 1)
                    nc.scalar.activation(res[hf][:, m, :], ps[:, B_Y + m % NY, :], ACT.Copy).then_inc(res_sb, 1)
                    if m < 2:
                        for k in range(4 * m, 4 * m + 4):
                            if hf == 0:
                                xt_copy(1, k, B_X1 + k % NX1)
                            else:
                                act.wait_ge(x1_in, 16)
                                square("n2", 0, k, X1[:, k, :])
                    elif m == 3:
                        root(*nxt)
                    if m >= 3:
                        act.wait_ge(res_sb, hf * DT + m + 1)
                        for k in MIX_SQUARES[m]:
                            square("mix", hf, k, res[hf][:, k, :])
                    if m >= 4:
                        modulate(*nxt, 2 * (m - 4), 2 * (m - 3))
            for hf in range(NHF):
                base = FFN0 + hf * PER_FFN
                extra = [sum(1 for h in range(NHF) for t, (k, _j) in enumerate(PROJ)
                             if k == "gate" and (h * PER_HALF + t) % 2 == s) for s in range(2)]

                def split_hi_f(n0, f2):
                    act.wait_ge(raw_in[n0 % 2], f2 * 8 + 16 * (n0 // 2 + 1 + extra[n0 % 2]))
                    act.wait_ge(w_done, f2 + (n0 - 1))
                    v = slice(0, tile_width(n0))
                    nc.scalar.activation(whi[:, n0 % 2, v], raw[:, n0 % 2, v], ACT.Copy).then_inc(w_hi, 1)

                def gate_up(fp):
                    for s in range(2):
                        split_hi_f(base + 2 + 2 * s, fp * 4)
                        act.wait_ge(w_done, fp * 4 + (base + 2 * s + 1))
                        act.wait_ge(a_ok, fp * 2 + (hf * FT + s + 2))
                        nc.scalar.activation(sg[:], ps[:, B_GU + 2 * s, :], ACT.Silu).then_inc(silu_ok, 1)
                        split_hi_f(base + 3 + 2 * s, fp * 4)
                        act.wait_ge(a_ok, fp * 2 + (hf * FT + s + 3))
                        nc.scalar.activation(ahi[:, bass.ds(fp * 2 + s, 1), :].rearrange("p a n -> p (a n)"), aa[:],
                                             ACT.Copy).then_inc(a_hi, 1)

                gate_up(0)
                root(*(("mix", 1) if hf == 0 else ("ffn", 0)))
                for fp in range(1, PEEL):
                    gate_up(fp)
                if hf:
                    result_out(0)
                with act.Fori(PEEL, FT // 2) as fp:
                    gate_up(fp)

                def down_tile(m, squares):
                    for c in range(len(DOWN_K)):
                        split_hi(base + 2 * FT + len(DOWN_K) * m + c + 2)
                    act.wait_ge(w_done, base + 2 * FT + len(DOWN_K) * (m + 1))
                    if m == 0 and hf:
                        act.wait_ge(y_out, 16 * TT * hf)
                    nc.scalar.activation(fres[:, m, :], ps[:, B_Y + m % NY, :], ACT.Copy).then_inc(res_sb, 1)
                    for k in squares:
                        act.wait_ge(res_sb, (NHF + hf) * DT + k + 1)
                        square("ffn", hf, k, fres[:, k, :])

                if hf == 0:
                    for k in range(DT):
                        act.wait_ge(x1_ok, NHF * DT)
                        square("n2", 1, k, X1[:, k, :])
                    down_tile(0, ())
                    root("n2", 1)
                    modulate("n2", 1, 0, 4)
                    down_tile(1, ())
                    modulate("n2", 1, 4, DT)
                    for k in range(2):
                        square("ffn", 0, k, fres[:, k, :])
                else:
                    down_tile(0, (0,))
                    down_tile(1, (1,))
                i_, at, _n = NORM["ffn", hf]

                def down_pair(i, last):
                    for s in range(2):
                        for c in range(len(DOWN_K)):
                            t = len(DOWN_K) * s + c
                            if not (last and t + 2 >= 2 * len(DOWN_K)):
                                split_hi_f(base + 2 * FT + t + 2, i * (2 * len(DOWN_K)))
                        act.wait_ge(w_done, i * (2 * len(DOWN_K)) + (base + 2 * FT + (s + 1) * len(DOWN_K)))
                        m = bass.ds(i * 2 + s, 1)
                        nc.scalar.activation(fres[:, m, :].rearrange("p a n -> p (a n)"), ps[:, B_Y + s, :],
                                             ACT.Copy).then_inc(res_sb, 1)
                        act.wait_ge(ssum_done, i * 2 + (at + s + i_))
                        nc.scalar.activation(sq[:, (at + s) % 2, :], ps[:, B_Y + s, :], ACT.Square).then_inc(sq_done, 1)

                if hf == 0:
                    with act.Fori(1, DT // 2) as i:
                        down_pair(i, False)
                else:
                    with act.Fori(1, DT // 2 - 1) as i:
                        down_pair(i, False)
                    down_pair(DT // 2 - 1, True)
            root("ffn", 1)
            result_out(1)

        @block.vector
        def _(dve):
            ch = Chain(dve, dchain)

            def split_lo(n):
                dve.wait_ge(w_hi, n + 1)
                v = slice(0, tile_width(n))
                nc.vector.tensor_tensor(wlo[:, n % 2, v], raw[:, n % 2, v], whi[:, n % 2, v].bitcast(F32),
                                        ALU.subtract).then_inc(w_lo, 1)

            def sum_squares(norm, hf, width):
                sum_squares_only(norm, hf)
                rms(norm, hf, width)

            def sum_squares_only(norm, hf):
                clear_sum(norm, hf)
                for k in range(NORM[norm, hf][2]):
                    add_square(norm, hf, k)

            def clear_sum(norm, hf):
                i, at, n = NORM[norm, hf]
                if i:
                    dve.wait_ge(rstd_ok, i)
                nc.vector.memset(ssum[:], 0.0).then_inc(ssum_done, 1)

            def add_square(norm, hf, k):
                i, at, n = NORM[norm, hf]
                dve.wait_ge(sq_done, at + k + 1)
                dve.wait_ge(ssum_done, at + k + i + 1)
                nc.vector.tensor_tensor(ssum[:], ssum[:], sq[:, (at + k) % 2, :], ALU.add).then_inc(ssum_done, 1)

            def rms(norm, hf, width):
                i, at, n = NORM[norm, hf]
                dve.wait_ge(ms_ps, i + 1)
                nc.vector.tensor_scalar(ssum[:], ps[:, B_OT, :], 1.0 / width, EPS, ALU.mult, ALU.add
                                        ).then_inc(ms_sb, 1)
                dve.wait_ge(rms_sb, i + 1)
                nc.vector.reciprocal(rstd[:], ssum[:]).then_inc(rstd_ok, 1)
                dve.wait_ge(rstd_ok, i + 1)

            def normed(norm, hf, k0, k1):
                m0 = (hf if norm == "n1" else NHF + hf) * DT
                src, tn_, hn_, hi_, lo_ = {"n1": (XT, tn, hn, hhi, hlo), "n2": (X1, tn2, hn2, h2hi, h2lo)}[norm]
                for k in range(k0, k1 + (k1 == DT)):
                    if k < DT:
                        if m0 + k >= 2:
                            dve.wait_ge(hn_done, m0 + k - 1)
                        nc.vector.tensor_tensor(tn_[:, k % 2, :], src[:, k, :], rstd[:], ALU.mult).then_inc(tn_done, 1)
                    if k:
                        dve.wait_ge(h_hi, m0 + k)
                        nc.vector.tensor_tensor(lo_[:, k - 1, :], hn_[:, (k - 1) % 2, :], hi_[:, k - 1, :].bitcast(F32),
                                                ALU.subtract).then_inc(h_lo, 1)

            def mod_step(m):
                part, k = m // DT, m % DT
                dve.wait_ge(mod_in[m % NM], 16 * (m // NM + 1))
                acc = macc[:, part % 2, :]
                if k == 0:
                    dve.wait_ge(silu_c, 1)
                    if part > 1:
                        dve.wait_ge(mod_sum, part - 1)
                    nc.vector.tensor_scalar(acc, wm[:, m % NM, :], siluc[:, k:k + 1], None, ALU.mult
                                            ).then_inc(mod_acc, 1)
                else:
                    dve.wait_ge(mod_acc, m)
                    nc.vector.scalar_tensor_tensor(acc, wm[:, m % NM, :], siluc[:, k:k + 1], acc,
                                                   ALU.mult, ALU.add).then_inc(mod_acc, 1)

            def mod_vector(part):
                dve.wait_ge(mod_sum, part + 1)
                if part == 0:
                    dve.wait_ge(vec_ok, 1)
                v = modT[:, part * DT:(part + 1) * DT]
                r = nc.vector.tensor_tensor(v, mod_bank(part), bmodT[:, part * DT:(part + 1) * DT], ALU.add)
                if part in (1, 2, 4, 5):
                    ch.inc(r)
                    ch.wait()
                if part in (1, 4):
                    r = nc.vector.scalar_tensor_tensor({1: a1, 4: a2}[part][:], v, 1.0, {1: g1T, 4: g2T}[part],
                                                       ALU.add, ALU.mult)
                elif part in (2, 5):
                    r = nc.vector.tensor_tensor({2: cm, 5: cf}[part][:], v, {2: gpmT, 5: gpfT}[part], ALU.mult)
                r.then_inc(mod_ready, 1)

            def residual(step, src, coef, xt):
                for k in range(step % 2 * 4, step % 2 * 4 + 4):
                    if step < 2:
                        ch.inc(nc.vector.tensor_tensor(src[:, k, :], src[:, k, :], rstd[:], ALU.mult))
                    else:
                        ch.wait()
                        nc.vector.scalar_tensor_tensor(xt[:, k, :], src[:, k, :], coef[:, k:k + 1], xt[:, k, :],
                                                       ALU.mult, ALU.add).then_inc(x1_ok, 1)

            def aux_cmp(hf):
                for s in range(2):
                    dve.wait_ge(vt_hi, hf * 2 + s + 1)
                    nc.vector.tensor_tensor(VS[:, s, hf * TT:(hf + 1) * TT, :, HD:P],
                                            ps[:, 4 + s, :].rearrange("p (t g d) -> p t g d", t=TT, g=N_KV),
                                            VS[:, s, hf * TT:(hf + 1) * TT, :, 0:HD].bitcast(F32),
                                            ALU.subtract).then_inc(vt_ok, 1)
                dve.wait_ge(gate_exp, hf + 1)
                ch.inc(nc.vector.tensor_scalar(gate[:], gate[:], 1.0, None, ALU.add))
                ch.wait()
                ch.inc(nc.vector.reciprocal(gate[:], gate[:]))
                ch.wait()
                if hf == 0:
                    gv = gate[:, 0, :].rearrange("p (h b) -> p h b", b=3)[:, :, 0]
                    ch.inc(nc.vector.tensor_scalar(gv, gv, nz[:], None, ALU.mult))
                    ch.wait()

            def aux_kc(hf):
                dve.wait_ge(kc_hi, hf + 1)
                ch.inc(nc.vector.tensor_tensor(KS[HD:P, :, CPH * hf:CPH * (hf + 1)],
                                               ps[0:HD, 7, 0:N_KV * CPH].rearrange("p (g c) -> p g c", g=N_KV),
                                               KS[0:HD, :, CPH * hf:CPH * (hf + 1)].bitcast(F32), ALU.subtract))
                nc.vector.tensor_tensor(VC[CPH * hf:CPH * (hf + 1), :, HD:P],
                                        ps[0:CPH, 7, 128:256].rearrange("p (g d) -> p g d", g=N_KV),
                                        VC[CPH * hf:CPH * (hf + 1), :, 0:HD].bitcast(F32),
                                        ALU.subtract).then_inc(kc_ok, 1)

            for m in range(2 * DT):
                mod_step(m)
            sum_squares("n1", 0, D)
            mod_vector(0)
            mod_vector(1)
            dve.wait_ge(mod_ready, 2)
            normed("n1", 0, 0, DT)
            dve.wait_ge(h_lo, DT)
            ch.inc(nc.vector.memset(cin[0:HD, :, :, :, 0:1], 0.0))
            nc.vector.memset(z[:, 0:2], 0.0).then_inc(pj_free, 2)
            ch.wait()
            split_lo(0)
            split_lo(1)
            for hf in range(NHF):
                base = hf * PER_HALF
                ev = hf * 6
                for t, (kind, j) in enumerate(PROJ):
                    T = hf * NPROJ + t
                    split_lo(base + t + 2)
                    bank = ps[:, B_PJ + t % 2, :]
                    dve.wait_ge(w_done, base + t + 1)
                    if kind in ("kcmp", "vcmp"):
                        kv = ("kcmp", "vcmp").index(kind)
                        v = bank.rearrange("p (c l) -> p l c", l=CMP_STRIDE)
                        if hf:
                            nc.vector.tensor_copy(cin[0:HD, kv, :, :, 0], acar[:, kv, :, :])
                        for g in range(N_KV):
                            gs = slice(g * HD, (g + 1) * HD)
                            pa = posT[gs, 0:CMP_STRIDE].unsqueeze(2).to_broadcast([HD, CMP_STRIDE, CPH - 1])
                            pb = posT[gs, CMP_STRIDE:CMP_LEN].unsqueeze(2).to_broadcast([HD, CMP_STRIDE, CPH])
                            nc.vector.tensor_tensor(cin[0:HD, kv, :, g, 1:CPH], v[gs, :, 0:CPH - 1], pa, ALU.add)
                            r = nc.vector.tensor_tensor(cin[HD:P, kv, :, g, :], v[gs, :, :], pb, ALU.add)
                            if hf == 0:
                                r = nc.vector.tensor_tensor(acar[:, kv, :, g], v[gs, :, CPH - 1],
                                                            posT[gs, 0:CMP_STRIDE], ALU.add)
                        r.then_inc(pj_free, 1)
                    elif kind in ("ksel", "kwin"):
                        ev += 1
                        dve.wait_ge(ev_a, ev)
                        o = N_CMP + (SEQ if kind == "kwin" else 0) + hf * HALF
                        for g in range(N_KV):
                            r = nc.vector.tensor_tensor(KS[HD:P, g, o:o + HALF], bank[g * HD:(g + 1) * HD, :],
                                                        KS[0:HD, g, o:o + HALF].bitcast(F32), ALU.subtract)
                        r.then_inc(pj_free, 1)
                    elif kind == "q":
                        ev += 1
                        dve.wait_ge(ev_a, ev)
                        for s in range(2):
                            h = 2 * j + s
                            for r_ in range(2):
                                r = nc.vector.scalar_tensor_tensor(
                                    qlo[r_ * HD:(r_ + 1) * HD, h, :], bank[s * HD:(s + 1) * HD, :],
                                    -(2.0 ** (h + 1)) / 8.0, qhi[r_ * HD:(r_ + 1) * HD, h, :].bitcast(F32),
                                    ALU.mult, ALU.subtract)
                        r.then_inc(pj_free, 1)
                    elif kind == "cv":
                        dve.wait_ge(pj_free, T + 2)
                        ch.wait()
                        if hf:
                            ch.inc(nc.vector.tensor_copy(z[:, 0:2], zcar[:, j, :]))
                        nc.vector.tensor_tensor(z[:, 2:HALF + 2], bank, cc_sb[:], ALU.mult).then_inc(pj_free, 1)
                        dve.wait_ge(pj_free, T + 3)
                        if hf:
                            ch.wait()
                        if hf == 0:
                            ch.inc(nc.vector.tensor_copy(zcar[:, j, :], z[:, HALF:HALF + 2]))
                        ch.inc(nc.vector.tensor_scalar(zc[:], z[:, 2:HALF + 2], cw2[:, j:j + 1], None, ALU.mult))
                        ch.wait()
                        ch.inc(nc.vector.scalar_tensor_tensor(zc[:], z[:, 1:HALF + 1], cw1[:, j:j + 1], zc[:],
                                                              ALU.mult, ALU.add))
                        ch.wait()
                        ch.inc(nc.vector.scalar_tensor_tensor(zc[:], z[:, 0:HALF], cw0[:, j:j + 1], zc[:],
                                                              ALU.mult, ALU.add))
                        ch.wait()
                        nc.vector.tensor_tensor(yc[:, j, :], zc[:], cb_sb[:], ALU.mult).then_inc(conv_y, 1)
                    else:
                        dst = {"vsel": vtmp[:, 0, :], "vwin": vtmp[:, 1, :], "gate": vtmp[:, 2, :],
                               "cb": cb_sb[:], "cc": cc_sb[:]}[kind]
                        if kind == "cb" and T > j:
                            dve.wait_ge(conv_y, hf * CT + j)
                        nc.vector.tensor_copy(dst, bank).then_inc(pj_free, 1)
                    if hf and t == 1:
                        rms("mix", 0, D)
                    elif hf and 2 <= t < 6:
                        dve.wait_ge(xr_in, 16)
                        residual(t - 2, res0, cm, XR)
                    elif t == AFTER_CMP + 1:
                        aux_cmp(hf)
                    elif t == AFTER_KC + 1:
                        aux_kc(hf)
                    elif kind == "cc" and j:
                        add_square("conv", hf, j - 1)
                    elif kind == "cb" and j == 0:
                        clear_sum("conv", hf)
                    if hf == 0:
                        for part, (t0, t1, after) in MOD_TILES.items():
                            if t0 <= t <= t1:
                                for m in range((t - t0) * DT // (t1 - t0 + 1), (t - t0 + 1) * DT // (t1 - t0 + 1)):
                                    mod_step(part * DT + m)
                            if t == min(after + 1, NPROJ - 1):
                                mod_vector(part)
                dve.wait_ge(conv_y, (hf + 1) * CT)
                ch.inc(nc.vector.memset(prob[hf][:, :, :, 0:1], 0.0))
                ch.wait()
                for what, u, i in ORDER_DVE[hf]:
                    qt, g = UNITS[hf][u]
                    U = hf * NU + u
                    ns = P * (qt + 1)
                    if what == "N1":
                        add_square("conv", hf, CT - 1)
                        rms("conv", hf, D_CONV)
                        for k in range(CT):
                            nc.vector.tensor_tensor(yc[:, k, :], yc[:, k, :], rstd[:], ALU.mult).then_inc(conv_n, 1)
                    elif what == "N2":
                        for k in range(CT):
                            dve.wait_ge(conv_hi, hf * CT + k + 1)
                            nc.vector.scalar_tensor_tensor(yclo[:, k, :], yc[:, k, :], gcT[:, k:k + 1],
                                                           ychi[:, k, :].bitcast(F32), ALU.mult, ALU.subtract
                                                           ).then_inc(conv_ok, 1)
                    elif what == "S":
                        h, bk = i
                        slope = 2.0 ** -(g * HPG + h + 1)
                        first = max(0, qt - (WIN_T - 1))
                        nb = banks_before(hf, u, h) + bk
                        if i == (0, 0) and u >= 2:
                            dve.wait_ge(pt_ps, tiles_before(hf, u - 1))
                        dve.wait_ge(s_ps, nb + 1)
                        for branch, k0, n_, at in score_banks(qt, hf)[bk]:
                            br = ("cmp", "sel", "win").index(branch)
                            s = smin[:, U % 2, 3 * h + br:3 * h + br + 1]
                            skip = 0
                            if branch == "cmp":
                                skip = 1
                                tab = dist_cmp[:, 56 - 8 * qt + 1:56 - 8 * qt + n_]
                                d0 = 0
                            elif branch == "sel":
                                tab = dist_sel[:, k0 - P * qt + SEQ - P:k0 - P * qt + SEQ - P + n_]
                                d0 = N_CMP + k0
                            else:
                                tab = dist_win[:, k0 - P * qt + (WIN_T - 1) * P:k0 - P * qt + (WIN_T - 1) * P + n_]
                                d0 = N_CMP + ns + k0 - P * first
                            init = 3.0e38
                            if branch == "sel" and k0 or branch == "win" and bk == 1 and n_ == 512 and qt >= WIN_T - 1:
                                init = s
                                dve.wait_ge(s_used, nb)
                            r = nc.vector.tensor_tensor_reduce(
                                prob[hf][:, U % 2, h, d0 + skip:d0 + n_], ps[:, B_S + nb % NS_B, at + skip:at + n_], tab,
                                slope, init, ALU.add, ALU.min, s)
                        r.then_inc(s_used, 1)
                    elif what == "W":
                        dve.wait_ge(e_done, 3 * (HPG * U + i + 1))
                        s = slice(3 * i, 3 * i + 3)
                        ch.inc(nc.vector.reciprocal(wgt[:, U % 2, s], ssumexp[:, U % 2, s]))
                        ch.wait()
                        s3 = g * 3 * HPG + 3 * i
                        nc.vector.tensor_tensor(wgt[:, U % 2, s], wgt[:, U % 2, s], gate[:, qt % TT, s3:s3 + 3],
                                                ALU.mult).then_inc(wgt_ok, 1)
                    elif what == "T":
                        M = tiles_before(hf, u) + i
                        n_ = CPH * (hf + 1) if i == 0 else P
                        dve.wait_ge(pt_hi, M + 1)
                        nc.vector.tensor_tensor(ptl[0:n_, M % 2, :], ps[0:n_, B_PT + M % NPT, :],
                                                pth[0:n_, M % 2, :].bitcast(F32), ALU.subtract).then_inc(pt_lo, 1)
                    elif what == "O1":
                        dve.wait_ge(o_sq, U + 1)
                        ch.inc(nc.vector.tensor_reduce(hs[:], oq[:, :, 0:HD], AX_X, ALU.add))
                        ch.wait()
                        nc.vector.tensor_scalar(hv[:], hs[:], 1.0 / HD, EPS, ALU.mult, ALU.add).then_inc(o_ms, 1)
                        dve.wait_ge(o_ms, U + 1)
                    elif what == "O2":
                        dve.wait_ge(y_hi, U + 1)
                        k0 = 2 * g
                        q0 = (qt % TT) * P
                        for k in range(2):
                            r = nc.vector.scalar_tensor_tensor(
                                yalo[:, k0 + k, q0:q0 + P], ps[:, B_OT, k * P:(k + 1) * P], gaT[:, k0 + k:k0 + k + 1],
                                yahi[:, k0 + k, q0:q0 + P].bitcast(F32), ALU.mult, ALU.subtract)
                        r.then_inc(y_ok, 1)
                nxt = ("n1", 1) if hf == 0 else ("n2", 0)
                for m in range(DT):
                    split_lo(base + NPROJ + m + 2)
                    if m == 0:
                        clear_sum(*nxt)
                    if m < 2:
                        for k in range(4 * m, 4 * m + 4):
                            add_square(*nxt, k)
                    elif m == 3:
                        rms(*nxt, D)
                        clear_sum("mix", hf)
                    if m >= 3:
                        for k in MIX_SQUARES[m]:
                            add_square("mix", hf, k)
                    if m >= 4:
                        normed(*nxt, 2 * (m - 4), 2 * (m - 3))
            for hf in range(NHF):
                base = FFN0 + hf * PER_FFN

                def split_lo_f(n0, f2):
                    dve.wait_ge(w_hi, f2 + (n0 + 1))
                    v = slice(0, tile_width(n0))
                    nc.vector.tensor_tensor(wlo[:, n0 % 2, v], raw[:, n0 % 2, v], whi[:, n0 % 2, v].bitcast(F32),
                                            ALU.subtract).then_inc(w_lo, 1)

                if hf == 0:
                    nc.vector.memset(sg[:], 0.0).then_inc(silu_ok, 2)
                    ch.inc(nc.vector.memset(aa[:, 0:1], 0.0))
                    ch.wait()
                    nc.vector.memset(aa[:, 0:1], 0.0).then_inc(a_ok, 2)
                    dve.wait_ge(a_ok, 2)
                    nc.vector.memset(aa[:, 0:1], 0.0).then_inc(a_lo, 1)

                def gate_up(fp):
                    for s in range(2):
                        split_lo_f(base + 2 + 2 * s, fp * 4)
                        split_lo_f(base + 3 + 2 * s, fp * 4)
                        dve.wait_ge(silu_ok, fp * 2 + (hf * FT + s + 3))
                        dve.wait_ge(w_done, fp * 4 + (base + 2 * s + 2))
                        dve.wait_ge(a_lo, fp * 2 + (hf * FT + s + 1))
                        nc.vector.tensor_tensor(aa[:], ps[:, B_GU + 2 * s + 1, :], sg[:], ALU.mult).then_inc(a_ok, 1)
                        dve.wait_ge(a_hi, fp * 2 + (hf * FT + s + 1))
                        f = bass.ds(fp * 2 + s, 1)
                        nc.vector.tensor_tensor(alo[:, f, :].rearrange("p a n -> p (a n)"), aa[:],
                                                ahi[:, f, :].rearrange("p a n -> p (a n)").bitcast(F32),
                                                ALU.subtract).then_inc(a_lo, 1)

                gate_up(0)
                if hf == 0:
                    rms("mix", 1, D)
                    dve.wait_ge(xr_in, 32)
                else:
                    rms("ffn", 0, D)
                    dve.wait_ge(x1_in, 32)
                coef = (cm, cf)[hf]
                residual(0, fres, coef, X1)
                for fp in range(1, PEEL):
                    gate_up(fp)
                    if fp == 1:
                        residual(1, fres, coef, X1)
                        residual(2, fres, coef, X1)
                    else:
                        residual(3, fres, coef, X1)
                with dve.Fori(PEEL, FT // 2) as fp:
                    gate_up(fp)
                i_, at, _n = NORM["ffn", hf]

                def down_splits(m):
                    for c in range(len(DOWN_K)):
                        split_lo(base + 2 * FT + len(DOWN_K) * m + c + 2)

                if hf == 0:
                    sum_squares_only("n2", 1)
                    down_splits(0)
                    rms("n2", 1, D)
                    clear_sum("ffn", 0)
                    normed("n2", 1, 0, 4)
                    down_splits(1)
                    normed("n2", 1, 4, DT)
                    for k in range(2):
                        add_square("ffn", 0, k)
                else:
                    clear_sum("ffn", 1)
                    for m in range(2):
                        down_splits(m)
                        add_square("ffn", 1, m)

                def down_pair(i, last):
                    for s in range(2):
                        for c in range(len(DOWN_K)):
                            t = len(DOWN_K) * s + c
                            if not (last and t + 2 >= 2 * len(DOWN_K)):
                                split_lo_f(base + 2 * FT + t + 2, i * (2 * len(DOWN_K)))
                        dve.wait_ge(sq_done, i * 2 + (at + s + 1))
                        dve.wait_ge(ssum_done, i * 2 + (at + s + i_ + 1))
                        nc.vector.tensor_tensor(ssum[:], ssum[:], sq[:, (at + s) % 2, :], ALU.add
                                                ).then_inc(ssum_done, 1)

                if hf == 0:
                    with dve.Fori(1, DT // 2) as i:
                        down_pair(i, False)
                else:
                    with dve.Fori(1, DT // 2 - 1) as i:
                        down_pair(i, False)
                    down_pair(DT // 2 - 1, True)
            rms("ffn", 1, D)
            dve.wait_ge(x1_in, 48)
            for step in range(4):
                residual(step, fres, cf, X1)

        @block.tensor
        def _(pe):
            def mean_square(norm, hf):
                i, at, n = NORM[norm, hf]
                pe.wait_ge(ssum_done, at + n + i + 1)
                nc.tensor.matmul(ps[:, B_OT, :], ones[:], ssum[:], start=True, stop=True).then_inc(ms_ps, 1)

            def three(dst, whi_, wlo_, mhi, mlo, start, stop):
                nc.tensor.matmul(dst, whi_, mhi, start=start, stop=False)
                nc.tensor.matmul(dst, whi_, mlo, start=False, stop=False)
                return nc.tensor.matmul(dst, wlo_, mhi, start=False, stop=stop)

            def feature_tile(dst, slot, hi_, lo_):
                for k in range(DT):
                    s = slice(k * P, (k + 1) * P)
                    r = three(dst, whi[:, slot, s], wlo[:, slot, s], hi_[:, k, :], lo_[:, k, :], k == 0, k == DT - 1)
                return r



            def mod_sums(part):
                pe.wait_ge(mod_acc, (part + 1) * DT)
                for m in range(DT):
                    r = nc.tensor.matmul(mod_bank(part)[:, m:m + 1], macc[:, part % 2, m * P:(m + 1) * P], ones[:, 0:1],
                                         start=True, stop=True)
                r.then_inc(mod_sum, 1)

            def result_back(hf):
                pe.wait_ge(x1_ok, (NHF + hf + 1) * DT)
                for n in range(2 * TT):
                    t, s = n // 2, n % 2
                    if n >= len(B_OUT):
                        pe.wait_ge(ft_sb, hf * 2 * TT + n - len(B_OUT) + 1)
                    for k in range(4):
                        r = nc.tensor.transpose(ps[:, B_OUT[n % len(B_OUT)], k * P:(k + 1) * P],
                                                X1[:, 4 * s + k, t * P:(t + 1) * P], ident[:])
                    r.then_inc(ft_ps, 1)

            pe.wait_ge(consts, 2)
            pe.wait_ge(small_in, 16 * (len(VEC_N) + N_KV))
            nc.tensor.transpose(ps[:, 0, 0:NVEC], vrow[:], ident[0:NVEC, 0:NVEC])
            nc.tensor.transpose(ps[:, 0, P:P + CMP_LEN], posr[:], ident[0:CMP_LEN, 0:CMP_LEN]).then_inc(vec_ps, 1)
            pe.wait_ge(vec_ok, 1)
            def x_transpose(hf, k, bank):
                for t in range(TT):
                    r = nc.tensor.transpose(ps[:, bank, t * P:(t + 1) * P], xin[hf][:, t, k * P:(k + 1) * P], ident[:])
                r.then_inc(xt_ps, 1)

            pe.wait_ge(x_in, 16 * TT)
            for k in range(DT):
                x_transpose(0, k, k)
            mean_square("n1", 0)
            mod_sums(0)
            mod_sums(1)
            pe.wait_ge(ms_sb, 1)
            for hf in range(NHF):
                base = hf * PER_HALF
                pe.wait_ge(h_lo, (hf + 1) * DT)
                if hf:
                    pe.wait_ge(res_sb, hf * DT)

                def pj(t0, i2):
                    pe.wait_ge(w_lo, i2 + (base + t0 + 1))
                    pe.wait_ge(pj_free, i2 + (hf * NPROJ + t0 + 1))
                    feature_tile(ps[:, B_PJ + t0 % 2, :], (base + t0) % 2, hhi, hlo).then_inc(w_done, 1)

                def pairs(t0, t1):
                    if t1 - t0 >= 4:
                        with pe.Fori(0, (t1 - t0) // 2) as i:
                            pj(t0, i * 2)
                            pj(t0 + 1, i * 2)
                    elif t1 > t0:
                        pj(t0, 0)
                        pj(t0 + 1, 0)

                pj(0, 0)
                if hf:
                    mean_square("mix", 0)
                pj(1, 0)
                pairs(2, AFTER_CMP + 1)
                pe.wait_ge(pj_free, hf * NPROJ + 2 + AFTER_CMP)
                pe.wait_ge(wc_in, 64 * (hf + 1))
                for kv in range(2):
                    for l_ in range(CMP_STRIDE):
                        r = nc.tensor.matmul(ps[:, 2 + kv, 0:N_KV * CPH], wc1[:, kv, l_, :],
                                             cin[:, kv, l_, :, :].rearrange("p g c -> p (g c)"),
                                             start=(l_ == 0), stop=(l_ == CMP_STRIDE - 1))
                    r.then_inc(cmp_ps, 1)
                for s in range(3):
                    for t in range(TT):
                        if s < 2:
                            r = nc.tensor.transpose(ps[:, 4 + s, t * P:(t + 1) * P], vtmp[:, s, t * P:(t + 1) * P],
                                                    ident[:])
                        else:
                            ng = 3 * N_HEADS
                            r = nc.tensor.transpose(ps[:, 6, t * ng:(t + 1) * ng], vtmp[0:ng, s, t * P:(t + 1) * P],
                                                    ident[0:ng, 0:ng])
                    r.then_inc(vt_ps, 1)
                pairs(AFTER_CMP + 1, AFTER_KC + 1)
                pe.wait_ge(gelu_a, 2 * hf + 2)
                pe.wait_ge(wk2_in, 32)
                nc.tensor.matmul(ps[0:HD, 7, 0:N_KV * CPH], wk2[:, 0, :], ck[:, 0, :], start=True, stop=True)
                for g in range(N_KV):
                    r = nc.tensor.matmul(ps[0:CPH, 7, 128 + g * HD:128 + (g + 1) * HD],
                                         ck[:, 1, g * CPH:(g + 1) * CPH], wk2[:, 1, :], start=True, stop=True)
                r.then_inc(kc_ps, 1)
                done = AFTER_KC + 1
                for part, (_t0, _t1, after) in MOD_TILES.items():
                    pairs(done, after + 1)
                    if after == NPROJ - 1:
                        pj(after, 0)
                    if hf == 0:
                        mod_sums(part)
                    done = after + 1
                pe.wait_ge(kc_ok, hf + 1)
                pe.wait_ge(vt_ok, 2 * hf + 2)
                pe.wait_ge(gate_exp, hf + 1)
                pe.wait_ge(pj_free, (hf + 1) * NPROJ + 2)
                for what, u, i in ORDER[hf]:
                    qt, g = UNITS[hf][u]
                    U = hf * NU + u
                    q0 = (qt % TT) * P
                    if what == "N1":
                        mean_square("conv", hf)
                    elif what == "S":
                        h, bk = g * HPG + i[0], i[1]
                        nb = banks_before(hf, u, i[0]) + bk
                        if nb >= NS_B:
                            pe.wait_ge(s_used, nb - NS_B + 1)
                        for branch, k0, n_, at in score_banks(qt, hf)[bk]:
                            o = {"cmp": 0, "sel": N_CMP, "win": N_CMP + SEQ}[branch] + k0
                            dst = ps[:, B_S + nb % NS_B, at:at + n_]
                            nc.tensor.matmul(dst, qhi[:, h, q0:q0 + P], KS[:, g, o:o + n_], start=True, stop=False)
                            r = nc.tensor.matmul(dst, qlo[:, h, q0:q0 + P], KS[:, g, o:o + n_],
                                                 start=False, stop=True)
                        r.then_inc(s_ps, 1)
                    elif what == "T":
                        M = tiles_before(hf, u) + i
                        branch, kt = key_tiles(qt)[i]
                        if i == 0:
                            pe.wait_ge(p_ok, HPG * (U + 1))
                        if M >= NPT:
                            pe.wait_ge(pt_lo, M - NPT + 1)
                        n_ = P
                        if branch == "cmp":
                            at, n_ = 0, CPH * (hf + 1)
                        elif branch == "sel":
                            at = N_CMP + P * kt
                        else:
                            at = N_CMP + P * (qt + 1) + P * (kt - max(0, qt - (WIN_T - 1)))
                        for h in range(HPG):
                            r = nc.tensor.transpose(ps[0:n_, B_PT + M % NPT, h * P:(h + 1) * P],
                                                    prob[hf][:, U % 2, h, at:at + n_], ident[:])
                        r.then_inc(pt_ps, 1)
                    elif what == "V":
                        M = tiles_before(hf, u) + i
                        tiles = key_tiles(qt)
                        branch, kt = tiles[i]
                        if i == 0 and U >= NO:
                            pe.wait_ge(o_sb, U - NO + 1)
                        pe.wait_ge(pt_lo, M + 1)
                        if branch == "cmp":
                            n_ = CPH * (hf + 1)
                            v = VC[0:n_, g, :]
                        else:
                            n_ = P
                            v = VS[:, ("sel", "win").index(branch), kt, g, :]
                        dst = ps[:, B_O + U % NO, :]
                        nc.tensor.matmul(dst, v, pth[0:n_, M % 2, :], start=(i == 0), stop=False)
                        nc.tensor.matmul(dst, v, ptl[0:n_, M % 2, :], start=False, stop=(i == len(tiles) - 1)
                                         ).then_inc(pv_done, 1)
                    elif what == "O1":
                        pe.wait_ge(o_sb, U + 1)
                        if U:
                            pe.wait_ge(y_ok, U)
                        for h in range(HPG):
                            r = nc.tensor.transpose(ps[:, B_OT, h * P:(h + 1) * P], osb[:, h * P:(h + 1) * P], ident[:])
                        r.then_inc(ot_ps, 1)
                    elif what == "O2":
                        pe.wait_ge(o_norm, U + 1)
                        for k in range(2):
                            r = nc.tensor.transpose(ps[:, B_OT, k * P:(k + 1) * P],
                                                    ob[:, 2 * k:2 * k + 2, :].rearrange("p h d -> p (h d)"), ident[:])
                        r.then_inc(y_ps, 1)
                pe.wait_ge(conv_ok, (hf + 1) * CT)
                for m in range(DT):
                    n = base + NPROJ + m
                    pe.wait_ge(w_lo, n + 1)
                    if m >= NY:
                        pe.wait_ge(res_sb, hf * DT + m - NY + 1)
                    for k in range(DT):
                        if m == 0 and k == CT:
                            pe.wait_ge(y_ok, (hf + 1) * NU)
                        s = slice(k * P, (k + 1) * P)
                        hi_, lo_ = (ychi, yclo) if k < CT else (yahi, yalo)
                        r = three(ps[:, B_Y + m % NY, :], whi[:, n % 2, s], wlo[:, n % 2, s],
                                  hi_[:, k % CT, :], lo_[:, k % CT, :], k == 0, k == DT - 1)
                    r.then_inc(w_done, 1)
                    if m < 2 and hf == 0:
                        pe.wait_ge(x_in, 16 * TT * NHF)
                        for k in range(4 * m, 4 * m + 4):
                            if k >= NX1:
                                pe.wait_ge(xt_sb, DT + k - NX1 + 1)
                            x_transpose(1, k, B_X1 + k % NX1)
                    elif m == 2:
                        mean_square(*(("n1", 1) if hf == 0 else ("n2", 0)))
            for hf in range(NHF):
                base = FFN0 + hf * PER_FFN
                pe.wait_ge(h_lo, (NHF + hf + 1) * DT)

                def gate_up(fp):
                    for s in range(2):
                        pe.wait_ge(w_lo, fp * 4 + (base + 2 * s + 1))
                        pe.wait_ge(silu_ok, fp * 2 + (hf * FT + s + 1))
                        feature_tile(ps[:, B_GU + 2 * s, :], 0, h2hi, h2lo).then_inc(w_done, 1)
                        pe.wait_ge(w_lo, fp * 4 + (base + 2 * s + 2))
                        pe.wait_ge(a_ok, fp * 2 + (hf * FT + s + 1))
                        feature_tile(ps[:, B_GU + 2 * s + 1, :], 1, h2hi, h2lo).then_inc(w_done, 1)

                gate_up(0)
                mean_square(*(("mix", 1) if hf == 0 else ("ffn", 0)))
                for fp in range(1, PEEL):
                    gate_up(fp)
                if hf:
                    result_back(0)
                with pe.Fori(PEEL, FT // 2) as fp:
                    gate_up(fp)

                def down_pair(i, first):
                    for s in range(2):
                        if not first:
                            pe.wait_ge(sq_done, i * 2 + (NORM["ffn", hf][1] + s - NY + 1))
                        for c, (k0, k1) in enumerate(DOWN_K):
                            t = len(DOWN_K) * s + c
                            pe.wait_ge(w_lo, i * (2 * len(DOWN_K)) + (base + 2 * FT + t + 1))
                            if first and s == 0 and c in (0, len(DOWN_K) - 1):
                                pe.wait_ge(a_lo, hf * FT + 1 + (FT if c else DOWN_K[1][1]))
                            for k in range(k0, k1):
                                v = slice((k - k0) * P, (k - k0 + 1) * P)
                                r = three(ps[:, B_Y + s, :], whi[:, t % 2, v], wlo[:, t % 2, v],
                                          ahi[:, k, :], alo[:, k, :], k == 0, k == FT - 1)
                            r.then_inc(w_done, 1)
                        if first and s == 0 and hf == 0:
                            mean_square("n2", 1)

                down_pair(0, True)
                with pe.Fori(1, DT // 2) as i:
                    down_pair(i, False)
            mean_square("ffn", 1)
            result_back(1)


_INS = ["x", "c", "w_mod", "b_mod", "g_pre_mix", "w_in", "conv_w", "pos_cmp", "w_ck1", "w_ck2", "w_cv1", "w_cv2",
        "g_conv_out", "g_attn_out", "w_out", "g_post_mix", "g_pre_ffn", "w_gate", "w_up", "w_down", "g_post_ffn"]


def kernel(**inputs):
    import concourse.bacc as _bacc
    from concourse.bass_utils import run_bass_kernel_spmd as _run

    nc = _bacc.Bacc("TRN2", target_bir_lowering=False, num_devices=1)
    arrays, args = {}, []
    for name in _INS:
        a = np.ascontiguousarray(inputs[name])
        arrays[f"in_{name}"] = a
        args.append(nc.dram_tensor(f"in_{name}", a.shape, mybir.dt.from_np(a.dtype), kind="ExternalInput").ap())
    out = nc.dram_tensor("out_x", [1, SEQ, D], F32, kind="ExternalOutput").ap()
    build(nc, *args, out)
    r = _run(nc, [arrays], core_ids=[0])
    return r.results[0]["out_x"]
```

```python
from contextlib import ExitStack

import numpy as np

import concourse.bass as bass
from concourse import mybir

F32 = mybir.dt.float32
F32R = mybir.dt.float32r
ALU = mybir.AluOpType
ACT = mybir.ActivationFunctionType
AX_X = mybir.AxisListType.X

P = 128
SEQ = 1024
D = 1024
DT = D // P
HALF = 512
NHF = SEQ // HALF
TT = HALF // P
D_CONV = 512
CT = D_CONV // P
N_KV, HPG, HD = 2, 4, 64
N_HEADS = N_KV * HPG
CMP_STRIDE = 16
CMP_LEN = 32
N_CMP = SEQ // CMP_STRIDE
CPH = N_CMP // NHF
WIN_T = 5
D_FF = 2816
FT = D_FF // P
COL_Q, COL_KV, COL_G = 1536, 2048, 2816
BIG = 1e30
EPS = 1e-6

PROJ = ([("kcmp", 0), ("vcmp", 0), ("vsel", 0), ("vwin", 0), ("gate", 0), ("ksel", 0), ("kwin", 0)]
        + [("q", j) for j in range(CT)]
        + [(kind, j) for j in range(CT) for kind in ("cb", "cc", "cv")])
NPROJ = len(PROJ)
AFTER_CMP, AFTER_KC = 5, 7
MOD_TILES = {2: (0, 5, 7), 3: (6, 11, 13), 4: (12, 17, 19), 5: (18, NPROJ - 1, NPROJ - 1)}
PER_HALF = NPROJ + DT
FFN0 = NHF * PER_HALF
PEEL = 4
DOWN_K = [(0, DT), (DT, 2 * DT), (2 * DT, FT)]
PER_FFN = 2 * FT + len(DOWN_K) * DT
NTILES = FFN0 + NHF * PER_FFN

NORMS = [("n1", 0, DT), ("conv", 0, CT), ("n1", 1, DT), ("mix", 0, DT), ("conv", 1, CT), ("n2", 0, DT),
         ("mix", 1, DT), ("n2", 1, DT), ("ffn", 0, DT), ("ffn", 1, DT)]
NORM = {}
_at = 0
for _i, (_name, _h, _n) in enumerate(NORMS):
    NORM[_name, _h] = (_i, _at, _n)
    _at += _n

VEC_N = (DT, 6 * DT, DT, DT, DT, DT, CT, CT, CT, CT, CT)
VEC_AT = [(sum(VEC_N[:i]), sum(VEC_N[:i + 1])) for i in range(len(VEC_N))]
NVEC = sum(VEC_N)

DOWN_PEEL = 4
N2_SQUARED = {0: 3, 1: 6, 2: DT}
N2_NORMED = {4: 2, 5: 4, 6: 6, 7: DT}
DOWN_SQUARES = {2: (0, 1), 3: (2, 3)}
MIX_SQUARES = {DT - 1: range(5)}
LATE_MIX_SQUARES = (range(5, DT), ())
NXT_SQUARED = {0: 4, 1: DT}
NXT_NORMED = {4: 2, 5: 5, 6: DT}
LAG = 3
WLAG = (3, 3)
FRONT = (1.6, 1.5)
HEADS_AT = ((0.2, "O1"), (0.4, "OR"), (0.6, "OP"), (0.9, "O2"))
PARTS = 6
NM = 4


def attention_order(hf):
    units = [(qt, g) for qt in range(TT * hf, TT * hf + TT) for g in range(N_KV)]

    def scores(u):
        nb = len(score_banks(units[u][0], hf))
        steps = []
        for h in range(HPG):
            for b in range(nb):
                steps.append(("S", u, (h, b)))
                if b == min(WLAG[hf], nb) - 1 and h:
                    steps.append(("W", u, h - 1))
        return steps + [("W", u, HPG - 1)]

    order = scores(0) + [("N1", 0, 0)]
    for u, (qt, g) in enumerate(units):
        n = len(key_tiles(qt))
        nxt = scores(u + 1) if u + 1 < len(units) else []
        total = len(nxt)
        body = []
        for i in range(n):
            body.append(("T", u, i))
            if i >= LAG:
                body.append(("V", u, i - LAG))
            while nxt and (total - len(nxt)) < (i + 1) * total * FRONT[hf] / n:
                body.append(nxt.pop(0))
        body += nxt + [("V", u, i) for i in range(n - min(n, LAG), n)]
        if u:
            fin = [(at, (what, u - 1, 0)) for at, what in HEADS_AT]
        else:
            fin = [(0.2, ("N2", 0, 0))]
        for at, step in reversed(fin):
            body.insert(int(at * len(body)), step)
        order += body + [("C", u, 0)]
    last = len(units) - 1
    order += [("O1", last, 0), ("OR", last, 0), ("X", 0, 0), ("OP", last, 0), ("O2", last, 0)]
    return units, order


def delayed(order, kinds):
    out, held = [], []
    last = {u: i for what, u, i in order if what == "T"}
    at = None
    for step in order:
        if step[0] == "T":
            out += [step] + held
            held, at = [], step
        elif step[0] in kinds and at and at[2] < last[at[1]]:
            held.append(step)
        else:
            out.append(step)
    return out


def scores_first(order):
    out, tile = [], None
    for step in order:
        if tile and step[0] != "S":
            out.append(tile)
            tile = None
        if step[0] == "T":
            tile = step
        else:
            out.append(step)
    return out


def second_halves(order):
    out, second = [], []
    for step in order:
        if second and (step[0] == "O2" or step[0] == "T" and step[1] == second[0][1]):
            out += second + [step]
        else:
            out += [step] + second
        second = [(step[0] + "2", step[1], step[2])] if step[0] in ("W", "OR") else []
    return out + second


def key_tiles(qt):
    first = max(0, qt - (WIN_T - 1))
    return [("cmp", 0)] + [("sel", k) for k in range(qt + 1)] + [("win", k) for k in range(first, qt + 1)]


def score_banks(qt, hf):
    wc = CPH * (hf + 1)
    sel = P * (qt + 1)
    first = max(0, qt - (WIN_T - 1))
    win = P * (qt + 1 - first)
    banks = [[("cmp", 0, wc, 0)]]
    if win > 512:
        banks[0].append(("win", P * first + 512, win - 512, 64))
    banks.append([("win", P * first, min(win, 512), 0)])
    for c in range(0, sel, 512):
        banks.append([("sel", c, min(512, sel - c), 0)])
    return banks


UNITS, ORDER, ORDER_DVE, ORDER_ACT = {}, {}, {}, {}
for _h in range(NHF):
    UNITS[_h], ORDER[_h] = attention_order(_h)
    ORDER_DVE[_h] = second_halves(scores_first(ORDER[_h]))
    ORDER_ACT[_h] = delayed(ORDER[_h], ("S",))
NU = len(UNITS[0])


def tiles_before(hf, u):
    return sum(len(key_tiles(qt)) for h in range(hf + 1) for v, (qt, g) in enumerate(UNITS[h]) if (h, v) < (hf, u))


def banks_before(hf, u, h):
    n = 0
    for a in range(hf + 1):
        for v, (qt, g) in enumerate(UNITS[a]):
            if (a, v) < (hf, u):
                n += HPG * len(score_banks(qt, a))
            elif (a, v) == (hf, u):
                n += h * len(score_banks(qt, a))
    return n


def build(nc, x, c, w_mod, b_mod, g_pre_mix, w_in, conv_w, pos_cmp, w_ck1, w_ck2, w_cv1, w_cv2,
          g_conv_out, g_attn_out, w_out, g_post_mix, g_pre_ffn, w_gate, w_up, w_down, g_post_ffn, out):
    xin_v = x[0].rearrange("(t p) d -> t p d", p=P)
    out_v = out[0].rearrange("(t p) d -> t p d", p=P)
    xT_dram = nc.dram_tensor("xT_dram", [NHF, P, DT * HALF], F32, kind="Internal").ap()
    x1_dram = nc.dram_tensor("x1_dram", [NHF, P, DT * HALF], F32, kind="Internal").ap()

    keep = ExitStack()
    with keep:
        def alloc(stack):
            def sb(name, shape, dt=F32):
                return stack.enter_context(nc.sbuf_tensor(name, shape, dt))
            return sb

        def sem(name):
            return keep.enter_context(nc.semaphore(name))

        sb = alloc(keep)
        raw = sb("raw", [P, 2, D])
        whi = sb("whi", [P, 2, D], F32R)
        wlo = sb("wlo", [P, 2, D], F32R)
        ident = sb("ident", [P, P])
        ones = sb("ones", [P, P])
        dist_sel = sb("dist_sel", [P, SEQ])
        dist_win = sb("dist_win", [P, WIN_T * P])
        dist_cmp = sb("dist_cmp", [P, 120])
        sq = sb("sq", [P, 2, HALF])
        ssum = sb("ssum", [P, HALF])
        rstd = sb("rstd", [P, HALF])
        vcol = sb("vcol", [P, NVEC])
        cT, bmodT, g1T, gpmT, g2T, gpfT, gcT, gaT, cw0, cw1, cw2 = (vcol[:, a:b] for a, b in VEC_AT)
        siluc = sb("siluc", [P, DT])
        modT = sb("modT", [P, 6 * DT])
        a1 = sb("a1", [P, DT])
        a2 = sb("a2", [P, DT])
        cm = sb("cm", [P, DT])
        cf = sb("cf", [P, DT])
        posT = sb("posT", [P, CMP_LEN])
        smin = sb("smin", [P, 2, 3 * HPG])
        ssumexp = sb("ssumexp", [P, 2, 3 * HPG])
        wgt = sb("wgt", [P, 2, 3 * HPG])
        nz = sb("nz", [P, 1])
        gate = sb("gate", [P, TT, 3 * N_HEADS])
        rtok = sb("rtok", [P, TT])
        zcar = sb("zcar", [P, CT, 2])
        hs = sb("hs", [P, HPG])
        hv = sb("hv", [P, HPG])
        hr = sb("hr", [P, HPG])
        half_neg = sb("half_neg", [P, HPG])

        mixer = ExitStack()
        sb = alloc(mixer)
        KS = sb("KS", [P, N_KV, N_CMP + 2 * SEQ], F32R)
        VS = sb("VS", [P, 2, SEQ // P, N_KV, P], F32R)
        VC = sb("VC", [N_CMP, N_KV, P], F32R)
        wk2 = sb("wk2", [P, 2, HD])
        acar = sb("acar", [HD, 2, CMP_STRIDE, N_KV])
        attn = ExitStack()
        sb = alloc(attn)
        qhi = sb("qhi", [P, N_HEADS, HALF], F32R)
        qlo = sb("qlo", [P, N_HEADS, HALF], F32R)
        yahi = sb("yahi", [P, CT, HALF], F32R)
        yalo = sb("yalo", [P, CT, HALF], F32R)
        ychi = sb("ychi", [P, CT, HALF], F32R)
        yclo = sb("yclo", [P, CT, HALF], F32R)
        PW = N_CMP + SEQ + WIN_T * P
        prob1 = sb("prob1", [P, 2, HPG, PW])
        pth = sb("pth", [P, 2, HALF], F32R)
        ptl = sb("ptl", [P, 2, HALF], F32R)
        osb = sb("osb", [P, HALF])
        oq = sb("oq", [P, HPG, P])
        ob = sb("ob", [P, HPG, HD])
        attn.close()
        first = ExitStack()
        sb = alloc(first)
        sb("under_q0", [P, 2, DT, HALF])
        sb("under_y0", [P, 4, CT, HALF])
        prob0 = sb("prob0", [P, 2, HPG, N_CMP + 2 * HALF])
        sb("between", [P, 2 * P])
        xin1 = sb("xin1", [P, TT, D])
        prob = (prob0, prob1)
        first.close()
        proj = ExitStack()
        sb = alloc(proj)
        xin0 = sb("xin0", [P, TT, D])
        XT = sb("XT", [P, DT, HALF])
        wc1 = sb("wc1", [P, 2, CMP_STRIDE, P])
        sb("under_conv_out", [P, 2, CT, HALF])
        hhi = sb("hhi", [P, DT, HALF], F32R)
        hlo = sb("hlo", [P, DT, HALF], F32R)
        macc = sb("macc", [P, 2, D])
        cin = sb("cin", [P, 2, CMP_STRIDE, N_KV, CPH])
        vtmp = sb("vtmp", [P, 3, HALF])
        cc_sb = sb("cc_sb", [P, HALF])
        cb_sb = sb("cb_sb", [P, HALF])
        z = sb("z", [P, HALF + 2])
        zc = sb("zc", [P, HALF])

        ck = sb("ck", [P, 2, N_KV * CPH])
        vrow = sb("vrow", [NVEC, P])
        posr = sb("posr", [CMP_LEN, P])
        proj.close()
        convv = ExitStack()
        sb = alloc(convv)
        sb("under_x2", [P, 2, DT, HALF])
        sb("under_yahi", [P, CT, HALF])
        yc = sb("yc", [P, CT, HALF])
        wm = sb("wm", [P, NM, D])
        xin = (xin0, xin1)
        convv.close()
        nrm = ExitStack()
        sb = alloc(nrm)
        sb("under_x", [P, 2, DT, HALF])
        sb("under_conv_w", [P, 2, 2 * CT, HALF])
        sb("under_h", [P, 2, DT, HALF])
        sb("under_macc", [P, 2, D])
        tn = sb("tn", [P, 2, HALF])
        hn = sb("hn", [P, 2, HALF])
        nrm.close()
        post = ExitStack()
        sb = alloc(post)
        res0 = sb("res0", [P, DT, HALF])
        sb("under_y", [P, 2 * DT, HALF])
        XR = sb("XR", [P, DT, HALF])
        post.close()
        mixer.close()
        ffn = ExitStack()
        sb = alloc(ffn)
        h2hi = sb("h2hi", [P, DT, HALF], F32R)
        h2lo = sb("h2lo", [P, DT, HALF], F32R)
        ahi = sb("ahi", [P, FT, HALF], F32R)
        alo = sb("alo", [P, FT, HALF], F32R)
        X1 = sb("X1", [P, DT, HALF])
        fres = sb("fres", [P, DT, HALF])
        ffn.close()
        ffn2 = ExitStack()
        sb = alloc(ffn2)
        sb("under_h2", [P, 2, DT, HALF])
        sb("under_a", [P, 2, FT, HALF])
        sb("under_x1", [P, 2, DT, HALF])
        tn2 = sb("tn2", [P, 2, HALF])
        hn2 = sb("hn2", [P, 2, HALF])
        sg = sb("sg", [P, HALF])
        aa = sb("aa", [P, HALF])
        ffn2.close()
        tail = ExitStack()
        sb = alloc(tail)
        fT = sb("fT", [P, TT, D])
        xT = sb("xT", [P, TT, D])
        tail.close()
        outv = ExitStack()
        sb = alloc(outv)
        sb("under_h3", [P, 2, DT, HALF])
        sb("under_a3", [P, 2, FT, HALF])
        sb("under_x3", [P, DT, HALF])
        osum = sb("osum", [P, TT, D])
        res = (res0, fres)
        outv.close()

        ps = keep.enter_context(nc.psum_tensor("ps", [P, 8, HALF], F32))
        B_PJ, B_S, NS_B, B_PT, NPT, B_O, NO, B_OT = 0, 0, 3, 3, 3, 6, 1, 7
        NPB = 4
        B_Y, NY = 0, 2
        B_GU = 2
        B_X1, NX1 = 2, 4
        B_BACK, NBACK = 2, 4
        B_OUT = (0, 1, 6)

        small_in = sem("small_in")
        consts = sem("consts")
        raw_in = [sem("raw_in0"), sem("raw_in1")]
        w_hi = sem("w_hi")
        w_lo = sem("w_lo")
        w_done = sem("w_done")
        mod_in = [[sem(f"mod_in_{q}{s}") for s in range(NM)] for q in ("sp", "pool")]
        mod_acc = sem("mod_acc")
        mod_sum = sem("mod_sum")
        mod_ready = sem("mod_ready")
        vec_ps = sem("vec_ps")
        vec_ok = sem("vec_ok")
        wk2_in = sem("wk2_in")
        silu_c = sem("silu_c")
        x_in = sem("x_in")
        xt_ps = sem("xt_ps")
        xt_sb = sem("xt_sb")
        xt_out = sem("xt_out")
        sq_done = sem("sq_done")
        ssum_done = sem("ssum_done")
        ms_ps = sem("ms_ps")
        ms_sb = sem("ms_sb")
        rms_sb = sem("rms_sb")
        rstd_ok = sem("rstd_ok")
        tn_done = sem("tn_done")
        hn_done = sem("hn_done")
        h_hi = sem("h_hi")
        h_lo = sem("h_lo")
        pj_free = sem("pj_free")
        ev_a = sem("ev_a")
        vt_ps = sem("vt_ps")
        vt_hi = sem("vt_hi")
        vt_ok = sem("vt_ok")
        gate_exp = sem("gate_exp")
        wc_in = sem("wc_in")
        cmp_ps = sem("cmp_ps")
        gelu_a = sem("gelu_a")
        kc_ps = sem("kc_ps")
        kc_hi = sem("kc_hi")
        kc_ok = sem("kc_ok")
        conv_y = sem("conv_y")
        conv_n = sem("conv_n")
        conv_hi = sem("conv_hi")
        conv_ok = sem("conv_ok")
        s_ps = sem("s_ps")
        s_used = sem("s_used")
        e_done = sem("e_done")
        inv_ok = sem("inv_ok")
        wgt_ok = sem("wgt_ok")
        hs_ok = sem("hs_ok")
        p_ok = sem("p_ok")
        pt_ps = sem("pt_ps")
        pt_hi = sem("pt_hi")
        pt_lo = sem("pt_lo")
        pv_done = sem("pv_done")
        o_sb = sem("o_sb")
        ot_ps = sem("ot_ps")
        oq_sb = sem("oq_sb")
        o_sum = sem("o_sum")
        o_sq = sem("o_sq")
        o_ms = sem("o_ms")
        o_rstd = sem("o_rstd")
        o_norm = sem("o_norm")
        y_ps = sem("y_ps")
        y_hi = sem("y_hi")
        y_ok = sem("y_ok")
        res_sb = sem("res_sb")
        xr_in = sem("xr_in")
        x1_ok = sem("x1_ok")
        x1_out = sem("x1_out")
        x1_in = sem("x1_in")
        silu_ok = sem("silu_ok")
        a_ok = sem("a_ok")
        a_hi = sem("a_hi")
        a_lo = sem("a_lo")
        ft_ps = sem("ft_ps")
        ft_sb = sem("ft_sb")
        y_out = sem("y_out")
        last_ok = sem("last_ok")
        dchain = sem("dchain")
        pchain = sem("pchain")

        def pt_hi_lo(hf, M):
            if M % NPB < 2:
                return pth[:, M % NPB, :], ptl[:, M % NPB, :]
            slot = (hf * PER_HALF + NPROJ + 1) % 2
            v = slice((M % NPB - 2) * HALF, (M % NPB - 1) * HALF)
            return whi[:, slot, v], wlo[:, slot, v]

        def mod_bank(part):
            return ps[:, B_PT + part % 2, 0:DT]

        def tile_width(n):
            t = (n - FFN0) % PER_FFN - 2 * FT
            k0, k1 = DOWN_K[t % len(DOWN_K)] if n >= FFN0 and t >= 0 else (0, DT)
            return (k1 - k0) * P

        def load_mod(eng, m):
            if m >= NM:
                eng.wait_ge(mod_acc, m - NM + 1)
            part, k = m // DT, m % DT
            eng.dma_start(wm[:, m % NM, :], w_mod[0, k * P:(k + 1) * P, part * D:(part + 1) * D]
                          ).then_inc(mod_in[m >= 2 * DT][m % NM], 16)

        block = keep.enter_context(nc.Block())

        class Chain:
            def __init__(self, eng, s):
                self.eng, self.s, self.n = eng, s, 0

            def inc(self, ins):
                ins.then_inc(self.s, 1)
                self.n += 1

            def wait(self):
                self.eng.wait_ge(self.s, self.n)

        @block.sync
        def _(sp):
            def small(dst, src):
                sp.dma_start(dst, src).then_inc(small_in, 16)

            def load_raw(n, src):
                if n >= 2:
                    sp.wait_ge(w_lo, n - 1)
                for dst, s in src:
                    sp.dma_start(dst, s).then_inc(raw_in[n % 2], 16)

            def tile_of(n, w, c0):
                return [(raw[:, n % 2, :].rearrange("p (k m) -> p k m", k=DT),
                         w[:, c0:c0 + P].rearrange("(k p) m -> p k m", p=P))]

            for (a, b), v in zip(VEC_AT, (c[0], b_mod[0], g_pre_mix[0], g_post_mix[0], g_pre_ffn[0], g_post_ffn[0],
                                          g_conv_out[0], g_attn_out[0], conv_w[0, 0], conv_w[0, 1], conv_w[0, 2])):
                small(vrow[a:b, :], v.rearrange("(k p) -> k p", p=P))
            for g in range(N_KV):
                small(posr[:, g * HD:(g + 1) * HD], pos_cmp[0])
            def load_w(n, w, c0):
                load_raw(n, tile_of(n, w, c0))

            def gate_up_pair(base, f2):
                for s in range(2):
                    for w_, w in enumerate((w_gate, w_up)):
                        sp.wait_ge(w_lo, f2 * 2 + (base + 2 * s + w_ - 1))
                        sp.dma_start(raw[:, w_, :].rearrange("p (k m) -> p k m", k=DT),
                                     w[0][:, bass.ds(f2 * P + s * P, P)].rearrange("(k p) m -> p k m", p=P)
                                     ).then_inc(raw_in[w_], 16)

            def store_first_half():
                for t in range(TT):
                    sp.wait_ge(ft_sb, (t + 1) * 2)
                    sp.dma_start(out_v[t], osum[:, t, :]).then_inc(y_out, 16)

            for m in range(NM):
                load_mod(sp, m)
            for t in range(TT):
                sp.dma_start(xin0[:, t, :], xin_v[t]).then_inc(x_in, 16)
            for m in range(NM, 2 * DT):
                load_mod(sp, m)
            sp.dma_start(wk2[:, 0, :], w_ck2[0]).then_inc(wk2_in, 16)
            sp.dma_start(wk2[:, 1, :], w_cv2[0]).then_inc(wk2_in, 16)
            for hf in range(NHF):
                for t, (kind, j) in enumerate(PROJ):
                    n = hf * PER_HALF + t
                    c0 = {"kcmp": COL_KV, "vcmp": COL_KV + P, "ksel": COL_KV + 2 * P, "vsel": COL_KV + 3 * P,
                          "kwin": COL_KV + 4 * P, "vwin": COL_KV + 5 * P, "gate": COL_G, "q": COL_Q + j * P,
                          "cb": j * P, "cc": D_CONV + j * P, "cv": 2 * D_CONV + j * P}[kind]
                    if kind == "gate":
                        ng = 3 * N_HEADS
                        r = raw[:, n % 2, :].rearrange("p (k m) -> p k m", k=DT)
                        src = [(r[:, :, 0:ng], w_in[0][:, COL_G:COL_G + ng].rearrange("(k p) m -> p k m", p=P)),
                               (r[:, :, ng:P], w_in[0][:, 0:P - ng].rearrange("(k p) m -> p k m", p=P))]
                        load_raw(n, src)
                    else:
                        load_w(n, w_in[0], c0)
                    if t == 2:
                        if hf:
                            sp.wait_ge(w_done, hf * PER_HALF)
                            sp.dma_start(XR[:].rearrange("p k n -> p (k n)"), xT_dram[0]).then_inc(xr_in, 16)
                        for kv, w1 in ((0, w_ck1), (1, w_cv1)):
                            for h2 in range(2):
                                sp.dma_start(wc1[h2 * HD:(h2 + 1) * HD, kv, :, :],
                                             w1[0, h2 * CMP_STRIDE:(h2 + 1) * CMP_STRIDE].rearrange("l d h -> d l h")
                                             ).then_inc(wc_in, 16)
                        sp.wait_ge(xt_sb, DT * (hf + 1))
                        sp.dma_start(xT_dram[hf], XT[:].rearrange("p k n -> p (k n)")).then_inc(xt_out, 16)
                    if hf and t == 10:
                        sp.wait_ge(x1_ok, DT)
                        sp.dma_start(x1_dram[0], XR[:].rearrange("p k n -> p (k n)")).then_inc(x1_out, 16)
                for m in range(DT):
                    if hf == 0 and m == 2:
                        sp.wait_ge(conv_y, CT)
                        sp.wait_ge(mod_sum, PARTS)
                        for t in range(TT):
                            sp.dma_start(xin1[:, t, :], xin_v[TT + t]).then_inc(x_in, 16)
                    if hf and m == 4:
                        sp.wait_ge(x1_out, 16)
                        sp.wait_ge(pt_ps, tiles_before(1, NU))
                        sp.dma_start(X1[:].rearrange("p k n -> p (k n)"), x1_dram[0]).then_inc(x1_in, 16)
                    load_w(hf * PER_HALF + NPROJ + m, w_out[0], m * P)
            for hf in range(NHF):
                base = FFN0 + hf * PER_FFN
                gate_up_pair(base, 0)
                if hf == 0:
                    sp.wait_ge(tn_done, (NHF + 1) * DT)
                    sp.wait_ge(xt_out, 16 * NHF)
                    sp.dma_start(X1[:].rearrange("p k n -> p (k n)"), xT_dram[1]).then_inc(xr_in, 16)
                else:
                    sp.wait_ge(tn_done, 2 * NHF * DT)
                    sp.wait_ge(x1_out, 32)
                    sp.dma_start(X1[:].rearrange("p k n -> p (k n)"), x1_dram[0]).then_inc(x1_in, 16)
                for fp in range(1, PEEL + 1):
                    gate_up_pair(base, 2 * fp)
                if hf == 0:
                    sp.wait_ge(x1_ok, NHF * DT)
                    sp.dma_start(x1_dram[1], X1[:].rearrange("p k n -> p (k n)")).then_inc(x1_out, 16)
                else:
                    store_first_half()
                with sp.Fori(PEEL + 1, FT // 2) as fp:
                    gate_up_pair(base, fp * 2)
                if hf == 1:
                    sp.wait_ge(ft_ps, 2 * TT)
                    sp.dma_start(X1[:].rearrange("p k n -> p (k n)"), x1_dram[1]).then_inc(x1_in, 16)
                with sp.Fori(0, DT // 2) as i:
                    for s in range(2 * len(DOWN_K)):
                        k0, k1 = DOWN_K[s % len(DOWN_K)]
                        sp.wait_ge(w_lo, i * (2 * len(DOWN_K)) + (base + 2 * FT + s - 1))
                        sp.dma_start(raw[:, s % 2, 0:(k1 - k0) * P].rearrange("p (k m) -> p k m", m=P),
                                     w_down[0][k0 * P:k1 * P, bass.ds(i * (2 * P) + s // len(DOWN_K) * P, P)]
                                     .rearrange("(k p) m -> p k m", p=P)).then_inc(raw_in[s % 2], 16)
            for t in range(TT):
                sp.wait_ge(last_ok, t + 1)
                sp.dma_start(out_v[TT + t], fT[:, t, :]).then_inc(y_out, 16)
            sp.wait_ge(y_out, 16 * TT * NHF)

        @block.gpsimd
        def _(pool):
            ch = Chain(pool, pchain)

            ch.inc(nc.gpsimd.memset(ident[:], 0.0))
            ch.wait()
            nc.gpsimd.affine_select(out=ident[:], in_=ident[:], compare_op=ALU.not_equal, fill=1.0, base=0,
                                    pattern=[[-1, P]], channel_multiplier=1).then_inc(consts, 1)
            nc.gpsimd.memset(ones[:], 1.0).then_inc(consts, 1)
            ch.inc(nc.gpsimd.memset(nz[:], 1.0))
            ch.inc(nc.gpsimd.memset(half_neg[:], -0.5))
            ch.inc(nc.gpsimd.iota(dist_sel[:], pattern=[[-1, SEQ]], base=SEQ - P, channel_multiplier=1,
                                  allow_small_or_imprecise_dtypes=True))
            ch.inc(nc.gpsimd.iota(dist_win[:], pattern=[[-1, WIN_T * P]], base=(WIN_T - 1) * P, channel_multiplier=1,
                                  allow_small_or_imprecise_dtypes=True))
            ch.inc(nc.gpsimd.iota(dist_cmp[:], pattern=[[-CMP_STRIDE, 120]], base=56 * CMP_STRIDE - (CMP_STRIDE - 1),
                                  channel_multiplier=1, allow_small_or_imprecise_dtypes=True))
            ch.wait()

            ch.inc(nc.gpsimd.affine_select(out=nz[:], in_=nz[:], compare_op=ALU.is_ge, fill=0.0, base=-(CMP_LEN - 1),
                                           pattern=[[0, 1]], channel_multiplier=1))
            ch.inc(nc.gpsimd.affine_select(out=dist_sel[:], in_=dist_sel[:], compare_op=ALU.is_ge, fill=BIG,
                                           base=SEQ - P, pattern=[[-1, SEQ]], channel_multiplier=1))
            ch.inc(nc.gpsimd.affine_select(out=dist_win[:], in_=dist_win[:], compare_op=ALU.is_ge, fill=BIG,
                                           base=(WIN_T - 1) * P, pattern=[[-1, WIN_T * P]], channel_multiplier=1))
            ch.inc(nc.gpsimd.affine_select(out=dist_cmp[:], in_=dist_cmp[:], compare_op=ALU.is_ge, fill=BIG,
                                           base=56 * CMP_STRIDE - (CMP_STRIDE - 1), pattern=[[-CMP_STRIDE, 120]],
                                           channel_multiplier=1))
            ch.wait()
            ch.inc(nc.gpsimd.affine_select(out=dist_win[:], in_=dist_win[:], compare_op=ALU.is_ge, fill=BIG,
                                           base=511 - (WIN_T - 1) * P, pattern=[[1, WIN_T * P]],
                                           channel_multiplier=-1))
            ch.wait()
            nc.gpsimd.memset(acar[:], 0.0).then_inc(consts, 1)
            for m in range(2 * DT, PARTS * DT):
                load_mod(pool, m)

            for hf in range(NHF):
                for what, u, i in ORDER[hf]:
                    qt, g = UNITS[hf][u]
                    U = hf * NU + u
                    if what == "W":
                        pool.wait_ge(wgt_ok, HPG * U + i + 1)
                        wc = CPH * (hf + 1)
                        ns = P * (qt + 1)
                        nw = P * min(qt + 1, WIN_T)
                        for b, lo_, n_ in ((0, 0, wc), (1, N_CMP, ns), (2, N_CMP + ns, nw)):
                            v = prob[hf][:, U % 2, i, lo_:lo_ + n_]
                            r = nc.gpsimd.tensor_scalar(v, v, wgt[:, U % 2, 3 * i + b:3 * i + b + 1], 1.0,
                                                        ALU.mult, ALU.mult)
                        r.then_inc(p_ok, 1)
                    elif what == "O1":
                        pool.wait_ge(oq_sb, U + 1)
                        if U:
                            pool.wait_ge(y_ps, U)
                        nc.gpsimd.tensor_tensor(ob[:], oq[:, :, 0:HD], oq[:, :, HD:P], ALU.add).then_inc(o_sum, 1)
                        pool.wait_ge(o_sum, U + 1)
                        nc.gpsimd.tensor_tensor(oq[:, :, 0:HD], ob[:], ob[:], ALU.mult).then_inc(o_sq, 1)
                    elif what == "OP":
                        pool.wait_ge(o_ms, U + 1)
                        nc.gpsimd.tensor_tensor(hr[:], hv[:], half_neg[:], ALU.pow).then_inc(o_rstd, 1)
                        pool.wait_ge(o_rstd, U + 1)
                        nc.gpsimd.tensor_tensor(ob[:], ob[:], hr[:].unsqueeze(2).to_broadcast([P, HPG, HD]),
                                                ALU.mult).then_inc(o_norm, 1)

        @block.scalar
        def _(act):
            def split_hi(n):
                extra = sum(1 for h in range(NHF) for t, (k, _j) in enumerate(PROJ)
                            if k == "gate" and h * PER_HALF + t <= n and (h * PER_HALF + t) % 2 == n % 2)
                act.wait_ge(raw_in[n % 2], 16 * (n // 2 + 1 + extra))
                if n >= 2:
                    act.wait_ge(w_done, n - 1)
                v = slice(0, tile_width(n))
                nc.scalar.activation(whi[:, n % 2, v], raw[:, n % 2, v], ACT.Copy).then_inc(w_hi, 1)

            def square(norm, hf, k, src):
                i, at, n = NORM[norm, hf]
                if at + k >= 2:
                    act.wait_ge(ssum_done, at + k + i)
                nc.scalar.activation(sq[:, (at + k) % 2, :], src, ACT.Square).then_inc(sq_done, 1)

            def squares(norm, hf, src, ready):
                for k in range(NORM[norm, hf][2]):
                    ready(k)
                    square(norm, hf, k, src(k))

            def root(norm, hf):
                i, at, n = NORM[norm, hf]
                act.wait_ge(ms_sb, i + 1)
                nc.scalar.activation(ssum[:], ssum[:], ACT.Sqrt).then_inc(rms_sb, 1)

            def modulate(norm, hf, k0, k1):
                m0 = (hf if norm == "n1" else NHF + hf) * DT
                tn_, hn_, hi_, a, b0 = {"n1": (tn, hn, hhi, a1, 0), "n2": (tn2, hn2, h2hi, a2, 3 * DT)}[norm]
                for k in range(k0, k1):
                    act.wait_ge(tn_done, m0 + k + 1)
                    if m0 + k >= 2:
                        act.wait_ge(h_lo, m0 + k - 1)
                    nc.scalar.activation(hn_[:, k % 2, :], tn_[:, k % 2, :], ACT.Identity,
                                         scale=a[:, k:k + 1], bias=modT[:, b0 + k:b0 + k + 1]).then_inc(hn_done, 1)
                    act.wait_ge(hn_done, m0 + k + 1)
                    nc.scalar.activation(hi_[:, k, :], hn_[:, k % 2, :], ACT.Copy).then_inc(h_hi, 1)

            def mix_squares(hf, tiles):
                for k in tiles:
                    act.wait_ge(res_sb, hf * DT + k + 1)
                    square("mix", hf, k, res[hf][:, k, :])

            def xt_copy(hf, k, bank):
                act.wait_ge(xt_ps, hf * DT + k + 1)
                nc.scalar.activation(XT[:, k, :], ps[:, bank, :], ACT.Copy).then_inc(xt_sb, 1)
                act.wait_ge(xt_sb, hf * DT + k + 1)
                square("n1", hf, k, XT[:, k, :])

            def result_out():
                for n in range(2 * TT):
                    act.wait_ge(ft_ps, n + 1)
                    nc.scalar.activation(osum[:, n // 2, n % 2 * HALF:(n % 2 + 1) * HALF], ps[:, B_OUT[n % len(B_OUT)], :],
                                         ACT.Copy).then_inc(ft_sb, 1)

            def back_out(m):
                for s, dst in enumerate((fT, xT)):
                    n = 2 * m + s
                    act.wait_ge(ft_ps, 2 * TT + n + 1)
                    nc.scalar.activation(dst[:, :, m * P:(m + 1) * P],
                                         ps[:, B_BACK + n % NBACK, :].rearrange("p (t f) -> p t f", t=TT),
                                         ACT.Copy).then_inc(ft_sb, 1)

            def aux_cmp(hf):
                for kv in range(2):
                    s = hf * 2 + kv
                    act.wait_ge(cmp_ps, s + 1)
                    nc.scalar.activation(ck[:, kv, :], ps[:, 2 + kv, 0:N_KV * CPH], ACT.Gelu_apprx_tanh
                                         ).then_inc(gelu_a, 1)
                for s in range(2):
                    act.wait_ge(vt_ps, hf * 3 + s + 1)
                    nc.scalar.activation(VS[:, s, hf * TT:(hf + 1) * TT, :, 0:HD],
                                         ps[:, 4 + s, :].rearrange("p (t g d) -> p t g d", t=TT, g=N_KV),
                                         ACT.Copy).then_inc(vt_hi, 1)
                act.wait_ge(vt_ps, hf * 3 + 3)
                nc.scalar.activation(gate[:], ps[:, 6, 0:TT * 3 * N_HEADS].rearrange("p (t n) -> p t n", t=TT), ACT.Exp,
                                     scale=-1.0).then_inc(gate_exp, 1)

            def aux_kc(hf):
                act.wait_ge(kc_ps, hf + 1)
                nc.scalar.activation(KS[0:HD, :, CPH * hf:CPH * (hf + 1)],
                                     ps[0:HD, 7, 0:N_KV * CPH].rearrange("p (g c) -> p g c", g=N_KV), ACT.Copy)
                nc.scalar.activation(VC[CPH * hf:CPH * (hf + 1), :, 0:HD],
                                     ps[0:CPH, 7, 128:256].rearrange("p (g d) -> p g d", g=N_KV),
                                     ACT.Copy).then_inc(kc_hi, 1)

            act.wait_ge(vec_ps, 1)
            nc.scalar.activation(vcol[:], ps[:, 0, 0:NVEC], ACT.Copy)
            nc.scalar.activation(posT[:], ps[:, 0, P:P + CMP_LEN], ACT.Copy).then_inc(vec_ok, 1)
            act.wait_ge(vec_ok, 1)
            nc.scalar.activation(siluc[:], cT, ACT.Silu).then_inc(silu_c, 1)

            for k in range(DT):
                xt_copy(0, k, k)
            root("n1", 0)
            split_hi(0)
            split_hi(1)
            act.wait_ge(mod_ready, 2)
            modulate("n1", 0, 0, DT)
            for hf in range(NHF):
                base = hf * PER_HALF
                for t, (kind, j) in enumerate(PROJ):
                    if t + 2 <= NPROJ:
                        split_hi(base + t + 2)
                    if hf and t < 2:
                        mix_squares(0, LATE_MIX_SQUARES[t])
                    if hf and t == 2:
                        root("mix", 0)
                    bank = ps[:, B_PJ + t % 2, :]
                    act.wait_ge(w_done, base + t + 1)
                    if kind in ("ksel", "kwin"):
                        o = N_CMP + (SEQ if kind == "kwin" else 0) + hf * HALF
                        for g in range(N_KV):
                            r = nc.scalar.activation(KS[0:HD, g, o:o + HALF], bank[g * HD:(g + 1) * HD, :], ACT.Copy)
                    elif kind == "q":
                        if j == 0:
                            act.wait_ge(h_lo, (hf + 1) * DT)
                            act.wait_ge(xt_out, 16 * (hf + 1))
                            if hf:
                                act.wait_ge(x1_ok, DT)
                        for s in range(2):
                            h = 2 * j + s
                            for r_ in range(2):
                                r = nc.scalar.activation(qhi[r_ * HD:(r_ + 1) * HD, h, :], bank[s * HD:(s + 1) * HD, :],
                                                         ACT.Copy, scale=-(2.0 ** (h + 1)) / 8.0)
                    else:
                        r = None
                    if r is not None:
                        r.then_inc(ev_a, 1)
                    if t == AFTER_CMP + 1:
                        aux_cmp(hf)
                    elif t == AFTER_KC + 1:
                        aux_kc(hf)
                    elif kind == "cb" and j:
                        act.wait_ge(conv_y, hf * CT + j)
                        square("conv", hf, j - 1, yc[:, j - 1, :])
                for what, u, i in ORDER_ACT[hf]:
                    qt, g = UNITS[hf][u]
                    U = hf * NU + u
                    wc = CPH * (hf + 1)
                    ns = P * (qt + 1)
                    nw = P * min(qt + 1, WIN_T)
                    if what == "N1":
                        act.wait_ge(conv_y, (hf + 1) * CT)
                        square("conv", hf, CT - 1, yc[:, CT - 1, :])
                        root("conv", hf)
                    elif what == "N2":
                        for k in range(CT):
                            act.wait_ge(conv_n, hf * CT + k + 1)
                            nc.scalar.activation(ychi[:, k, :], yc[:, k, :], ACT.Copy, scale=gcT[:, k:k + 1]
                                                 ).then_inc(conv_hi, 1)
                    elif what == "S":
                        h, bk = i
                        nb = len(score_banks(qt, hf))
                        br = {0: 0, 1: 2, nb - 1: 1}.get(bk)
                        if br is not None:
                            lo_, n_ = ((1, wc - 1), (N_CMP, ns), (N_CMP + ns, nw))[br]
                            act.wait_ge(s_used, banks_before(hf, u, h) + bk + 1)
                            v = prob[hf][:, U % 2, h, lo_:lo_ + n_]
                            s = 3 * h + br
                            nc.scalar.activation(v, v, ACT.Exp, bias=smin[:, U % 2, s:s + 1], scale=-1.0,
                                                 accum_out=ssumexp[:, U % 2, s:s + 1]).then_inc(e_done, 1)
                    elif what == "T":
                        M = tiles_before(hf, u) + i
                        n_ = CPH * (hf + 1) if i == 0 else P
                        act.wait_ge(pt_ps, M + 1)
                        if M >= NPB:
                            act.wait_ge(pv_done, M - NPB + 1)
                        nc.scalar.activation(pt_hi_lo(hf, M)[0][0:n_, :], ps[0:n_, B_PT + M % NPT, :], ACT.Copy).then_inc(pt_hi, 1)
                    elif what == "C":
                        act.wait_ge(pv_done, tiles_before(hf, u + 1))
                        if U:
                            act.wait_ge(ot_ps, U)
                        nc.scalar.activation(osb[:], ps[:, B_O + U % NO, :], ACT.Copy).then_inc(o_sb, 1)
                    elif what == "O1":
                        act.wait_ge(ot_ps, U + 1)
                        nc.scalar.activation(oq[:], ps[:, B_OT, :].rearrange("p (h d) -> p h d", h=HPG),
                                             ACT.Copy).then_inc(oq_sb, 1)
                    elif what == "O2":
                        act.wait_ge(y_ps, U + 1)
                        k0 = 2 * g
                        q0 = (qt % TT) * P
                        for k in range(2):
                            r = nc.scalar.activation(yahi[:, k0 + k, q0:q0 + P], ps[:, B_OT, k * P:(k + 1) * P],
                                                     ACT.Copy, scale=gaT[:, k0 + k:k0 + k + 1])
                        r.then_inc(y_hi, 1)
                split_hi(base + NPROJ + 1)
                nxt = ("n1", 1) if hf == 0 else ("n2", 0)
                for m in range(DT):
                    split_hi(base + NPROJ + m + 2)
                    if m == 0 and hf == 0:
                        for k in range(NXT_SQUARED[0]):
                            xt_copy(1, k, B_X1 + k % NX1)
                    act.wait_ge(w_done, base + NPROJ + m + 1)
                    nc.scalar.activation(res[hf][:, m, :], ps[:, B_Y + m % NY, :], ACT.Copy).then_inc(res_sb, 1)
                    for k in range(NXT_SQUARED.get(m - 1, 0), NXT_SQUARED.get(m, 0)):
                        if hf == 0:
                            if m:
                                xt_copy(1, k, B_X1 + k % NX1)
                        else:
                            act.wait_ge(x1_in, 16)
                            square("n2", 0, k, X1[:, k, :])
                    if m == 3:
                        root(*nxt)
                    modulate(*nxt, NXT_NORMED.get(m - 1, 0), NXT_NORMED.get(m, 0))
                    mix_squares(hf, MIX_SQUARES.get(m, ()))
            for hf in range(NHF):
                base = FFN0 + hf * PER_FFN
                extra = [sum(1 for h in range(NHF) for t, (k, _j) in enumerate(PROJ)
                             if k == "gate" and (h * PER_HALF + t) % 2 == s) for s in range(2)]

                def split_hi_f(n0, f2):
                    act.wait_ge(raw_in[n0 % 2], f2 * 8 + 16 * (n0 // 2 + 1 + extra[n0 % 2]))
                    act.wait_ge(w_done, f2 + (n0 - 1))
                    v = slice(0, tile_width(n0))
                    nc.scalar.activation(whi[:, n0 % 2, v], raw[:, n0 % 2, v], ACT.Copy).then_inc(w_hi, 1)

                def gate_up(fp):
                    for s in range(2):
                        split_hi_f(base + 2 + 2 * s, fp * 4)
                        act.wait_ge(w_done, fp * 4 + (base + 2 * s + 1))
                        act.wait_ge(a_ok, fp * 2 + (hf * FT + s + 2))
                        nc.scalar.activation(sg[:], ps[:, B_GU + 2 * s, :], ACT.Silu).then_inc(silu_ok, 1)
                        split_hi_f(base + 3 + 2 * s, fp * 4)
                        act.wait_ge(a_ok, fp * 2 + (hf * FT + s + 3))
                        nc.scalar.activation(ahi[:, bass.ds(fp * 2 + s, 1), :].rearrange("p a n -> p (a n)"), aa[:],
                                             ACT.Copy).then_inc(a_hi, 1)
                        if hf == 0 and isinstance(fp, int) and fp == 0:
                            mix_squares(1, LATE_MIX_SQUARES[s])

                gate_up(0)
                root(*(("mix", 1) if hf == 0 else ("ffn", 0)))
                for fp in range(1, PEEL):
                    gate_up(fp)
                if hf:
                    result_out()
                with act.Fori(PEEL, FT // 2) as fp:
                    gate_up(fp)

                def down_tile(m):
                    for c in range(len(DOWN_K)):
                        t = len(DOWN_K) * m + c
                        if base + 2 * FT + t + 2 < NTILES:
                            split_hi(base + 2 * FT + t + 2)
                        if hf == 0:
                            for k in range(N2_SQUARED.get(t - 1, 0), N2_SQUARED.get(t, 0)):
                                square("n2", 1, k, X1[:, k, :])
                            modulate("n2", 1, N2_NORMED.get(t - 1, 0), N2_NORMED.get(t, 0))
                    act.wait_ge(w_done, base + 2 * FT + len(DOWN_K) * (m + 1))
                    if m == 0 and hf:
                        act.wait_ge(y_out, 16 * TT * hf)
                    if hf:
                        nc.scalar.activation(fres[:, m, :], ps[:, B_Y + m % NY, :], ACT.Copy, scale=cf[:, m:m + 1]
                                             ).then_inc(res_sb, 1)
                        square("ffn", 1, m, ps[:, B_Y + m % NY, :])
                        if m:
                            back_out(m - 1)
                        return
                    nc.scalar.activation(fres[:, m, :], ps[:, B_Y + m % NY, :], ACT.Copy).then_inc(res_sb, 1)
                    if m == 0:
                        root("n2", 1)
                    act.wait_ge(res_sb, NHF * DT + m + 1)
                    for k in DOWN_SQUARES.get(m, ()):
                        square("ffn", 0, k, fres[:, k, :])

                if hf == 0:
                    act.wait_ge(x1_ok, NHF * DT)
                for m in range(DT if hf else DOWN_PEEL):
                    down_tile(m)
                if hf == 0:
                    i_, at, _n = NORM["ffn", 0]
                    with act.Fori(DOWN_PEEL // 2, DT // 2) as i:
                        for s in range(2):
                            for c in range(len(DOWN_K)):
                                split_hi_f(base + 2 * FT + len(DOWN_K) * s + c + 2, i * (2 * len(DOWN_K)))
                            act.wait_ge(w_done, i * (2 * len(DOWN_K)) + (base + 2 * FT + (s + 1) * len(DOWN_K)))
                            m = bass.ds(i * 2 + s, 1)
                            nc.scalar.activation(fres[:, m, :].rearrange("p a n -> p (a n)"), ps[:, B_Y + s, :],
                                                 ACT.Copy).then_inc(res_sb, 1)
                            act.wait_ge(ssum_done, i * 2 + (at + s + i_))
                            nc.scalar.activation(sq[:, (at + s) % 2, :], ps[:, B_Y + s, :], ACT.Square
                                                 ).then_inc(sq_done, 1)
            act.wait_ge(ms_sb, len(NORMS))
            nc.scalar.activation(rtok[:], rtok[:], ACT.Sqrt).then_inc(rms_sb, 1)
            back_out(DT - 1)

        @block.vector
        def _(dve):
            ch = Chain(dve, dchain)

            def split_lo(n):
                dve.wait_ge(w_hi, n + 1)
                v = slice(0, tile_width(n))
                nc.vector.tensor_tensor(wlo[:, n % 2, v], raw[:, n % 2, v], whi[:, n % 2, v].bitcast(F32),
                                        ALU.subtract).then_inc(w_lo, 1)

            def clear_sum(norm, hf):
                i, at, n = NORM[norm, hf]
                if i:
                    dve.wait_ge(rstd_ok, i)
                nc.vector.memset(ssum[:], 0.0).then_inc(ssum_done, 1)

            def add_square(norm, hf, k):
                i, at, n = NORM[norm, hf]
                dve.wait_ge(sq_done, at + k + 1)
                dve.wait_ge(ssum_done, at + k + i + 1)
                nc.vector.tensor_tensor(ssum[:], ssum[:], sq[:, (at + k) % 2, :], ALU.add).then_inc(ssum_done, 1)

            def mean(norm, hf, width):
                i, at, n = NORM[norm, hf]
                dve.wait_ge(ms_ps, i + 1)
                nc.vector.tensor_scalar(ssum[:], ps[:, B_OT, :], 1.0 / width, EPS, ALU.mult, ALU.add
                                        ).then_inc(ms_sb, 1)

            def inverse_root(norm, hf):
                i, at, n = NORM[norm, hf]
                dve.wait_ge(rms_sb, i + 1)
                nc.vector.reciprocal(rstd[:], ssum[:]).then_inc(rstd_ok, 1)
                dve.wait_ge(rstd_ok, i + 1)

            def rms(norm, hf, width):
                mean(norm, hf, width)
                inverse_root(norm, hf)

            def normed(norm, hf, k0, k1):
                m0 = (hf if norm == "n1" else NHF + hf) * DT
                src, tn_, hn_, hi_, lo_ = {"n1": (XT, tn, hn, hhi, hlo), "n2": (X1, tn2, hn2, h2hi, h2lo)}[norm]
                for k in range(k0, k1 + (k0 < k1 == DT)):
                    if k < DT:
                        if m0 + k >= 2:
                            dve.wait_ge(hn_done, m0 + k - 1)
                        nc.vector.tensor_tensor(tn_[:, k % 2, :], src[:, k, :], rstd[:], ALU.mult).then_inc(tn_done, 1)
                    if k:
                        dve.wait_ge(h_hi, m0 + k)
                        nc.vector.tensor_tensor(lo_[:, k - 1, :], hn_[:, (k - 1) % 2, :], hi_[:, k - 1, :].bitcast(F32),
                                                ALU.subtract).then_inc(h_lo, 1)

            def mod_step(m):
                part, k = m // DT, m % DT
                later = m >= 2 * DT
                dve.wait_ge(mod_in[later][m % NM], 16 * ((m - 2 * DT * later) // NM + 1))
                acc = macc[:, part % 2, :]
                if k == 0:
                    dve.wait_ge(silu_c, 1)
                    if part > 1:
                        dve.wait_ge(mod_sum, part - 1)
                    nc.vector.tensor_scalar(acc, wm[:, m % NM, :], siluc[:, k:k + 1], None, ALU.mult
                                            ).then_inc(mod_acc, 1)
                else:
                    dve.wait_ge(mod_acc, m)
                    nc.vector.scalar_tensor_tensor(acc, wm[:, m % NM, :], siluc[:, k:k + 1], acc,
                                                   ALU.mult, ALU.add).then_inc(mod_acc, 1)

            def mod_vector(part):
                dve.wait_ge(mod_sum, part + 1)
                if part == 0:
                    dve.wait_ge(vec_ok, 1)
                v = modT[:, part * DT:(part + 1) * DT]
                r = nc.vector.tensor_tensor(v, mod_bank(part), bmodT[:, part * DT:(part + 1) * DT], ALU.add)
                if part in (1, 2, 4, 5):
                    ch.inc(r)
                    ch.wait()
                if part in (1, 4):
                    r = nc.vector.scalar_tensor_tensor({1: a1, 4: a2}[part][:], v, 1.0, {1: g1T, 4: g2T}[part],
                                                       ALU.add, ALU.mult)
                elif part in (2, 5):
                    r = nc.vector.tensor_tensor({2: cm, 5: cf}[part][:], v, {2: gpmT, 5: gpfT}[part], ALU.mult)
                r.then_inc(mod_ready, 1)

            def residual(step, src, coef, xt):
                for k in range(step % 2 * 4, step % 2 * 4 + 4):
                    if step < 2:
                        ch.inc(nc.vector.tensor_tensor(src[:, k, :], src[:, k, :], rstd[:], ALU.mult))
                    else:
                        ch.wait()
                        nc.vector.scalar_tensor_tensor(xt[:, k, :], src[:, k, :], coef[:, k:k + 1], xt[:, k, :],
                                                       ALU.mult, ALU.add).then_inc(x1_ok, 1)

            def aux_cmp(hf):
                for s in range(2):
                    dve.wait_ge(vt_hi, hf * 2 + s + 1)
                    nc.vector.tensor_tensor(VS[:, s, hf * TT:(hf + 1) * TT, :, HD:P],
                                            ps[:, 4 + s, :].rearrange("p (t g d) -> p t g d", t=TT, g=N_KV),
                                            VS[:, s, hf * TT:(hf + 1) * TT, :, 0:HD].bitcast(F32),
                                            ALU.subtract).then_inc(vt_ok, 1)
                dve.wait_ge(gate_exp, hf + 1)
                ch.inc(nc.vector.tensor_scalar(gate[:], gate[:], 1.0, None, ALU.add))
                ch.wait()
                ch.inc(nc.vector.reciprocal(gate[:], gate[:]))
                ch.wait()
                if hf == 0:
                    gv = gate[:, 0, :].rearrange("p (h b) -> p h b", b=3)[:, :, 0]
                    ch.inc(nc.vector.tensor_scalar(gv, gv, nz[:], None, ALU.mult))
                    ch.wait()

            def aux_kc(hf):
                dve.wait_ge(kc_hi, hf + 1)
                ch.inc(nc.vector.tensor_tensor(KS[HD:P, :, CPH * hf:CPH * (hf + 1)],
                                               ps[0:HD, 7, 0:N_KV * CPH].rearrange("p (g c) -> p g c", g=N_KV),
                                               KS[0:HD, :, CPH * hf:CPH * (hf + 1)].bitcast(F32), ALU.subtract))
                nc.vector.tensor_tensor(VC[CPH * hf:CPH * (hf + 1), :, HD:P],
                                        ps[0:CPH, 7, 128:256].rearrange("p (g d) -> p g d", g=N_KV),
                                        VC[CPH * hf:CPH * (hf + 1), :, 0:HD].bitcast(F32),
                                        ALU.subtract).then_inc(kc_ok, 1)

            for m in range(NM):
                mod_step(m)
            clear_sum("n1", 0)
            for k in range(DT):
                mod_step(NM + k)
                add_square("n1", 0, k)
            mod_step(NM + DT)
            mean("n1", 0, D)
            for m in range(NM + DT + 1, 2 * DT - 1):
                mod_step(m)
            inverse_root("n1", 0)
            split_lo(0)
            mod_step(2 * DT - 1)
            mod_vector(0)
            mod_vector(1)
            dve.wait_ge(mod_ready, 2)
            nc.vector.memset(z[:, 0:2], 0.0).then_inc(pj_free, 2)
            normed("n1", 0, 0, DT)
            split_lo(1)
            dve.wait_ge(h_lo, DT)
            ch.inc(nc.vector.memset(cin[0:HD, :, :, :, 0:1], 0.0))
            ch.wait()
            for hf in range(NHF):
                base = hf * PER_HALF
                ev = hf * 6
                for t, (kind, j) in enumerate(PROJ):
                    T = hf * NPROJ + t
                    if t + 2 <= NPROJ:
                        split_lo(base + t + 2)
                    bank = ps[:, B_PJ + t % 2, :]
                    dve.wait_ge(w_done, base + t + 1)
                    if kind in ("kcmp", "vcmp"):
                        kv = ("kcmp", "vcmp").index(kind)
                        v = bank.rearrange("p (c l) -> p l c", l=CMP_STRIDE)
                        if hf:
                            nc.vector.tensor_copy(cin[0:HD, kv, :, :, 0], acar[:, kv, :, :])
                        for g in range(N_KV):
                            gs = slice(g * HD, (g + 1) * HD)
                            pa = posT[gs, 0:CMP_STRIDE].unsqueeze(2).to_broadcast([HD, CMP_STRIDE, CPH - 1])
                            pb = posT[gs, CMP_STRIDE:CMP_LEN].unsqueeze(2).to_broadcast([HD, CMP_STRIDE, CPH])
                            nc.vector.tensor_tensor(cin[0:HD, kv, :, g, 1:CPH], v[gs, :, 0:CPH - 1], pa, ALU.add)
                            r = nc.vector.tensor_tensor(cin[HD:P, kv, :, g, :], v[gs, :, :], pb, ALU.add)
                            if hf == 0:
                                r = nc.vector.tensor_tensor(acar[:, kv, :, g], v[gs, :, CPH - 1],
                                                            posT[gs, 0:CMP_STRIDE], ALU.add)
                        r.then_inc(pj_free, 1)
                    elif kind in ("ksel", "kwin"):
                        ev += 1
                        dve.wait_ge(ev_a, ev)
                        o = N_CMP + (SEQ if kind == "kwin" else 0) + hf * HALF
                        for g in range(N_KV):
                            r = nc.vector.tensor_tensor(KS[HD:P, g, o:o + HALF], bank[g * HD:(g + 1) * HD, :],
                                                        KS[0:HD, g, o:o + HALF].bitcast(F32), ALU.subtract)
                        r.then_inc(pj_free, 1)
                    elif kind == "q":
                        ev += 1
                        dve.wait_ge(ev_a, ev)
                        for s in range(2):
                            h = 2 * j + s
                            for r_ in range(2):
                                r = nc.vector.scalar_tensor_tensor(
                                    qlo[r_ * HD:(r_ + 1) * HD, h, :], bank[s * HD:(s + 1) * HD, :],
                                    -(2.0 ** (h + 1)) / 8.0, qhi[r_ * HD:(r_ + 1) * HD, h, :].bitcast(F32),
                                    ALU.mult, ALU.subtract)
                        r.then_inc(pj_free, 1)
                    elif kind == "cv":
                        dve.wait_ge(pj_free, T + 2)
                        ch.wait()
                        if hf:
                            ch.inc(nc.vector.tensor_copy(z[:, 0:2], zcar[:, j, :]))
                        nc.vector.tensor_tensor(z[:, 2:HALF + 2], bank, cc_sb[:], ALU.mult).then_inc(pj_free, 1)
                        dve.wait_ge(pj_free, T + 3)
                        if hf:
                            ch.wait()
                        if hf == 0:
                            ch.inc(nc.vector.tensor_copy(zcar[:, j, :], z[:, HALF:HALF + 2]))
                        ch.inc(nc.vector.tensor_scalar(zc[:], z[:, 2:HALF + 2], cw2[:, j:j + 1], None, ALU.mult))
                        ch.wait()
                        ch.inc(nc.vector.scalar_tensor_tensor(zc[:], z[:, 1:HALF + 1], cw1[:, j:j + 1], zc[:],
                                                              ALU.mult, ALU.add))
                        ch.wait()
                        ch.inc(nc.vector.scalar_tensor_tensor(zc[:], z[:, 0:HALF], cw0[:, j:j + 1], zc[:],
                                                              ALU.mult, ALU.add))
                        ch.wait()
                        nc.vector.tensor_tensor(yc[:, j, :], zc[:], cb_sb[:], ALU.mult).then_inc(conv_y, 1)
                    else:
                        dst = {"vsel": vtmp[:, 0, :], "vwin": vtmp[:, 1, :], "gate": vtmp[:, 2, :],
                               "cb": cb_sb[:], "cc": cc_sb[:]}[kind]
                        if kind == "cb" and T > j:
                            dve.wait_ge(conv_y, hf * CT + j)
                        nc.vector.tensor_copy(dst, bank).then_inc(pj_free, 1)
                    if hf and t < 2:
                        for k in LATE_MIX_SQUARES[t]:
                            add_square("mix", 0, k)
                    if hf and t == 2:
                        rms("mix", 0, D)
                    elif hf and 3 <= t < 7:
                        dve.wait_ge(xr_in, 16)
                        residual(t - 3, res0, cm, XR)
                    if t == AFTER_CMP + 1:
                        aux_cmp(hf)
                    elif t == AFTER_KC + 1:
                        aux_kc(hf)
                    elif kind == "cc" and j:
                        add_square("conv", hf, j - 1)
                    elif kind == "cb" and j == 0:
                        clear_sum("conv", hf)
                    if hf == 0:
                        for part, (t0, t1, after) in MOD_TILES.items():
                            if t0 <= t <= t1:
                                for m in range((t - t0) * DT // (t1 - t0 + 1), (t - t0 + 1) * DT // (t1 - t0 + 1)):
                                    mod_step(part * DT + m)
                            if t == after + 1:
                                mod_vector(part)
                dve.wait_ge(conv_y, (hf + 1) * CT)
                ch.inc(nc.vector.memset(prob[hf][:, :, :, 0:1], 0.0))
                ch.wait()
                for what, u, i in ORDER_DVE[hf]:
                    qt, g = UNITS[hf][u]
                    U = hf * NU + u
                    ns = P * (qt + 1)
                    if what == "N1":
                        add_square("conv", hf, CT - 1)
                        if hf == 0:
                            mod_vector(PARTS - 1)
                        rms("conv", hf, D_CONV)
                        for k in range(CT):
                            nc.vector.tensor_tensor(yc[:, k, :], yc[:, k, :], rstd[:], ALU.mult).then_inc(conv_n, 1)
                    elif what == "N2":
                        for k in range(CT):
                            dve.wait_ge(conv_hi, hf * CT + k + 1)
                            nc.vector.scalar_tensor_tensor(yclo[:, k, :], yc[:, k, :], gcT[:, k:k + 1],
                                                           ychi[:, k, :].bitcast(F32), ALU.mult, ALU.subtract
                                                           ).then_inc(conv_ok, 1)
                    elif what == "S":
                        h, bk = i
                        slope = 2.0 ** -(g * HPG + h + 1)
                        first = max(0, qt - (WIN_T - 1))
                        nb = banks_before(hf, u, h) + bk
                        if i == (0, 0) and u >= 2:
                            dve.wait_ge(pt_ps, tiles_before(hf, u - 1))
                        dve.wait_ge(s_ps, nb + 1)
                        for branch, k0, n_, at in score_banks(qt, hf)[bk]:
                            br = ("cmp", "sel", "win").index(branch)
                            s = smin[:, U % 2, 3 * h + br:3 * h + br + 1]
                            skip = 0
                            if branch == "cmp":
                                skip = 1
                                tab = dist_cmp[:, 56 - 8 * qt + 1:56 - 8 * qt + n_]
                                d0 = 0
                            elif branch == "sel":
                                tab = dist_sel[:, k0 - P * qt + SEQ - P:k0 - P * qt + SEQ - P + n_]
                                d0 = N_CMP + k0
                            else:
                                tab = dist_win[:, k0 - P * qt + (WIN_T - 1) * P:k0 - P * qt + (WIN_T - 1) * P + n_]
                                d0 = N_CMP + ns + k0 - P * first
                            init = 3.0e38
                            if branch == "sel" and k0 or branch == "win" and bk == 1 and n_ == 512 and qt >= WIN_T - 1:
                                init = s
                                dve.wait_ge(s_used, nb)
                            r = nc.vector.tensor_tensor_reduce(
                                prob[hf][:, U % 2, h, d0 + skip:d0 + n_], ps[:, B_S + nb % NS_B, at + skip:at + n_], tab,
                                slope, init, ALU.add, ALU.min, s)
                        r.then_inc(s_used, 1)
                    elif what == "W":
                        dve.wait_ge(e_done, 3 * (HPG * U + i + 1))
                        s = slice(3 * i, 3 * i + 3)
                        nc.vector.reciprocal(wgt[:, U % 2, s], ssumexp[:, U % 2, s]).then_inc(inv_ok, 1)
                    elif what == "W2":
                        dve.wait_ge(inv_ok, HPG * U + i + 1)
                        s = slice(3 * i, 3 * i + 3)
                        s3 = g * 3 * HPG + 3 * i
                        nc.vector.tensor_tensor(wgt[:, U % 2, s], wgt[:, U % 2, s], gate[:, qt % TT, s3:s3 + 3],
                                                ALU.mult).then_inc(wgt_ok, 1)
                    elif what == "T":
                        M = tiles_before(hf, u) + i
                        n_ = CPH * (hf + 1) if i == 0 else P
                        dve.wait_ge(pt_hi, M + 1)
                        nc.vector.tensor_tensor(pt_hi_lo(hf, M)[1][0:n_, :], ps[0:n_, B_PT + M % NPT, :],
                                                pt_hi_lo(hf, M)[0][0:n_, :].bitcast(F32), ALU.subtract).then_inc(pt_lo, 1)
                    elif what == "OR":
                        dve.wait_ge(o_sq, U + 1)
                        nc.vector.tensor_reduce(hs[:], oq[:, :, 0:HD], AX_X, ALU.add).then_inc(hs_ok, 1)
                    elif what == "OR2":
                        dve.wait_ge(hs_ok, U + 1)
                        nc.vector.tensor_scalar(hv[:], hs[:], 1.0 / HD, EPS, ALU.mult, ALU.add).then_inc(o_ms, 1)
                    elif what == "O2":
                        dve.wait_ge(y_hi, U + 1)
                        k0 = 2 * g
                        q0 = (qt % TT) * P
                        for k in range(2):
                            r = nc.vector.scalar_tensor_tensor(
                                yalo[:, k0 + k, q0:q0 + P], ps[:, B_OT, k * P:(k + 1) * P], gaT[:, k0 + k:k0 + k + 1],
                                yahi[:, k0 + k, q0:q0 + P].bitcast(F32), ALU.mult, ALU.subtract)
                        r.then_inc(y_ok, 1)
                split_lo(base + NPROJ + 1)
                nxt = ("n1", 1) if hf == 0 else ("n2", 0)
                for m in range(DT):
                    split_lo(base + NPROJ + m + 2)
                    if m == 0:
                        clear_sum(*nxt)
                    for k in range(NXT_SQUARED.get(m - 1, 0), NXT_SQUARED.get(m, 0)):
                        add_square(*nxt, k)
                    if m == 3:
                        rms(*nxt, D)
                        clear_sum("mix", hf)
                    normed(*nxt, NXT_NORMED.get(m - 1, 0), NXT_NORMED.get(m, 0))
                    for k in MIX_SQUARES.get(m, ()):
                        add_square("mix", hf, k)
                    if hf and m == 3:
                        dve.wait_ge(pv_done, tiles_before(1, NU))
                        nc.vector.memset(sg[:], 0.0).then_inc(silu_ok, 2)
                        ch.inc(nc.vector.memset(aa[:, 0:1], 0.0))
                        ch.wait()
                        nc.vector.memset(aa[:, 0:1], 0.0).then_inc(a_ok, 2)
                        dve.wait_ge(a_ok, 2)
                        nc.vector.memset(aa[:, 0:1], 0.0).then_inc(a_lo, 1)
            for hf in range(NHF):
                base = FFN0 + hf * PER_FFN

                def split_lo_f(n0, f2):
                    dve.wait_ge(w_hi, f2 + (n0 + 1))
                    v = slice(0, tile_width(n0))
                    nc.vector.tensor_tensor(wlo[:, n0 % 2, v], raw[:, n0 % 2, v], whi[:, n0 % 2, v].bitcast(F32),
                                            ALU.subtract).then_inc(w_lo, 1)

                def gate_up(fp):
                    for s in range(2):
                        split_lo_f(base + 2 + 2 * s, fp * 4)
                        split_lo_f(base + 3 + 2 * s, fp * 4)
                        dve.wait_ge(silu_ok, fp * 2 + (hf * FT + s + 3))
                        dve.wait_ge(w_done, fp * 4 + (base + 2 * s + 2))
                        dve.wait_ge(a_lo, fp * 2 + (hf * FT + s + 1))
                        nc.vector.tensor_tensor(aa[:], ps[:, B_GU + 2 * s + 1, :], sg[:], ALU.mult).then_inc(a_ok, 1)
                        dve.wait_ge(a_hi, fp * 2 + (hf * FT + s + 1))
                        f = bass.ds(fp * 2 + s, 1)
                        nc.vector.tensor_tensor(alo[:, f, :].rearrange("p a n -> p (a n)"), aa[:],
                                                ahi[:, f, :].rearrange("p a n -> p (a n)").bitcast(F32),
                                                ALU.subtract).then_inc(a_lo, 1)
                        if hf == 0 and isinstance(fp, int) and fp == 0:
                            for k in LATE_MIX_SQUARES[s]:
                                add_square("mix", 1, k)

                gate_up(0)
                if hf == 0:
                    rms("mix", 1, D)
                    dve.wait_ge(xr_in, 32)
                else:
                    rms("ffn", 0, D)
                    dve.wait_ge(x1_in, 32)
                coef = (cm, cf)[hf]
                residual(0, fres, coef, X1)
                for fp in range(1, PEEL):
                    gate_up(fp)
                    if fp < PEEL - 1:
                        residual(fp, fres, coef, X1)
                    if fp == PEEL - 2:
                        residual(fp + 1, fres, coef, X1)
                with dve.Fori(PEEL, FT // 2) as fp:
                    gate_up(fp)
                i_, at, _n = NORM["ffn", hf]

                def down_tile(m):
                    for c in range(len(DOWN_K)):
                        t = len(DOWN_K) * m + c
                        if base + 2 * FT + t + 2 < NTILES:
                            split_lo(base + 2 * FT + t + 2)
                        if hf == 0:
                            for k in range(N2_SQUARED.get(t - 1, 0), N2_SQUARED.get(t, 0)):
                                add_square("n2", 1, k)
                            normed("n2", 1, N2_NORMED.get(t - 1, 0), N2_NORMED.get(t, 0))
                    if m == 0 and hf == 0:
                        rms("n2", 1, D)
                        clear_sum("ffn", 0)
                    for k in DOWN_SQUARES.get(m, ()) if hf == 0 else (m,):
                        add_square("ffn", hf, k)

                clear_sum(*(("n2", 1) if hf == 0 else ("ffn", 1)))
                for m in range(DT if hf else DOWN_PEEL):
                    down_tile(m)
                if hf == 0:
                    with dve.Fori(DOWN_PEEL // 2, DT // 2) as i:
                        for s in range(2):
                            for c in range(len(DOWN_K)):
                                split_lo_f(base + 2 * FT + len(DOWN_K) * s + c + 2, i * (2 * len(DOWN_K)))
                            dve.wait_ge(sq_done, i * 2 + (at + s + 1))
                            dve.wait_ge(ssum_done, i * 2 + (at + s + i_ + 1))
                            nc.vector.tensor_tensor(ssum[:], ssum[:], sq[:, (at + s) % 2, :], ALU.add
                                                    ).then_inc(ssum_done, 1)
            dve.wait_ge(ms_ps, len(NORMS))
            nc.vector.tensor_scalar(rtok[:], ps[:, B_OT, 0:TT], 1.0 / D, EPS, ALU.mult, ALU.add).then_inc(ms_sb, 1)
            dve.wait_ge(rms_sb, len(NORMS))
            nc.vector.reciprocal(rtok[:], rtok[:]).then_inc(rstd_ok, 1)
            dve.wait_ge(rstd_ok, len(NORMS))
            dve.wait_ge(ft_sb, 2 * TT + 2 * DT)
            for t in range(TT):
                nc.vector.scalar_tensor_tensor(fT[:, t, :], fT[:, t, :], rtok[:, t:t + 1], xT[:, t, :],
                                               ALU.mult, ALU.add).then_inc(last_ok, 1)

        @block.tensor
        def _(pe):
            def mean_square(norm, hf):
                i, at, n = NORM[norm, hf]
                pe.wait_ge(ssum_done, at + n + i + 1)
                nc.tensor.matmul(ps[:, B_OT, :], ones[:], ssum[:], start=True, stop=True).then_inc(ms_ps, 1)

            def three(dst, whi_, wlo_, mhi, mlo, start, stop):
                nc.tensor.matmul(dst, whi_, mhi, start=start, stop=False)
                nc.tensor.matmul(dst, whi_, mlo, start=False, stop=False)
                return nc.tensor.matmul(dst, wlo_, mhi, start=False, stop=stop)

            def feature_tile(dst, slot, hi_, lo_, h0=None):
                for k in range(DT):
                    if h0 is not None:
                        pe.wait_ge(h_lo, h0 + k + 1)
                    s = slice(k * P, (k + 1) * P)
                    r = three(dst, whi[:, slot, s], wlo[:, slot, s], hi_[:, k, :], lo_[:, k, :], k == 0, k == DT - 1)
                return r



            def mod_sums(part):
                pe.wait_ge(mod_acc, (part + 1) * DT)
                for m in range(DT):
                    r = nc.tensor.matmul(mod_bank(part)[:, m:m + 1], macc[:, part % 2, m * P:(m + 1) * P], ones[:, 0:1],
                                         start=True, stop=True)
                r.then_inc(mod_sum, 1)

            def result_back():
                pe.wait_ge(x1_ok, (NHF + 1) * DT)
                for n in range(2 * TT):
                    t, s = n // 2, n % 2
                    if n >= len(B_OUT):
                        pe.wait_ge(ft_sb, n - len(B_OUT) + 1)
                    for k in range(4):
                        r = nc.tensor.transpose(ps[:, B_OUT[n % len(B_OUT)], k * P:(k + 1) * P],
                                                X1[:, 4 * s + k, t * P:(t + 1) * P], ident[:])
                    r.then_inc(ft_ps, 1)

            def back(m):
                pe.wait_ge(res_sb, (NHF + 1) * DT + m + 1)
                pe.wait_ge(x1_in, 48)
                for s, src in enumerate((fres, X1)):
                    n = 2 * m + s
                    if n >= NBACK:
                        pe.wait_ge(ft_sb, 2 * TT + n - NBACK + 1)
                    for t in range(TT):
                        r = nc.tensor.transpose(ps[:, B_BACK + n % NBACK, t * P:(t + 1) * P],
                                                src[:, m, t * P:(t + 1) * P], ident[:])
                    r.then_inc(ft_ps, 1)

            pe.wait_ge(consts, 1)
            pe.wait_ge(small_in, 16 * (len(VEC_N) + N_KV))
            nc.tensor.transpose(ps[:, 0, 0:NVEC], vrow[:], ident[0:NVEC, 0:NVEC])
            nc.tensor.transpose(ps[:, 0, P:P + CMP_LEN], posr[:], ident[0:CMP_LEN, 0:CMP_LEN]).then_inc(vec_ps, 1)
            pe.wait_ge(vec_ok, 1)
            def x_transpose(hf, k, bank):
                for t in range(TT):
                    r = nc.tensor.transpose(ps[:, bank, t * P:(t + 1) * P], xin[hf][:, t, k * P:(k + 1) * P], ident[:])
                r.then_inc(xt_ps, 1)

            pe.wait_ge(x_in, 16 * TT)
            for k in range(DT):
                x_transpose(0, k, k)
            pe.wait_ge(consts, 3)
            mean_square("n1", 0)
            mod_sums(0)
            mod_sums(1)
            pe.wait_ge(ms_sb, 1)
            for hf in range(NHF):
                base = hf * PER_HALF
                if hf:
                    pe.wait_ge(res_sb, hf * DT - 1)

                def pj(t0, i2, h0=None):
                    pe.wait_ge(w_lo, i2 + (base + t0 + 1))
                    pe.wait_ge(pj_free, i2 + (hf * NPROJ + t0 + 1))
                    feature_tile(ps[:, B_PJ + t0 % 2, :], (base + t0) % 2, hhi, hlo, h0).then_inc(w_done, 1)

                def pairs(t0, t1):
                    if t1 - t0 >= 4:
                        with pe.Fori(0, (t1 - t0) // 2) as i:
                            pj(t0, i * 2)
                            pj(t0 + 1, i * 2)
                    elif t1 > t0:
                        pj(t0, 0)
                        pj(t0 + 1, 0)

                pj(0, 0, hf * DT)
                if hf:
                    pe.wait_ge(res_sb, hf * DT)
                pj(1, 0)
                if hf:
                    mean_square("mix", 0)
                pairs(2, AFTER_CMP + 1)
                pe.wait_ge(pj_free, hf * NPROJ + 2 + AFTER_CMP)
                pe.wait_ge(wc_in, 64 * (hf + 1))
                for kv in range(2):
                    for l_ in range(CMP_STRIDE):
                        r = nc.tensor.matmul(ps[:, 2 + kv, 0:N_KV * CPH], wc1[:, kv, l_, :],
                                             cin[:, kv, l_, :, :].rearrange("p g c -> p (g c)"),
                                             start=(l_ == 0), stop=(l_ == CMP_STRIDE - 1))
                    r.then_inc(cmp_ps, 1)
                for s in range(3):
                    for t in range(TT):
                        if s < 2:
                            r = nc.tensor.transpose(ps[:, 4 + s, t * P:(t + 1) * P], vtmp[:, s, t * P:(t + 1) * P],
                                                    ident[:])
                        else:
                            ng = 3 * N_HEADS
                            r = nc.tensor.transpose(ps[:, 6, t * ng:(t + 1) * ng], vtmp[0:ng, s, t * P:(t + 1) * P],
                                                    ident[0:ng, 0:ng])
                    r.then_inc(vt_ps, 1)
                pairs(AFTER_CMP + 1, AFTER_KC + 1)
                pe.wait_ge(gelu_a, 2 * hf + 2)
                pe.wait_ge(wk2_in, 32)
                nc.tensor.matmul(ps[0:HD, 7, 0:N_KV * CPH], wk2[:, 0, :], ck[:, 0, :], start=True, stop=True)
                for g in range(N_KV):
                    r = nc.tensor.matmul(ps[0:CPH, 7, 128 + g * HD:128 + (g + 1) * HD],
                                         ck[:, 1, g * CPH:(g + 1) * CPH], wk2[:, 1, :], start=True, stop=True)
                r.then_inc(kc_ps, 1)
                done = AFTER_KC + 1
                for part, (_t0, _t1, after) in MOD_TILES.items():
                    pairs(done, after + 1)
                    if after == NPROJ - 1:
                        pj(after, 0)
                    if hf == 0 and part == 2:
                        pe.wait_ge(vt_ok, 2)
                    if hf == 0 and part < PARTS - 1:
                        mod_sums(part)
                    done = after + 1
                pe.wait_ge(kc_ok, hf + 1)
                pe.wait_ge(vt_ok, 2 * hf + 2)
                pe.wait_ge(gate_exp, hf + 1)
                pe.wait_ge(pj_free, (hf + 1) * NPROJ + 2)
                def second_x(k0, k1):
                    pe.wait_ge(x_in, 16 * TT * NHF)
                    for k in range(k0, k1):
                        if k >= NX1:
                            pe.wait_ge(xt_sb, DT + k - NX1 + 1)
                        x_transpose(1, k, B_X1 + k % NX1)

                def w_out_part(m, k0, k1):
                    n = base + NPROJ + m
                    for k in range(k0, k1):
                        s = slice(k * P, (k + 1) * P)
                        hi_, lo_ = (ychi, yclo) if k < CT else (yahi, yalo)
                        r = three(ps[:, B_Y + m % NY, :], whi[:, n % 2, s], wlo[:, n % 2, s],
                                  hi_[:, k % CT, :], lo_[:, k % CT, :], k == 0, k == DT - 1)
                    return r

                for what, u, i in ORDER[hf]:
                    qt, g = UNITS[hf][u]
                    U = hf * NU + u
                    q0 = (qt % TT) * P
                    if what == "X":
                        pe.wait_ge(conv_ok, (hf + 1) * CT)
                        pe.wait_ge(s_used, banks_before(hf, NU, 0))
                        pe.wait_ge(pt_lo, tiles_before(hf, NU))
                        w_out_part(0, 0, CT)
                        if hf == 0:
                            second_x(0, NX1)
                    elif what == "N1":
                        if hf == 0:
                            mod_sums(PARTS - 1)
                        mean_square("conv", hf)
                    elif what == "S":
                        h, bk = g * HPG + i[0], i[1]
                        nb = banks_before(hf, u, i[0]) + bk
                        if nb >= NS_B:
                            pe.wait_ge(s_used, nb - NS_B + 1)
                        for branch, k0, n_, at in score_banks(qt, hf)[bk]:
                            o = {"cmp": 0, "sel": N_CMP, "win": N_CMP + SEQ}[branch] + k0
                            dst = ps[:, B_S + nb % NS_B, at:at + n_]
                            nc.tensor.matmul(dst, qhi[:, h, q0:q0 + P], KS[:, g, o:o + n_], start=True, stop=False)
                            r = nc.tensor.matmul(dst, qlo[:, h, q0:q0 + P], KS[:, g, o:o + n_],
                                                 start=False, stop=True)
                        r.then_inc(s_ps, 1)
                    elif what == "T":
                        M = tiles_before(hf, u) + i
                        branch, kt = key_tiles(qt)[i]
                        if i == 0:
                            pe.wait_ge(p_ok, HPG * (U + 1))
                        if U == 0 and i == 0:
                            pe.wait_ge(mod_ready, PARTS)
                        if M >= NPT:
                            pe.wait_ge(pt_lo, M - NPT + 1)
                        n_ = P
                        if branch == "cmp":
                            at, n_ = 0, CPH * (hf + 1)
                        elif branch == "sel":
                            at = N_CMP + P * kt
                        else:
                            at = N_CMP + P * (qt + 1) + P * (kt - max(0, qt - (WIN_T - 1)))
                        for h in range(HPG):
                            r = nc.tensor.transpose(ps[0:n_, B_PT + M % NPT, h * P:(h + 1) * P],
                                                    prob[hf][:, U % 2, h, at:at + n_], ident[:])
                        r.then_inc(pt_ps, 1)
                    elif what == "V":
                        M = tiles_before(hf, u) + i
                        tiles = key_tiles(qt)
                        branch, kt = tiles[i]
                        if i == 0 and U >= NO:
                            pe.wait_ge(o_sb, U - NO + 1)
                        pe.wait_ge(pt_lo, M + 1)
                        if branch == "cmp":
                            n_ = CPH * (hf + 1)
                            v = VC[0:n_, g, :]
                        else:
                            n_ = P
                            v = VS[:, ("sel", "win").index(branch), kt, g, :]
                        dst = ps[:, B_O + U % NO, :]
                        nc.tensor.matmul(dst, v, pt_hi_lo(hf, M)[0][0:n_, :], start=(i == 0), stop=False)
                        nc.tensor.matmul(dst, v, pt_hi_lo(hf, M)[1][0:n_, :], start=False, stop=(i == len(tiles) - 1)
                                         ).then_inc(pv_done, 1)
                    elif what == "O1":
                        pe.wait_ge(o_sb, U + 1)
                        if U:
                            pe.wait_ge(y_ok, U)
                        for h in range(HPG):
                            r = nc.tensor.transpose(ps[:, B_OT, h * P:(h + 1) * P], osb[:, h * P:(h + 1) * P], ident[:])
                        r.then_inc(ot_ps, 1)
                    elif what == "O2":
                        pe.wait_ge(o_norm, U + 1)
                        for k in range(2):
                            r = nc.tensor.transpose(ps[:, B_OT, k * P:(k + 1) * P],
                                                    ob[:, 2 * k:2 * k + 2, :].rearrange("p h d -> p (h d)"), ident[:])
                        r.then_inc(y_ps, 1)
                pe.wait_ge(y_ok, (hf + 1) * NU)
                for m in range(DT):
                    if m:
                        pe.wait_ge(w_lo, base + NPROJ + m + 1)
                    if m >= NY:
                        pe.wait_ge(res_sb, hf * DT + m - NY + 1)
                    w_out_part(m, 0 if m else CT, DT).then_inc(w_done, 1)
                    if m == 0 and hf == 0:
                        second_x(NX1, DT)
                    if m == 2:
                        mean_square(*(("n1", 1) if hf == 0 else ("n2", 0)))
            for hf in range(NHF):
                base = FFN0 + hf * PER_FFN

                def gate_up(fp):
                    for s in range(2):
                        pe.wait_ge(w_lo, fp * 4 + (base + 2 * s + 1))
                        pe.wait_ge(silu_ok, fp * 2 + (hf * FT + s + 1))
                        first = isinstance(fp, int) and fp == 0 and s == 0
                        feature_tile(ps[:, B_GU + 2 * s, :], 0, h2hi, h2lo, (NHF + hf) * DT if first else None
                                     ).then_inc(w_done, 1)
                        pe.wait_ge(w_lo, fp * 4 + (base + 2 * s + 2))
                        pe.wait_ge(a_ok, fp * 2 + (hf * FT + s + 1))
                        feature_tile(ps[:, B_GU + 2 * s + 1, :], 1, h2hi, h2lo).then_inc(w_done, 1)

                gate_up(0)
                mean_square(*(("mix", 1) if hf == 0 else ("ffn", 0)))
                for fp in range(1, PEEL):
                    gate_up(fp)
                if hf:
                    result_back()
                with pe.Fori(PEEL, FT // 2) as fp:
                    gate_up(fp)

                def down_pair(i):
                    first = isinstance(i, int) and i == 0
                    for s in range(2):
                        if isinstance(i, int):
                            if i:
                                pe.wait_ge(res_sb, i * 2 + ((NHF + hf) * DT + s - NY + 1))
                                if hf:
                                    pe.wait_ge(sq_done, i * 2 + (NORM["ffn", 1][1] + s - NY + 1))
                        else:
                            pe.wait_ge(sq_done, i * 2 + (NORM["ffn", hf][1] + s - NY + 1))
                        for c, (k0, k1) in enumerate(DOWN_K):
                            t = len(DOWN_K) * s + c
                            pe.wait_ge(w_lo, i * (2 * len(DOWN_K)) + (base + 2 * FT + t + 1))
                            if first and s == 0 and c in (0, len(DOWN_K) - 1):
                                pe.wait_ge(a_lo, hf * FT + 1 + (FT if c else DOWN_K[1][1]))
                            for k in range(k0, k1):
                                v = slice((k - k0) * P, (k - k0 + 1) * P)
                                r = three(ps[:, B_Y + s, :], whi[:, t % 2, v], wlo[:, t % 2, v],
                                          ahi[:, k, :], alo[:, k, :], k == 0, k == FT - 1)
                            r.then_inc(w_done, 1)
                        if first and s == 0 and hf == 0:
                            mean_square("n2", 1)
                        if hf and (i or s):
                            back(i * 2 + s - 1)

                for i in range(DT // 2 if hf else DOWN_PEEL // 2):
                    down_pair(i)
                if hf == 0:
                    with pe.Fori(DOWN_PEEL // 2, DT // 2) as i:
                        down_pair(i)
            pe.wait_ge(ssum_done, NORM["ffn", 1][1] + DT + len(NORMS))
            for t in range(TT):
                r = nc.tensor.matmul(ps[:, B_OT, t:t + 1], ssum[:, t * P:(t + 1) * P], ones[:, 0:1],
                                     start=True, stop=True)
            r.then_inc(ms_ps, 1)
            back(DT - 1)


_INS = ["x", "c", "w_mod", "b_mod", "g_pre_mix", "w_in", "conv_w", "pos_cmp", "w_ck1", "w_ck2", "w_cv1", "w_cv2",
        "g_conv_out", "g_attn_out", "w_out", "g_post_mix", "g_pre_ffn", "w_gate", "w_up", "w_down", "g_post_ffn"]


def kernel(**inputs):
    import concourse.bacc as _bacc
    from concourse.bass_utils import run_bass_kernel_spmd as _run

    nc = _bacc.Bacc("TRN2", target_bir_lowering=False, num_devices=1)
    arrays, args = {}, []
    for name in _INS:
        a = np.ascontiguousarray(inputs[name])
        arrays[f"in_{name}"] = a
        args.append(nc.dram_tensor(f"in_{name}", a.shape, mybir.dt.from_np(a.dtype), kind="ExternalInput").ap())
    out = nc.dram_tensor("out_x", [1, SEQ, D], F32, kind="ExternalOutput").ap()
    build(nc, *args, out)
    r = _run(nc, [arrays], core_ids=[0])
    return r.results[0]["out_x"]
```
